# Optimizing a Trainium2 kernel written in Bass

```python
import jax
import jax.numpy as jnp
from jax import lax
import numpy as np
import math
import jax, jax.numpy as jnp

D_MODEL = 1024
BATCH = 1
SEQ = 256
DEPTH = 1

HEAD_DIM = 64
MIX_WIDTH = D_MODEL
A_WIDTH = D_MODEL // 4
A_HEADS = A_WIDTH // HEAD_DIM
A_DK = HEAD_DIM
A_DV = HEAD_DIM
B_WIDTH = D_MODEL // 2
B_BLOCKS = B_WIDTH // HEAD_DIM
B_CONV = 4
LRU_C = 8.0
C_WIDTH = MIX_WIDTH - A_WIDTH - B_WIDTH
C_HEADS = C_WIDTH // HEAD_DIM
C_DV = HEAD_DIM
C_DK = C_DV // 2
C_GATE_RANK = 16
C_GATE_NORM = 16.0
CHUNK = 64
D_FF = 2688
FFN_CONV = 3
EPS = 1e-6
F_FLOOR = 1e-20

IN_SIZES = (A_HEADS * A_DK, A_HEADS * A_DK, A_HEADS * A_DV, A_HEADS * A_DV,
            B_WIDTH, B_WIDTH,
            C_HEADS * C_DK, C_HEADS * C_DK, C_WIDTH, C_WIDTH, C_GATE_RANK)
IN_SPLITS = tuple(int(s) for s in np.cumsum(IN_SIZES)[:-1])
IN_COLS = int(sum(IN_SIZES))


def rmsnorm(x, w):
    xf = x.astype(jnp.float32)
    y = xf * lax.rsqrt(jnp.mean(xf * xf, axis=-1, keepdims=True) + EPS)
    return (y * w.astype(jnp.float32)).astype(x.dtype)

def head_rmsnorm(o, w):
    b, t, h, d = o.shape
    return rmsnorm(o, w.reshape(h, d)).reshape(b, t, h * d)

def causal_dwconv(x, w, bias):
    k_w = w.shape[0]
    t = x.shape[1]
    xp = jnp.pad(x, ((0, 0), (k_w - 1, 0), (0, 0)))
    y = bias + xp[:, k_w - 1:k_w - 1 + t] * w[k_w - 1]
    for k in range(k_w - 1):
        y = y + xp[:, k:k + t] * w[k]
    return y

def chunked_gated_linear_attention(q, k, v, log_f):
    b_sz, t, h, dk = q.shape
    dv = v.shape[-1]
    n = t // CHUNK

    def to_chunks(a):
        return a.astype(jnp.float32).reshape(b_sz, n, CHUNK, h, a.shape[-1]).transpose(1, 0, 3, 2, 4)

    qc, kc, vc, gc = to_chunks(q), to_chunks(k), to_chunks(v), to_chunks(log_f)
    causal = jnp.tril(jnp.ones((CHUNK, CHUNK), dtype=bool))[:, :, None]

    def step(state, inp):
        qi, ki, vi, gi = inp
        cum = jnp.cumsum(gi, axis=2)
        diff = cum[:, :, :, None, :] - cum[:, :, None, :, :]
        decay = jnp.where(causal, jnp.exp(jnp.where(causal, diff, 0.0)), 0.0)
        scores = jnp.einsum('bhid,bhijd,bhjd->bhij', qi, decay, ki)
        last = cum[:, :, -1:, :]
        out = (jnp.einsum('bhij,bhjv->bhiv', scores, vi)
               + jnp.einsum('bhid,bhdv->bhiv', qi * jnp.exp(cum), state))
        state = (jnp.exp(last[:, :, 0, :, None]) * state
                 + jnp.einsum('bhjd,bhjv->bhdv', ki * jnp.exp(last - cum), vi))
        return state, out

    s0 = jnp.zeros((b_sz, h, dk, dv), jnp.float32)
    _, o = lax.scan(step, s0, (qc, kc, vc, gc))
    return o.transpose(1, 0, 3, 2, 4).reshape(b_sz, t, h, dv).astype(q.dtype)

def hgrn2_mixer(q, f_logit, i, g, lower_bound, norm_w):
    b_sz, t, _ = q.shape
    lb = lower_bound.astype(jnp.float32)
    z = f_logit.astype(jnp.float32)
    f = lb + (1.0 - lb) * jax.nn.sigmoid(z)
    log_f = jnp.log(jnp.maximum(f, F_FLOOR))
    key = (1.0 - lb) * jax.nn.sigmoid(-z)
    heads = lambda a, d: a.reshape(b_sz, t, A_HEADS, d)
    o = chunked_gated_linear_attention(heads(q, A_DK), heads(key, A_DK), heads(i, A_DV), heads(log_f, A_DK))
    return head_rmsnorm(o, norm_w) * jax.nn.silu(g)

def rglru_mixer(xb, gb, conv_w, conv_b, w_a, b_a, w_x, b_x, lam):
    b_sz, t, _ = xb.shape
    xc = causal_dwconv(xb, conv_w, conv_b)
    xh = xc.reshape(b_sz, t, B_BLOCKS, HEAD_DIM)
    r = jax.nn.sigmoid(jnp.einsum('bthi,hij->bthj', xh, w_a).reshape(b_sz, t, B_WIDTH) + b_a)
    gi = jax.nn.sigmoid(jnp.einsum('bthi,hij->bthj', xh, w_x).reshape(b_sz, t, B_WIDTH) + b_x)
    log_a = (-LRU_C * r.astype(jnp.float32)) * jax.nn.softplus(-lam.astype(jnp.float32))
    a = jnp.exp(log_a)
    u = jnp.sqrt(jnp.maximum(-jnp.expm1(2.0 * log_a), 0.0)) * (gi * xc).astype(jnp.float32)

    def combine(left, right):
        a1, u1 = left
        a2, u2 = right
        return a1 * a2, a2 * u1 + u2

    _, hs = lax.associative_scan(combine, (a, u), axis=1)
    return hs.astype(xb.dtype) * jax.nn.gelu(gb)

def gla_mixer(q, k, v, g, g_lr, w_g_up, b_g, norm_w):
    b_sz, t, _ = q.shape
    log_f = jax.nn.log_sigmoid((g_lr @ w_g_up + b_g).astype(jnp.float32)) / C_GATE_NORM
    qh = q.reshape(b_sz, t, C_HEADS, C_DK) * (C_DK ** -0.5)
    kh = k.reshape(b_sz, t, C_HEADS, C_DK)
    vh = v.reshape(b_sz, t, C_HEADS, C_DV)
    o = chunked_gated_linear_attention(qh, kh, vh, log_f.reshape(b_sz, t, C_HEADS, C_DK))
    return head_rmsnorm(o, norm_w) * jax.nn.silu(g)

def first_inputs(seed: int = 0) -> dict:
    key = jax.random.key(seed)
    ks = jax.random.split(key, 24)
    f32 = jnp.float32

    def nrm(k, shape, scale):
        return scale * jax.random.normal(k, shape, f32)

    def gain(k, shape):
        return 1.0 + 0.05 * jax.random.normal(k, shape, f32)

    a0 = jax.random.uniform(ks[11], (DEPTH, B_WIDTH), f32, 0.9, 0.999)
    sig = a0 ** (1.0 / LRU_C)
    lam = jnp.log(sig) - jnp.log1p(-sig)
    return {
        'x': jax.random.normal(ks[0], (BATCH, SEQ, D_MODEL), f32),
        'norm_mix': gain(ks[1], (DEPTH, D_MODEL)),
        'w_in': nrm(ks[2], (DEPTH, D_MODEL, IN_COLS), D_MODEL ** -0.5),
        'hgrn_lower_bounds': nrm(ks[3], (DEPTH, A_HEADS * A_DK), 0.5),
        'hgrn_norm': gain(ks[4], (DEPTH, A_HEADS * A_DV)),
        'rg_conv_w': nrm(ks[5], (DEPTH, B_CONV, B_WIDTH), B_CONV ** -0.5),
        'rg_conv_b': nrm(ks[6], (DEPTH, B_WIDTH), 0.05),
        'rg_w_a': nrm(ks[7], (DEPTH, B_BLOCKS, HEAD_DIM, HEAD_DIM), HEAD_DIM ** -0.5),
        'rg_b_a': nrm(ks[8], (DEPTH, B_WIDTH), 0.1),
        'rg_w_x': nrm(ks[9], (DEPTH, B_BLOCKS, HEAD_DIM, HEAD_DIM), HEAD_DIM ** -0.5),
        'rg_b_x': nrm(ks[10], (DEPTH, B_WIDTH), 0.1),
        'rg_lambda': lam,
        'gla_w_gate_up': nrm(ks[12], (DEPTH, C_GATE_RANK, C_HEADS * C_DK), C_GATE_RANK ** -0.5),
        'gla_b_gate': nrm(ks[13], (DEPTH, C_HEADS * C_DK), 0.1),
        'gla_norm': gain(ks[14], (DEPTH, C_WIDTH)),
        'w_out': nrm(ks[15], (DEPTH, MIX_WIDTH, D_MODEL), MIX_WIDTH ** -0.5),
        'norm_ffn': gain(ks[16], (DEPTH, D_MODEL)),
        'ffn_w_gate': nrm(ks[17], (DEPTH, D_MODEL, D_FF), D_MODEL ** -0.5),
        'ffn_w_val': nrm(ks[18], (DEPTH, D_MODEL, D_FF), D_MODEL ** -0.5),
        'ffn_conv_w': nrm(ks[19], (DEPTH, FFN_CONV, D_FF), FFN_CONV ** -0.5),
        'ffn_conv_b': nrm(ks[20], (DEPTH, D_FF), 0.05),
        'ffn_w_down': nrm(ks[21], (DEPTH, D_FF, D_MODEL), D_FF ** -0.5),
        'norm_final': gain(ks[22], (D_MODEL,)),
    }

def first_block(x, norm_mix, w_in, hgrn_lower_bounds, hgrn_norm, rg_conv_w, rg_conv_b, rg_w_a, rg_b_a,
              rg_w_x, rg_b_x, rg_lambda, gla_w_gate_up, gla_b_gate, gla_norm, w_out, norm_ffn,
              ffn_w_gate, ffn_w_val, ffn_conv_w, ffn_conv_b, ffn_w_down, norm_final):
    lb = jax.nn.softmax(hgrn_lower_bounds.astype(jnp.float32), axis=0)
    lb = jnp.cumsum(lb, axis=0) - lb[0]
    for l in range(DEPTH):
        h = rmsnorm(x, norm_mix[l])
        proj = h @ w_in[l]
        a_q, a_f, a_i, a_g, b_x, b_g, c_q, c_k, c_v, c_g, c_lr = jnp.split(proj, IN_SPLITS, axis=-1)
        o_a = hgrn2_mixer(a_q, a_f, a_i, a_g, lb[l], hgrn_norm[l])
        o_b = rglru_mixer(b_x, b_g, rg_conv_w[l], rg_conv_b[l], rg_w_a[l], rg_b_a[l],
                          rg_w_x[l], rg_b_x[l], rg_lambda[l])
        o_c = gla_mixer(c_q, c_k, c_v, c_g, c_lr, gla_w_gate_up[l], gla_b_gate[l], gla_norm[l])
        x = x + jnp.concatenate([o_a, o_b, o_c], axis=-1) @ w_out[l]
        h = rmsnorm(x, norm_ffn[l])
        gate = causal_dwconv(h @ ffn_w_gate[l], ffn_conv_w[l], ffn_conv_b[l])
        x = x + (jax.nn.gelu(gate) * (h @ ffn_w_val[l])) @ ffn_w_down[l]
    return rmsnorm(x, norm_final)


DEPTH_2 = 2

BLK = 128
GRID_W = 64
WIN_HEADS = 4
WIN_KV_HEADS = 2
WINDOW = 128
MLA_HEADS = 4
MLA_Q_RANK = 256
MLA_KV_RANK = 128
MLA_NOPE = 64
MLA_ROPE = 32
MLA_V = 64
AX_HEADS = 4
AX_KV_HEADS = 2
DIFF_HEADS = 4
DIFF_QK = 32
DIFF_V = 64
A_COLS = (WIN_HEADS + 2 * WIN_KV_HEADS) * HEAD_DIM
B_COLS = MLA_Q_RANK + MLA_KV_RANK + MLA_ROPE
C_COLS = (AX_HEADS + 2 * AX_KV_HEADS) * HEAD_DIM
D_COLS = DIFF_HEADS * (4 * DIFF_QK + DIFF_V)
N_IN = A_COLS + B_COLS + C_COLS + D_COLS
D_MIX = WIN_HEADS * HEAD_DIM + MLA_HEADS * MLA_V + AX_HEADS * HEAD_DIM + DIFF_HEADS * DIFF_V
D_FF_2 = 2816
ROPE_BASE = 10000.0
NORM_EPS = 1e-5
NEG_INF = -1e30


def _layer_norm(x, g, b):
    xf = x.astype(jnp.float32)
    mu = jnp.mean(xf, -1, keepdims=True)
    xc = xf - mu
    var = jnp.mean(xc * xc, -1, keepdims=True)
    y = xc * lax.rsqrt(var + NORM_EPS) * g.astype(jnp.float32) + b.astype(jnp.float32)
    return y.astype(x.dtype)

def _rms_norm(x, g):
    xf = x.astype(jnp.float32)
    y = xf * lax.rsqrt(jnp.mean(xf * xf, -1, keepdims=True) + NORM_EPS)
    return (y * g.astype(jnp.float32)).astype(x.dtype)

def _swiglu(h, w_gu, w_down):
    gate, up = jnp.split(h @ w_gu, 2, axis=-1)
    return (jax.nn.silu(gate) * up) @ w_down

def _alibi_slopes(n):
    return 2.0 ** (-8.0 * (jnp.arange(n, dtype=jnp.float32) + 1.0) / n)

def _rope_angles(pos, dim):
    inv = ROPE_BASE ** (-jnp.arange(0, dim, 2, dtype=jnp.float32) / dim)
    ang = pos.astype(jnp.float32)[:, None] * inv[None, :]
    return jnp.cos(ang), jnp.sin(ang)

def _apply_rope(x, cos, sin):
    c = cos[:, None, :]
    s = sin[:, None, :]
    x1, x2 = jnp.split(x.astype(jnp.float32), 2, axis=-1)
    return jnp.concatenate([x1 * c - x2 * s, x1 * s + x2 * c], -1).astype(x.dtype)

def _dense_attention(q, k, v, scale):
    B, S, Hq, Dk = q.shape
    Hkv = k.shape[2]
    G = Hq // Hkv
    nb = S // BLK
    qb = q.reshape(B, nb, BLK, Hkv, G, Dk).transpose(1, 0, 2, 3, 4, 5)

    def block(qi):
        s = jnp.einsum('bqhgd,bkhd->bhgqk', qi, k).astype(jnp.float32) * scale
        p = jax.nn.softmax(s, axis=-1)
        return jnp.einsum('bhgqk,bkhd->bqhgd', p.astype(v.dtype), v)

    o = lax.map(block, qb)
    return o.transpose(1, 0, 2, 3, 4, 5).reshape(B, S, Hq * v.shape[-1])

def _mixer_window(a, sink, slopes):
    B, S, _ = a.shape
    nb = S // BLK
    G = WIN_HEADS // WIN_KV_HEADS
    q, k, v = jnp.split(a, [WIN_HEADS * HEAD_DIM, (WIN_HEADS + WIN_KV_HEADS) * HEAD_DIM], axis=-1)
    qb = q.reshape(B, nb, BLK, WIN_KV_HEADS, G, HEAD_DIM)

    def band(t):
        tp = jnp.pad(t.reshape(B, S, WIN_KV_HEADS, HEAD_DIM), ((0, 0), (BLK, BLK), (0, 0), (0, 0)))
        tp = tp.reshape(B, nb + 2, BLK, WIN_KV_HEADS, HEAD_DIM)
        return jnp.concatenate([tp[:, :-2], tp[:, 1:-1], tp[:, 2:]], axis=2)

    kw = band(k)
    vw = band(v)
    s = jnp.einsum('bnqhgd,bnkhd->bnhgqk', qb, kw).astype(jnp.float32) * (HEAD_DIM ** -0.5)
    dist = jnp.abs(jnp.arange(BLK)[:, None] - jnp.arange(3 * BLK)[None, :] + BLK)
    kpos = jnp.arange(nb)[:, None] * BLK - BLK + jnp.arange(3 * BLK)[None, :]
    allowed = (dist <= WINDOW)[None] & ((kpos >= 0) & (kpos < S))[:, None, :]
    bias = -slopes.reshape(WIN_KV_HEADS, G, 1, 1) * dist.astype(jnp.float32)
    s = jnp.where(allowed[None, :, None, None], s + bias, NEG_INF)
    sink_logit = jnp.broadcast_to(sink.astype(jnp.float32).reshape(1, 1, WIN_KV_HEADS, G, 1, 1),
                                  s.shape[:-1] + (1,))
    p = jax.nn.softmax(jnp.concatenate([s, sink_logit], axis=-1), axis=-1)[..., :-1]
    o = jnp.einsum('bnhgqk,bnkhd->bnqhgd', p.astype(vw.dtype), vw)
    return o.reshape(B, S, WIN_HEADS * HEAD_DIM)

def _mixer_mla(b, q_norm_g, w_uq, kv_norm_g, w_ukv, pos):
    B, S, _ = b.shape
    c_q, c_kv, k_rope = jnp.split(b, [MLA_Q_RANK, MLA_Q_RANK + MLA_KV_RANK], axis=-1)
    q = (_rms_norm(c_q, q_norm_g) @ w_uq).reshape(B, S, MLA_HEADS, MLA_NOPE + MLA_ROPE)
    kv = (_rms_norm(c_kv, kv_norm_g) @ w_ukv).reshape(B, S, MLA_HEADS, MLA_NOPE + MLA_V)
    cos, sin = _rope_angles(pos, MLA_ROPE)
    q = jnp.concatenate([q[..., :MLA_NOPE], _apply_rope(q[..., MLA_NOPE:], cos, sin)], axis=-1)
    k_r = _apply_rope(k_rope[:, :, None, :], cos, sin)
    k = jnp.concatenate([kv[..., :MLA_NOPE], jnp.broadcast_to(k_r, (B, S, MLA_HEADS, MLA_ROPE))], axis=-1)
    v = kv[..., MLA_NOPE:]
    return _dense_attention(q, k, v, (MLA_NOPE + MLA_ROPE) ** -0.5)

def _mixer_axial(c, q_g, k_g):
    B, S, _ = c.shape
    q, k, v = jnp.split(c, [AX_HEADS * HEAD_DIM, (AX_HEADS + AX_KV_HEADS) * HEAD_DIM], axis=-1)
    q = _rms_norm(q.reshape(B, S, AX_HEADS, HEAD_DIM), q_g)
    k = _rms_norm(k.reshape(B, S, AX_KV_HEADS, HEAD_DIM), k_g)
    v = v.reshape(B, S, AX_KV_HEADS, HEAD_DIM)
    rows = S // GRID_W
    row = jnp.repeat(jnp.arange(rows, dtype=jnp.int32), GRID_W)
    col = jnp.tile(jnp.arange(GRID_W, dtype=jnp.int32), rows)
    half = HEAD_DIM // 2
    cr, sr = _rope_angles(row, half)
    cc, sc = _rope_angles(col, half)

    def axial(t):
        return jnp.concatenate([_apply_rope(t[..., :half], cr, sr), _apply_rope(t[..., half:], cc, sc)], axis=-1)

    return _dense_attention(axial(q), axial(k), v, HEAD_DIM ** -0.5)

def _mixer_diff(d, lam_params, subln_g, slopes, layer_idx):
    B, S, _ = d.shape
    H = DIFF_HEADS
    q, k, v = jnp.split(d, [H * 2 * DIFF_QK, H * 4 * DIFF_QK], axis=-1)
    q = q.reshape(B, S, H, 2, DIFF_QK)
    k = k.reshape(B, S, H, 2, DIFF_QK)
    v = v.reshape(B, S, H, DIFF_V)
    lam_init = 0.8 - 0.6 * math.exp(-0.3 * layer_idx)
    lp = lam_params.astype(jnp.float32)
    lam = jnp.exp(jnp.sum(lp[0] * lp[1])) - jnp.exp(jnp.sum(lp[2] * lp[3])) + lam_init
    nb = S // BLK
    qb = q.reshape(B, nb, BLK, H, 2, DIFF_QK).transpose(1, 0, 2, 3, 4, 5)
    kpos = jnp.arange(S)
    scale = DIFF_QK ** -0.5

    def block(args):
        qi, i = args
        tq = i * BLK + jnp.arange(BLK)
        dist = jnp.abs(tq[:, None] - kpos[None, :]).astype(jnp.float32)
        bias = -slopes[:, None, None] * dist
        s = jnp.einsum('bqhmd,bkhmd->bhmqk', qi, k).astype(jnp.float32) * scale + bias[None, :, None]
        p = jax.nn.softmax(s, axis=-1)
        w = p[:, :, 0] - lam * p[:, :, 1]
        return jnp.einsum('bhqk,bkhd->bqhd', w.astype(v.dtype), v)

    o = lax.map(block, (qb, jnp.arange(nb)))
    o = o.transpose(1, 0, 2, 3, 4).reshape(B, S, H, DIFF_V)
    o = _rms_norm(o, subln_g) * (1.0 - lam_init)
    return o.reshape(B, S, H * DIFF_V)

def _token_mixers(h, w_in, sink, mla_q_norm, mla_w_uq, mla_kv_norm, mla_w_ukv,
                  ax_q_norm, ax_k_norm, diff_lambda, diff_subln, w_out, layer_idx):
    S = h.shape[1]
    proj = h @ w_in
    a, b, c, d = jnp.split(proj, [A_COLS, A_COLS + B_COLS, A_COLS + B_COLS + C_COLS], axis=-1)
    pos = jnp.arange(S, dtype=jnp.int32)
    slopes = _alibi_slopes(WIN_HEADS + DIFF_HEADS)
    o_a = _mixer_window(a, sink, slopes[:WIN_HEADS])
    o_b = _mixer_mla(b, mla_q_norm, mla_w_uq, mla_kv_norm, mla_w_ukv, pos)
    o_c = _mixer_axial(c, ax_q_norm, ax_k_norm)
    o_d = _mixer_diff(d, diff_lambda, diff_subln, slopes[WIN_HEADS:], layer_idx)
    return jnp.concatenate([o_a, o_b, o_c, o_d], axis=-1) @ w_out

def second_inputs(seed: int = 0) -> dict:
    key = jax.random.key(seed)
    ks = jax.random.split(key, 20)
    f32 = jnp.float32
    beta = (8 * DEPTH_2) ** -0.25

    def nrm(k, shape, scale):
        return jax.random.normal(k, shape, f32) * scale

    return {
        "x": nrm(ks[0], (BATCH, SEQ, D_MODEL), 1.0),
        "w_in": nrm(ks[1], (DEPTH_2, D_MODEL, N_IN), D_MODEL ** -0.5),
        "win_sink": nrm(ks[2], (DEPTH_2, WIN_HEADS), 0.5),
        "mla_q_norm": 1.0 + nrm(ks[3], (DEPTH_2, MLA_Q_RANK), 0.02),
        "mla_w_uq": nrm(ks[4], (DEPTH_2, MLA_Q_RANK, MLA_HEADS * (MLA_NOPE + MLA_ROPE)), MLA_Q_RANK ** -0.5),
        "mla_kv_norm": 1.0 + nrm(ks[5], (DEPTH_2, MLA_KV_RANK), 0.02),
        "mla_w_ukv": nrm(ks[6], (DEPTH_2, MLA_KV_RANK, MLA_HEADS * (MLA_NOPE + MLA_V)), MLA_KV_RANK ** -0.5),
        "ax_q_norm": 1.0 + nrm(ks[7], (DEPTH_2, HEAD_DIM), 0.02),
        "ax_k_norm": 1.0 + nrm(ks[8], (DEPTH_2, HEAD_DIM), 0.02),
        "diff_lambda": nrm(ks[9], (DEPTH_2, 4, DIFF_QK), 0.1),
        "diff_subln": 1.0 + nrm(ks[10], (DEPTH_2, DIFF_V), 0.02),
        "w_out": nrm(ks[11], (DEPTH_2, D_MIX, D_MODEL), beta * D_MIX ** -0.5),
        "ffn_w_gu": nrm(ks[12], (DEPTH_2, 2, D_MODEL, 2 * D_FF_2), D_MODEL ** -0.5),
        "ffn_w_down": nrm(ks[13], (DEPTH_2, 2, D_FF_2, D_MODEL), beta * D_FF_2 ** -0.5),
        "ln_g": 1.0 + nrm(ks[14], (DEPTH_2, 3, D_MODEL), 0.02),
        "ln_b": nrm(ks[15], (DEPTH_2, 3, D_MODEL), 0.02),
    }

def second_block(x, w_in, win_sink, mla_q_norm, mla_w_uq, mla_kv_norm, mla_w_ukv,
              ax_q_norm, ax_k_norm, diff_lambda, diff_subln, w_out,
              ffn_w_gu, ffn_w_down, ln_g, ln_b):
    alpha = (2 * DEPTH_2) ** 0.25
    for l in range(DEPTH_2):
        x = _layer_norm(alpha * x + 0.5 * _swiglu(x, ffn_w_gu[l, 0], ffn_w_down[l, 0]), ln_g[l, 0], ln_b[l, 0])
        mix = _token_mixers(x, w_in[l], win_sink[l], mla_q_norm[l], mla_w_uq[l], mla_kv_norm[l], mla_w_ukv[l],
                            ax_q_norm[l], ax_k_norm[l], diff_lambda[l], diff_subln[l], w_out[l], l)
        x = _layer_norm(alpha * x + mix, ln_g[l, 1], ln_b[l, 1])
        x = _layer_norm(alpha * x + 0.5 * _swiglu(x, ffn_w_gu[l, 1], ffn_w_down[l, 1]), ln_g[l, 2], ln_b[l, 2])
    return x


def setup_inputs(seed=0):
    out = dict(first_inputs(seed))
    for name, value in second_inputs(seed + 1).items():
        if name != "x":
            out[name + "_2"] = value
    return out


def reference(
    x, norm_mix, w_in, hgrn_lower_bounds, hgrn_norm, rg_conv_w, rg_conv_b, rg_w_a, rg_b_a,
    rg_w_x, rg_b_x, rg_lambda, gla_w_gate_up, gla_b_gate, gla_norm, w_out, norm_ffn, ffn_w_gate,
    ffn_w_val, ffn_conv_w, ffn_conv_b, ffn_w_down, norm_final, w_in_2, win_sink_2, mla_q_norm_2,
    mla_w_uq_2, mla_kv_norm_2, mla_w_ukv_2, ax_q_norm_2, ax_k_norm_2, diff_lambda_2,
    diff_subln_2, w_out_2, ffn_w_gu_2, ffn_w_down_2, ln_g_2, ln_b_2,
):
    x = first_block(
        x, norm_mix, w_in, hgrn_lower_bounds, hgrn_norm, rg_conv_w, rg_conv_b, rg_w_a, rg_b_a,
        rg_w_x, rg_b_x, rg_lambda, gla_w_gate_up, gla_b_gate, gla_norm, w_out, norm_ffn,
        ffn_w_gate, ffn_w_val, ffn_conv_w, ffn_conv_b, ffn_w_down, norm_final,
    )
    return second_block(
        x, w_in_2, win_sink_2, mla_q_norm_2, mla_w_uq_2, mla_kv_norm_2, mla_w_ukv_2,
        ax_q_norm_2, ax_k_norm_2, diff_lambda_2, diff_subln_2, w_out_2, ffn_w_gu_2,
        ffn_w_down_2, ln_g_2, ln_b_2,
    )


_drawn_inputs = setup_inputs


def setup_inputs(seed=0):
    import zlib

    import numpy as np

    out = dict(_drawn_inputs(seed))
    spreads = {}
    factors = {'hgrn_norm': 3.765,
     'rg_b_a': 8.0,
     'rg_b_x': 4.866,
     'gla_b_gate': 4.128,
     'gla_norm': 3.719,
     'win_sink_2': 8.0,
     'mla_q_norm_2': 8.0,
     'mla_kv_norm_2': 8.0,
     'ax_q_norm_2': 8.0,
     'ax_k_norm_2': 8.0,
     'diff_subln_2': 8.0}
    for name, (base, spread) in spreads.items():
        noise = np.random.default_rng([zlib.crc32(name.encode()), seed]).standard_normal(out[name].shape)
        drawn = base * np.exp(spread * noise) if base else spread * noise
        out[name] = jnp.asarray(drawn.astype(out[name].dtype))
    for name, factor in factors.items():
        out[name] = (out[name] * factor).astype(out[name].dtype)
    return out
```

```python
from contextlib import ExitStack

import numpy as np
import concourse.bass as bass
from concourse import mybir
from concourse.alu_op_type import AluOpType as ALU

F32 = mybir.dt.float32
BF16 = mybir.dt.bfloat16
I32 = mybir.dt.int32
ACT = mybir.ActivationFunctionType
X = mybir.AxisListType.X

P = 128
S = 256
M = S // P
D = 1024
KD = D // P
HALF = 512
HD = 64

A_Q, A_F, A_I, A_G, B_X, B_G, C_Q, C_K, C_V, C_G, C_LR = 0, 256, 512, 768, 1024, 1536, 2048, 2176, 2304, 2560, 2816
IN1 = 2832
LR_RANK = 16
DFF1 = 2688
FT1 = DFF1 // P
EPS1 = 1e-6
F_FLOOR = 1e-20
LEVELS = [1, 2, 4, 8, 16, 32, 64, 128]
CHUNK = 64
BANK_HEADS = [[(0, 0, 64, 0), (2, 0, 64, 1), (4, 0, 32, 2)],
              [(1, 64, 64, 0), (3, 64, 64, 1), (6, 64, 32, 2)],
              [(5, 32, 32, 2)],
              [(7, 96, 32, 2)]]
BANK_SLOT = [0, 3, 6, 7]

LAYERS = 2
IN2 = 2208
WIN_Q, WIN_K, WIN_V = 0, 256, 384
MLA_Q, MLA_KV, MLA_KR = 512, 768, 896
AX_Q, AX_V = 928, 1312
DF_Q, DF_K, DF_V = 1440, 1696, 1952
NOPE, ROPE = 64, 32
DFF2 = 2816
FT2 = DFF2 // P
EPS2 = 1e-5
ALPHA = float((2 * LAYERS) ** 0.25)
GELU_RING, SWI_RING = 3, 2


def constants():
    t = {}
    t["ident"] = np.eye(P, dtype=np.float32)
    slopes = (2.0 ** (-8.0 * (np.arange(8, dtype=np.float32) + 1.0) / 8)).astype(np.float32)
    q = np.arange(S)[:, None]
    k = np.arange(S)[None, :]
    dist = np.abs(q - k).astype(np.float32)
    win = np.where(dist <= 128, -slopes[:4, None, None] * dist, np.float32(-1e30)).astype(np.float32)
    dif = (-slopes[4:, None, None] * dist).astype(np.float32)
    t["win_bias"] = np.ascontiguousarray(win.reshape(4, M, P, S).transpose(2, 1, 0, 3))
    t["dif_bias"] = np.ascontiguousarray(dif.reshape(4, M, P, S).transpose(2, 1, 0, 3))

    def angles(pos, dim):
        inv = (np.float32(10000.0) ** (-np.arange(0, dim, 2, dtype=np.float32) / np.float32(dim))).astype(np.float32)
        a = pos.astype(np.float32)[:, None] * inv[None, :]
        return np.cos(a).astype(np.float32), np.sin(a).astype(np.float32)

    pos = np.arange(S)
    cm, sm = angles(pos, ROPE)
    cr, sr = angles(pos // 64, 32)
    cc, sc = angles(pos % 64, 32)
    rope = np.stack([cm, sm, cr, cc, sr, sc], 1)
    t["rope"] = np.ascontiguousarray(rope.reshape(M, P, 6, 16).transpose(1, 0, 2, 3))
    j = np.arange(P)[:, None]
    i = np.arange(P)[None, :]
    masks = [((j // (2 * s) == i // (2 * s)) & (j % (2 * s) < s) & (i % (2 * s) >= s)) for s in LEVELS[:-1]]
    t["masks"] = np.ascontiguousarray(np.stack(masks, 1).astype(np.int32))
    keep = np.ones((P, 2, 3, S), np.float32)
    keep[:, 0, :, ::CHUNK] = 0
    keep[:, 1, :, ::S] = 0
    t["keep"] = keep
    li = [0.8 - 0.6 * np.exp(-0.3 * l) for l in range(LAYERS)]
    t["lam_init"] = np.array([[v, 1.0 - v] for v in li], np.float32)
    return t


CONSTS = {"ident": (P, P), "win_bias": (P, M, 4, S), "dif_bias": (P, M, 4, S), "rope": (P, M, 6, 16),
          "masks": (P, 7, P), "keep": (P, 2, 3, S), "lam_init": (LAYERS, 2)}


class Counter:

    def __init__(self, nc, ctx, name):
        self.sem, self.n = ctx.enter_context(nc.semaphore(name)), 0

    def tick(self, ins, by=1):
        ins.then_inc(self.sem, by)
        self.n += by
        return (self, self.n)


def program(nc, A, C, out):
    ctx = ExitStack()
    with ctx:
        def sb(name, shape, dt=F32):
            return ctx.enter_context(nc.sbuf_tensor(name, shape, dt))

        pe, act, dve, pool, sp = nc.tensor, nc.scalar, nc.vector, nc.gpsimd, nc.sync
        bank = [ctx.enter_context(nc.psum_tensor(f"bank{i}", [P, HALF], F32)) for i in range(8)]
        counters = []

        def counter(name):
            counters.append(Counter(nc, ctx, name))
            return counters[-1]

        c_pe, c_act, c_dve, c_pool = (counter(n) for n in ("pe_steps", "act_steps", "dve_steps", "pool_steps"))
        c_wide = [counter(f"wide_loaded{i}") for i in range(2)]
        c_gu = [counter(f"gate_up_loaded{i}") for i in range(3)]
        c_dn = [counter(f"down_loaded{i}") for i in range(3)]
        c_gu_used = [counter(f"gate_up_used{i}") for i in range(3)]
        c_dn_used = [counter(f"down_used{i}") for i in range(3)]
        c_gate, c_up, c_conv, c_gelu, c_prod = (counter(n) for n in ("gate_done", "up_done", "conv_done", "nonlin_done", "product_done"))
        c_par = counter("parameters_loaded")
        c_gain = counter("gains_loaded")
        c_gain2, c_row2, c_ln2 = counter("layer_gains_loaded"), counter("layer_rows_loaded"), counter("layer_ln_loaded")
        c_ident = counter("identity_loaded")
        c_uq = counter("mla_weights_loaded")
        c_row = counter("rows_loaded")
        c_lng = counter("ln_rows_loaded")
        c_out = counter("output_stored")

        def need(eng, *marks):
            best = {}
            for c, v in marks:
                best[id(c)] = (c, max(v, best.get(id(c), (c, 0))[1]))
            for c, v in best.values():
                if v > 0:
                    eng.wait_ge(c.sem, v)

        def did(eng, ins):
            return {id(pe): c_pe, id(act): c_act, id(dve): c_dve, id(pool): c_pool}[id(eng)].tick(ins)

        def fresh_counters():
            nc.all_engine_barrier()
            for c in counters:
                if c not in (c_gain, c_row, c_lng):
                    sp.sem_clear(c.sem)
                    c.n = 0
            for c in (*c_gu_used, *c_dn_used):
                sp.sem_inc(c.sem, 1)
                c.n = 1
            nc.all_engine_barrier()
            wide_state.update(next=0, free=[None, None])

        wide = [sb(f"wide{i}", [P, KD, HALF]) for i in range(2)]
        w_gu = [sb(f"w_gu{i}", [P, 2, KD, P]) for i in range(3)]
        w_dn = [sb(f"w_dn{i}", [P, D]) for i in range(3)]
        for c in (*c_gu_used, *c_dn_used):
            c.tick(sp.nop())
        x = sb("x", [P, M, D])
        n = sb("n", [P, M, D])
        xT = sb("xT", [P, KD, S])
        catT = sb("catT", [P, KD, S])
        proj = sb("proj", [P, M, IN2])
        actT = sb("actT", [P, 3, S])
        nonlin = sb("nonlin", [P, 2, S])
        conv = sb("conv", [P, 2, S])
        ident = sb("ident", [P, P])
        zeros = sb("zeros", [P, HALF], BF16)
        rows = sb("rows", [P, P])
        rows2 = sb("rows2", [P, P])
        par1 = sb("par1", [P, 60])
        parc = sb("parc", [P, 4, FT1])
        lnT = sb("lnT", [P, 6, KD])
        gb = sb("gb", [P, 2, D])
        stats = sb("stats", [P, M, 2, 6])
        mv = sb("mv", [P, M, 2])
        ms = sb("ms", [P, M])
        sd = sb("sd", [P, M])
        rs = sb("rs", [P, M])
        nmr = sb("nmr", [P, M])
        gbo = sb("gbo", [P, M, D])
        big = sb("big", [P, 14600])

        class Carve:
            def __init__(self):
                self.at = 0

            def __call__(self, *shape):
                size = int(np.prod(shape))
                v = big[:, self.at:self.at + size]
                self.at += size
                assert self.at <= 14600, self.at
                if len(shape) == 2:
                    v = v.rearrange("p (a b) -> p a b", a=shape[0])
                if len(shape) == 3:
                    v = v.rearrange("p (a b c) -> p a b c", a=shape[0], b=shape[1])
                if len(shape) == 4:
                    v = v.rearrange("p (a b c d) -> p a b c d", a=shape[0], b=shape[1], c=shape[2])
                return v

        def bc(ap, axis, count):
            shape = list(ap.shape)
            shape.insert(axis, count)
            return ap.unsqueeze(axis).to_broadcast(shape)

        def all_partitions(ap1d, width):
            return ap1d.rearrange("(a n) -> a n", a=1).to_broadcast([P, width])

        wide_state = {"next": 0, "free": [None, None]}

        def load_wide(dram, width):
            i = wide_state["next"]
            wide_state["next"] = 1 - i
            if wide_state["free"][i]:
                need(sp, wide_state["free"][i])
            m = c_wide[i].tick(sp.dma_start(wide[i][:, :, 0:width], dram.rearrange("(k p) n -> p k n", p=P)), 16)
            return i, m

        def stats_and_rstd(m, eps, centred, y_done):
            need(dve, *y_done)
            for h in range(2):
                k = did(dve, dve.bn_stats(stats[:, m, h, :], x[:, m, h * HALF:(h + 1) * HALF]))
            need(dve, k)
            k = did(dve, dve.bn_aggr(mv[:, m, :], stats[:, m, :, :].rearrange("p a b -> p (a b)")))
            need(dve, k)
            if centred:
                k = did(dve, dve.tensor_scalar(ms[:, m:m + 1], mv[:, m, 1:2], eps, None, ALU.add))
            else:
                k = did(dve, dve.scalar_tensor_tensor(out=ms[:, m:m + 1], in0=mv[:, m, 0:1], scalar=mv[:, m, 0:1],
                                                      in1=mv[:, m, 1:2], op0=ALU.mult, op1=ALU.add))
                need(dve, k)
                k = did(dve, dve.tensor_scalar(ms[:, m:m + 1], ms[:, m:m + 1], eps, None, ALU.add))
            need(act, k)
            k = did(act, act.activation(sd[:, m:m + 1], ms[:, m:m + 1], ACT.Sqrt))
            need(dve, k)
            k = did(dve, dve.reciprocal(rs[:, m:m + 1], sd[:, m:m + 1]))
            if centred:
                need(dve, k)
                k = did(dve, dve.scalar_tensor_tensor(out=nmr[:, m:m + 1], in0=mv[:, m, 0:1], scalar=-1.0,
                                                      in1=rs[:, m:m + 1], op0=ALU.mult, op1=ALU.mult))
            return k

        def transpose_tiles(src, dst, gain, bias, src_done, extra=()):
            done = []
            freed = [extra, extra]
            for k in range(KD):
                b = 6 + k % 2
                need(pe, *freed[k % 2], *src_done)
                for m in range(M):
                    t = pe.transpose(bank[b][:, m * P:(m + 1) * P], src[:, m, k * P:(k + 1) * P], ident[:, :])
                t = did(pe, t)
                e = (dve, act)[k % 2]
                need(e, t)
                g = gain(k) if gain else None
                if e is dve:
                    if g is None:
                        i = dve.tensor_copy(dst[:, k, :], bank[b][:, 0:S])
                    elif bias:
                        i = dve.tensor_scalar(dst[:, k, :], bank[b][:, 0:S], g, bias(k), ALU.mult, ALU.add)
                    else:
                        i = dve.tensor_scalar(dst[:, k, :], bank[b][:, 0:S], g, None, ALU.mult)
                elif g is None:
                    i = act.activation(dst[:, k, :], bank[b][:, 0:S], ACT.Copy)
                elif bias:
                    i = act.activation(dst[:, k, :], bank[b][:, 0:S], ACT.Identity, scale=g, bias=bias(k))
                else:
                    i = act.activation(dst[:, k, :], bank[b][:, 0:S], ACT.Copy, scale=g)
                t = did(e, i)
                freed[k % 2] = (t,)
                done.append(t)
            return done[-2:]

        def norm(added, alpha, eps, centred, gain, bias, token_gain=None):
            nd = []
            for m in range(M):
                yd = []
                if added:
                    need(dve, *added)
                    for h in range(2):
                        xs = x[:, m, h * HALF:(h + 1) * HALF]
                        yd.append(did(dve, dve.scalar_tensor_tensor(out=xs, in0=xs, scalar=alpha, in1=bank[2 * m + h][:, :],
                                                                    op0=ALU.mult, op1=ALU.add)))
                k = stats_and_rstd(m, eps, centred, yd)
                e = (act, dve)[m]
                need(e, k)
                if e is dve:
                    if centred:
                        i = dve.tensor_scalar(n[:, m, :], x[:, m, :], rs[:, m:m + 1], nmr[:, m:m + 1], ALU.mult, ALU.add)
                    else:
                        i = dve.tensor_scalar(n[:, m, :], x[:, m, :], rs[:, m:m + 1], None, ALU.mult)
                elif centred:
                    i = act.activation(n[:, m, :], x[:, m, :], ACT.Identity, scale=rs[:, m:m + 1], bias=nmr[:, m:m + 1])
                else:
                    i = act.activation(n[:, m, :], x[:, m, :], ACT.Copy, scale=rs[:, m:m + 1])
                nd.append(did(e, i))
            done = transpose_tiles(n, xT, gain, bias, nd)
            if token_gain:
                need(pool, token_gain, *nd, *done)
                for m in range(M):
                    k = did(pool, pool.tensor_tensor(x[:, m, :], n[:, m, :], gb[:, 0, :], ALU.mult))
                    if bias:
                        need(pool, k)
                        k = did(pool, pool.tensor_tensor(x[:, m, :], x[:, m, :], gb[:, 1, :], ALU.add))
                done = [*done, k]
            return done

        def token_chunk(src, slot, loaded, width, ready, banks):
            need(pe, loaded, *ready)
            for m in range(M):
                for k in range(KD):
                    i = pe.matmul(bank[banks[m]][:, 0:width], src[:, k, m * P:(m + 1) * P], wide[slot][:, k, 0:width],
                                  start=(k == 0), stop=(k == KD - 1))
            t = did(pe, i)
            wide_state["free"][slot] = t
            return t

        def out_product(w_dram, ready):
            for h in range(2):
                slot, ld = load_wide(w_dram[:, h * HALF:(h + 1) * HALF], HALF)
                t = token_chunk(catT, slot, ld, HALF, ready, [h, 2 + h])
            return [t]

        def ffn(gate_w, up_w, down_w, tiles, ring, ready, convolved):
            base = {id(c): c.n for c in counters}
            turns = tiles // ring
            need(pe, *ready)
            for b in range(4):
                pe.matmul(bank[b][:, :], zeros[:, 0:P], zeros[:, :], start=True, stop=False, skip_group_check=True)
            need(dve, *ready)
            need(act, *ready)
            with nc.Fori(0, turns) as it:
                for t in range(ring):
                    sp.wait_ge(c_gu_used[t].sem, base[id(c_gu_used[t])] + it)
                    for w, dram in ((0, gate_w), (1, up_w)):
                        sp.dma_start(w_gu[t][:, w], dram(it * ring + t).rearrange("(k p) n -> p k n", p=P)).then_inc(c_gu[t].sem, 16)
                for t in range(ring):
                    sp.wait_ge(c_dn_used[t].sem, base[id(c_dn_used[t])] + it)
                    sp.dma_start(w_dn[t][:, :], down_w(it * ring + t)).then_inc(c_dn[t].sem, 16)
                for t in range(ring):
                    g, u = bank[4 + t % 2], bank[6 + t % 2]
                    pe.wait_ge(c_gu[t].sem, base[id(c_gu[t])] + (it + 1) * 32)
                    if t >= 2:
                        pe.wait_ge(c_prod.sem, base[id(c_prod)] + it * ring + t - 1)
                    for w, b, c in ((0, g, c_gate), (1, u, c_up)):
                        for k in range(KD):
                            i = pe.matmul(b[:, 0:S], w_gu[t][:, w, k, :], xT[:, k, :], start=(k == 0), stop=(k == KD - 1))
                            if w == 0 and k == 0 and t > 0:
                                i.then_inc(c_gu_used[t - 1].sem, 1)
                        i.then_inc(c.sem, 1)
                    if convolved:
                        tile = it * ring + t
                        act.wait_ge(c_gate.sem, base[id(c_gate)] + it * ring + t + 1)
                        act.activation(conv[:, t % 2, :], g[:, 0:S], ACT.Identity, scale=parc[:, 2, bass.ds(tile, 1)],
                                       bias=parc[:, 3, bass.ds(tile, 1)]).then_inc(c_conv.sem, 1)
                        for tap in (1, 0):
                            lag = 2 - tap
                            cs = conv[:, t % 2, lag:S]
                            dve.wait_ge(c_conv.sem, base[id(c_conv)] + (it * ring + t) * 3 + lag)
                            dve.scalar_tensor_tensor(out=cs, in0=g[:, 0:S - lag], scalar=parc[:, tap, bass.ds(tile, 1)], in1=cs,
                                                     op0=ALU.mult, op1=ALU.add).then_inc(c_conv.sem, 1)
                        act.wait_ge(c_conv.sem, base[id(c_conv)] + (it * ring + t) * 3 + 3)
                        act.activation(nonlin[:, t % 2, :], conv[:, t % 2, :], ACT.Gelu_apprx_tanh).then_inc(c_gelu.sem, 1)
                    else:
                        act.wait_ge(c_gate.sem, base[id(c_gate)] + it * ring + t + 1)
                        act.activation(nonlin[:, t % 2, :], g[:, 0:S], ACT.Silu).then_inc(c_gelu.sem, 1)
                    dve.wait_ge(c_gelu.sem, base[id(c_gelu)] + it * ring + t + 1)
                    dve.wait_ge(c_up.sem, base[id(c_up)] + it * ring + t + 1)
                    dve.scalar_tensor_tensor(out=actT[:, t, :], in0=nonlin[:, t % 2, :], scalar=1.0 if convolved else 0.5,
                                             in1=u[:, 0:S], op0=ALU.mult, op1=ALU.mult).then_inc(c_prod.sem, 1)
                for t in range(ring):
                    pe.wait_ge(c_prod.sem, base[id(c_prod)] + it * ring + t + 1)
                    pe.wait_ge(c_dn[t].sem, base[id(c_dn[t])] + (it + 1) * 16)
                    for m in range(M):
                        for h in range(2):
                            i = pe.matmul(bank[2 * m + h][:, :], actT[:, t, m * P:(m + 1) * P], w_dn[t][:, h * HALF:(h + 1) * HALF],
                                          start=False, stop=False, skip_group_check=True)
                            if t == 0 and m == 0 and h == 0:
                                i.then_inc(c_gu_used[ring - 1].sem, 1)
                    i.then_inc(c_dn_used[t].sem, 1)
            for t in range(ring):
                c_gu[t].n += 32 * turns
                c_dn[t].n += 16 * turns
                c_gu_used[t].n += turns
                c_dn_used[t].n += turns
            for c, per in ((c_gate, 1), (c_up, 1), (c_gelu, 1), (c_prod, 1), (c_conv, 3 if convolved else 0)):
                c.n += per * tiles
            for b in range(4):
                i = pe.matmul(bank[b][:, :], zeros[:, 0:P], zeros[:, :], start=False, stop=True, skip_group_check=True)
            return [did(pe, i)]


        def layer(l):
            at = 0
            gv = {}
            for name, width in (("mla_q_norm_2", 256), ("mla_kv_norm_2", 128), ("ax_q_norm_2", 64), ("ax_k_norm_2", 64),
                                ("diff_subln_2", 64), ("win_sink_2", 4)):
                gv[name] = gains[:, at:at + width]
                c_gain2.tick(act.dma_start(gv[name], all_partitions(A[name][l], width)), 16)
                at += width
            gv["lam"] = gains[:, at:at + 128]
            c_gain2.tick(act.dma_start(gv["lam"], all_partitions(A["diff_lambda_2"][l].rearrange("a b -> (a b)"), 128)), 16)
            at += 128
            gv["init"] = gains[:, at:at + 2]
            gains_in = c_gain2.tick(act.dma_start(gv["init"], all_partitions(C["lam_init"][l], 2)), 16)
            c_row2.tick(act.dma_start(rows[0:24, :], A["ln_g_2"][l].rearrange("a (k p) -> (a k) p", p=P)), 16)
            rows_in = c_row2.tick(act.dma_start(rows[24:48, :], A["ln_b_2"][l].rearrange("a (k p) -> (a k) p", p=P)), 16)
            need(pe, rows_in)
            t = did(pe, pe.transpose(bank[4][:, 0:48], rows[0:48, :], ident[0:48, 0:48]))
            need(dve, t)
            ln_ok = did(dve, dve.tensor_copy(lnT[:, :, :].rearrange("p a b -> p (a b)"), bank[4][:, 0:48]))
            need(act, ln_ok)

            def ln_rows(i, free):
                need(sp, *free)
                c_ln2.tick(sp.dma_start(gb[:, 0, :], all_partitions(A["ln_g_2"][l, i], D)), 16)
                return c_ln2.tick(sp.dma_start(gb[:, 1, :], all_partitions(A["ln_b_2"][l, i], D)), 16)

            def swiglu(i, ready):
                wgu, wd = A["ffn_w_gu_2"][l, i], A["ffn_w_down_2"][l, i]
                return ffn(lambda j: wgu[:, bass.ds(j * P, P)], lambda j: wgu[:, bass.ds(j * P + DFF2, P)],
                           lambda j: wd[bass.ds(j * P, P), :], FT2, SWI_RING, ready, False)

            gb_in = ln_rows(0, ())
            summed = swiglu(0, [ln_ok])
            done = norm(summed, ALPHA, EPS2, True, lambda k: lnT[:, 0, k:k + 1], lambda k: lnT[:, 3, k:k + 1], token_gain=gb_in)
            pool_done = done[-1:]

            W2 = A["w_in_2"][l]
            freed = [list(done), list(done)]
            chunk_ok = []
            for ci, c0 in enumerate(range(0, IN2, HALF)):
                width = min(HALF, IN2 - c0)
                slot, ld = load_wide(W2[:, c0:c0 + width], width)
                b0 = 2 * (ci % 2)
                t = token_chunk(xT, slot, ld, width, freed[ci % 2], [b0, b0 + 1])
                need(dve, t)
                need(act, t)
                k1 = did(dve, dve.tensor_copy(proj[:, 0, c0:c0 + width], bank[b0][:, 0:width]))
                k2_ = did(act, act.activation(proj[:, 1, c0:c0 + width], bank[b0 + 1][:, 0:width], ACT.Copy))
                freed[ci % 2] = [k1, k2_]
                chunk_ok += [k1, k2_]
            uq_in = c_uq.tick(sp.dma_start(wuq.rearrange("p a b -> p (a b)")[:, 0:768].rearrange("p (k n) -> p k n", k=2),
                                              A["mla_w_uq_2"][l].rearrange("(k p) n -> p k n", p=P)), 16)
            ukv_in = c_uq.tick(sp.dma_start(wukv[:, :, :].rearrange("p a b -> p (a b)"), A["mla_w_ukv_2"][l]), 16)
            gb_in = ln_rows(1, pool_done)
            wuq3 = wuq.rearrange("p a b -> p (a b)")[:, 0:768].rearrange("p (k n) -> p k n", k=2)
            wukv2 = wukv[:, :, :].rearrange("p a b -> p (a b)")

            need(dve, gains_in)
            lp = gv["lam"].rearrange("p (a b) -> p a b", a=4)
            lsum, lexp, lam = small[:, 0, 0:2], small[:, 1, 0:2], small[:, 2, 0:1]
            k = did(dve, dve.tensor_tensor(sq2[:, 0:64].rearrange("p (a b) -> p a b", a=2), lp[:, 0:4:2, :], lp[:, 1:4:2, :], ALU.mult))
            need(dve, k)
            k = did(dve, dve.tensor_reduce(lsum, sq2[:, 0:64].rearrange("p (a b) -> p a b", a=2), X, ALU.add))
            need(act, k)
            k = did(act, act.activation(lexp, lsum, ACT.Exp))
            need(dve, k)
            k = did(dve, dve.tensor_tensor(lam, lexp[:, 0:1], lexp[:, 1:2], ALU.subtract))
            need(dve, k)
            lam_ok = did(dve, dve.tensor_tensor(lam, lam, gv["init"][:, 0:1], ALU.add))
            nsink = small[:, 3, 0:4]
            sink_ok = did(dve, dve.tensor_scalar(nsink, gv["win_sink_2"], -1.0, None, ALU.mult))

            need(act, *chunk_ok, gains_in)
            need(dve, *chunk_ok)
            for m in range(M):
                did(act, act.activation(cn[:, m, 0:256], proj[:, m, MLA_Q:MLA_Q + 256], ACT.Square, accum_out=hq[:, m, 0:1]))
                k = did(act, act.activation(cn[:, m, 256:384], proj[:, m, MLA_KV:MLA_KV + 128], ACT.Square, accum_out=hq[:, m, 1:2]))
                need(dve, k)
                need(dve, (c_dve, c_dve.n))
                k = did(dve, dve.tensor_tensor(sq2, proj[:, m, AX_Q:AX_Q + 384], proj[:, m, AX_Q:AX_Q + 384], ALU.mult))
                need(dve, k)
                k = did(dve, dve.tensor_reduce(hq[:, m, 2:8], sq2.rearrange("p (h d) -> p h d", d=HD), X, ALU.add))
            need(dve, k)
            hr = hq[:, :, 8:16]
            did(dve, dve.tensor_scalar(hr[:, :, 0:1], hq[:, :, 0:1], 1.0 / 256, EPS2, ALU.mult, ALU.add))
            did(dve, dve.tensor_scalar(hr[:, :, 1:2], hq[:, :, 1:2], 1.0 / 128, EPS2, ALU.mult, ALU.add))
            k = did(dve, dve.tensor_scalar(hr[:, :, 2:8], hq[:, :, 2:8], 1.0 / HD, EPS2, ALU.mult, ALU.add))
            need(act, k)
            k = did(act, act.activation(hr, hr, ACT.Sqrt))
            need(dve, k)
            k = did(dve, dve.reciprocal(hr, hr))
            need(dve, k)
            for m in range(M):
                did(dve, dve.scalar_tensor_tensor(out=cn[:, m, 0:256], in0=proj[:, m, MLA_Q:MLA_Q + 256], scalar=hr[:, m, 0:1],
                                                  in1=gv["mla_q_norm_2"], op0=ALU.mult, op1=ALU.mult))
                cn_ok = did(dve, dve.scalar_tensor_tensor(out=cn[:, m, 256:384], in0=proj[:, m, MLA_KV:MLA_KV + 128],
                                                          scalar=hr[:, m, 1:2], in1=gv["mla_kv_norm_2"], op0=ALU.mult, op1=ALU.mult))
            for m in range(M):
                axh = proj[:, m, AX_Q:AX_Q + 384].rearrange("p (h d) -> p h d", d=HD)
                k = did(dve, dve.tensor_tensor(axh, axh, bc(hr[:, m, 2:8], 2, HD), ALU.mult))
                need(dve, k)
                did(dve, dve.tensor_tensor(axh[:, 0:4], axh[:, 0:4], bc(gv["ax_q_norm_2"], 1, 4), ALU.mult))
                k = did(dve, dve.tensor_tensor(axh[:, 4:6], axh[:, 4:6], bc(gv["ax_k_norm_2"], 1, 2), ALU.mult))

            tf = {6: (), 7: ()}
            for j in range(3):
                b = 6 + j % 2
                need(pe, cn_ok, *tf[b])
                for m in range(M):
                    i = pe.transpose(bank[b][:, m * P:(m + 1) * P], cn[:, m, j * P:(j + 1) * P], ident[:, :])
                t = did(pe, i)
                need(act, t)
                ct_ok = did(act, act.activation(cT[:, j, :], bank[b][:, 0:S], ACT.Copy))
                tf[b] = (ct_ok,)
            need(pe, ct_ok, uq_in, ukv_in, *freed[0], *freed[1])
            for m in range(M):
                for k_ in range(2):
                    pe.matmul(bank[m][:, 0:384], cT[:, k_, m * P:(m + 1) * P], wuq3[:, k_, :], start=(k_ == 0), stop=(k_ == 1))
                i = pe.matmul(bank[2 + m][:, :], cT[:, 2, m * P:(m + 1) * P], wukv2, start=True, stop=True)
            t = did(pe, i)
            mq = n[:, :, 0:384].rearrange("p m (h d) -> p m h d", d=96)
            mkk = n[:, :, 384:768].rearrange("p m (h d) -> p m h d", d=96)
            mv_ = n[:, :, 768:1024].rearrange("p m (h d) -> p m h d", d=HD)
            need(act, t, *done)
            need(dve, t, *done)
            for m in range(M):
                k = did(act, act.activation(n[:, m, 0:384], bank[m][:, 0:384], ACT.Copy))
                kv4 = bank[2 + m][:, :].rearrange("p (h d) -> p h d", d=128)
                did(act, act.activation(mkk[:, m, :, 0:NOPE], kv4[:, :, 0:NOPE], ACT.Copy))
                mla_copied = did(act, act.activation(mv_[:, m, :, :], kv4[:, :, NOPE:128], ACT.Copy))
            need(dve, mla_copied)

            def rotate(m, a, b_, cosv, sinv, heads, tmp):
                t1, t2 = tmp[:, m, 0, 0:16 * heads].rearrange("p (h d) -> p h d", d=16), tmp[:, m, 1, 0:16 * heads].rearrange("p (h d) -> p h d", d=16)
                cv, sv = bc(cosv, 1, heads), bc(sinv, 1, heads)
                need(dve, (c_dve, c_dve.n))
                did(dve, dve.tensor_tensor(t1, a, sv, ALU.mult))
                k = did(dve, dve.tensor_tensor(t2, b_, sv, ALU.mult))
                need(dve, k)
                did(dve, dve.tensor_tensor(a, a, cv, ALU.mult))
                k = did(dve, dve.tensor_tensor(b_, b_, cv, ALU.mult))
                need(dve, k)
                did(dve, dve.tensor_tensor(a, a, t2, ALU.subtract))
                return did(dve, dve.tensor_tensor(b_, b_, t1, ALU.add))

            for m in range(M):
                rp = rope[:, m, :].rearrange("p (a b) -> p a b", a=6)
                rotate(m, mq[:, m, :, 64:80], mq[:, m, :, 80:96], rp[:, 0, :], rp[:, 1, :], 4, rt)
                kr = proj[:, m, MLA_KR:MLA_KR + 32].rearrange("p (a b) -> p a b", a=2)
                k = rotate(m, kr[:, 0:1, :], kr[:, 1:2, :], rp[:, 0, :], rp[:, 1, :], 1, rt)
                need(dve, k)
                mla_ok = did(dve, dve.tensor_copy(mkk[:, m, :, 64:96], bc(proj[:, m, MLA_KR:MLA_KR + 32], 1, 4)))
                axh = proj[:, m, AX_Q:AX_Q + 384].rearrange("p (h d) -> p h d", d=HD)
                for hf in range(2):
                    ax_ok = rotate(m, axh[:, :, 32 * hf:32 * hf + 16], axh[:, :, 32 * hf + 16:32 * hf + 32], rp[:, 2 + hf, :], rp[:, 4 + hf, :], 6, rt)

            sets = [(qT, kT), (qT2, kT2)]
            proj_h = {}

            def views(kind):
                if kind == "win":
                    return ([(lambda m, h=h: proj[:, m, WIN_Q + h * HD:WIN_Q + (h + 1) * HD]) for h in range(4)],
                            [(lambda m, h=h: proj[:, m, WIN_K + h * HD:WIN_K + (h + 1) * HD]) for h in range(2)], HD)
                if kind == "mla":
                    return ([(lambda m, h=h: mq[:, m, h, :]) for h in range(4)], [(lambda m, h=h: mkk[:, m, h, :]) for h in range(4)], 96)
                if kind == "ax":
                    return ([(lambda m, h=h: proj[:, m, AX_Q + h * HD:AX_Q + (h + 1) * HD]) for h in range(4)],
                            [(lambda m, h=h: proj[:, m, AX_Q + 256 + h * HD:AX_Q + 256 + (h + 1) * HD]) for h in range(2)], HD)
                return ([(lambda m, h=h: proj[:, m, DF_Q + h * HD:DF_Q + (h + 1) * HD]) for h in range(4)],
                        [(lambda m, h=h: proj[:, m, DF_K + h * HD:DF_K + (h + 1) * HD]) for h in range(4)], HD)

            ready_of = {"win": [*chunk_ok], "mla": [mla_ok, mla_copied], "ax": [ax_ok], "dif": [*chunk_ok]}
            kinds = ["win", "dif", "ax", "mla"]
            tr_state = {"free": {6: tf[6], 7: tf[7]}, "n": 0}
            set_reads = [(), ()]

            def transposes(kind):
                si = kinds.index(kind) % 2
                q_, k_ = sets[si]
                qv, kv, dim = views(kind)
                need(pe, *ready_of[kind])
                for dst, vs in ((q_, qv), (k_, kv)):
                    for p0 in range(0, len(vs), 2):
                        b = 6 + tr_state["n"] % 2
                        tr_state["n"] += 1
                        need(pe, *tr_state["free"][b])
                        for z in range(2):
                            for m in range(M):
                                i = pe.transpose(bank[b][0:dim, (2 * z + m) * P:(2 * z + m + 1) * P], vs[p0 + z](m), ident[:, :])
                        t = did(pe, i)
                        need(act, t, *set_reads[si])
                        e = did(act, act.activation(dst[0:dim, p0:p0 + 2, :], bank[b][0:dim, :].rearrange("p (a b) -> p a b", a=2), ACT.Copy))
                        tr_state["free"][b] = (e,)
                ready_t[kind] = e

            ready_t = {}
            units = [(kind, m, pr) for kind in kinds for pr in range(4 if kind == "dif" else 2) for m in range(M)]
            out_col = {"win": 0, "mla": 256, "ax": 512, "dif": 768}
            cat = proj
            v_of = {"win": (proj, WIN_V), "mla": (n, 768), "ax": (proj, AX_V), "dif": (proj, DF_V)}
            om = [gbo[:, m, :] for m in range(M)]
            st = {}
            bank_s, bank_t, bank_o = {0: (), 1: ()}, {2: (), 3: ()}, {4: (), 5: ()}
            for d_ in (bank_s, bank_t, bank_o):
                for b in d_:
                    d_[b] = (mla_copied, ln_ok)
            pb_read, ptb_read = [(), ()], [(), ()]

            def stage0(u):
                kind, m, pr = units[u]
                si = kinds.index(kind) % 2
                q_, k_ = sets[si]
                i2 = u % 2
                need(pe, ready_t[kind], *bank_s[i2])
                for z in range(2):
                    if kind == "dif":
                        r0, qh, kh, dim = 32 * z, pr, pr, 32
                    else:
                        r0, qh, dim = 0, 2 * pr + z, (96 if kind == "mla" else HD)
                        kh = qh if kind == "mla" else pr
                    i = pe.matmul(bank[i2][:, z * S:(z + 1) * S], q_[r0:r0 + dim, qh, m * P:(m + 1) * P], k_[r0:r0 + dim, kh, :],
                                  start=True, stop=True)
                    if kind == "dif" and z == 0:
                        need(pe, did(pe, i))
                t = did(pe, i)
                if u + 1 == len(units) or units[u + 1][0] != kind:
                    set_reads[si] = (t,)
                s3 = bank[i2][:, :].rearrange("p (a b) -> p a b", a=2)
                p3 = pb[:, i2, :].rearrange("p (a b) -> p a b", a=2)
                nm, sm, rr = small[:, 4 + i2, 0:2], small[:, 6 + i2, 0:2], small[:, 8 + i2, 0:2]
                scale = {"win": 1.0, "dif": 1.0, "ax": SCALE_C, "mla": SCALE_B}[kind]
                need(dve, t, *pb_read[i2])
                if kind in ("win", "dif"):
                    bias = win_bias[:, m, 2 * pr:2 * pr + 2, :] if kind == "win" else bc(dif_bias[:, m, pr, :], 1, 2)
                    k = did(dve, dve.scalar_tensor_tensor(out=p3, in0=s3, scalar=SCALE_A if kind == "win" else SCALE_D, in1=bias,
                                                          op0=ALU.mult, op1=ALU.add))
                    bank_s[i2] = (k,)
                    src = p3
                    need(dve, k)
                else:
                    src = s3
                k = did(dve, dve.tensor_reduce(nm, src, X, ALU.max, negate=True))
                need(dve, k)
                if kind == "win":
                    k = did(dve, dve.tensor_tensor(nm, nm, nsink[:, 2 * pr:2 * pr + 2], ALU.min))
                elif scale != 1.0:
                    k = did(dve, dve.tensor_scalar(nm, nm, scale, None, ALU.mult))
                need(act, k, *pb_read[i2])
                for z in range(2):
                    k = did(act, act.activation(p3[:, z, :], src[:, z, :], ACT.Exp, scale=scale, bias=nm[:, z:z + 1], accum_out=sm[:, z:z + 1]))
                if kind in ("ax", "mla"):
                    bank_s[i2] = (k,)
                if kind == "win":
                    ex = small[:, 10 + i2, 0:2]
                    for z in range(2):
                        k = did(act, act.activation(ex[:, z:z + 1], nm[:, z:z + 1], ACT.Exp, bias=gv["win_sink_2"][:, 2 * pr + z:2 * pr + z + 1]))
                    need(dve, k)
                    k = did(dve, dve.tensor_tensor(sm, sm, ex, ALU.add))
                need(dve, k)
                k = did(dve, dve.reciprocal(rr, sm))
                if kind == "dif":
                    need(dve, k)
                    k = did(dve, dve.tensor_scalar(rr[:, 1:2], rr[:, 1:2], lam, None, ALU.mult))
                    need(dve, k)
                    k = did(dve, dve.tensor_scalar(p3[:, 1, :], p3[:, 1, :], rr[:, 1:2], None, ALU.mult))
                    need(dve, k)
                    k = did(dve, dve.scalar_tensor_tensor(out=p3[:, 0, :], in0=p3[:, 0, :], scalar=rr[:, 0:1], in1=p3[:, 1, :],
                                                          op0=ALU.mult, op1=ALU.subtract))
                st[u] = k

            def stage1(u):
                kind, m, pr = units[u]
                i2 = u % 2
                maps = 1 if kind == "dif" else 2
                b = 2 + i2
                need(pe, st[u], *bank_t[b])
                for z in range(maps):
                    for kt in range(M):
                        i = pe.transpose(bank[b][:, (2 * z + kt) * P:(2 * z + kt + 1) * P], pb[:, i2, z * S + kt * P:z * S + (kt + 1) * P], ident[:, :])
                t = did(pe, i)
                pb_read[i2] = (t,)
                need(act, t, *ptb_read[i2])
                w = 2 * maps * P
                k = did(act, act.activation(ptb[:, i2, 0:w], bank[b][:, 0:w], ACT.Copy))
                bank_t[b] = (k,)
                st[u] = (st[u], k)

            def stage2(u):
                kind, m, pr = units[u]
                i2 = u % 2
                maps = 1 if kind == "dif" else 2
                b = 4 + i2
                sdone, k = st[u]
                need(pe, k, *bank_o[b])
                vb, v0 = v_of[kind]
                for z in range(maps):
                    vh = {"win": pr, "ax": pr, "mla": 2 * pr + z, "dif": pr}[kind]
                    for kt in range(M):
                        i = pe.matmul(bank[b][:, z * HD:(z + 1) * HD], ptb[:, i2, (2 * z + kt) * P:(2 * z + kt + 1) * P],
                                      vb[:, kt, v0 + vh * HD:v0 + (vh + 1) * HD], start=(kt == 0), stop=(kt == 1))
                t = did(pe, i)
                ptb_read[i2] = (t,)
                need(dve, t)
                if kind == "dif":
                    o0 = out_col[kind] + pr * HD
                    k = did(dve, dve.tensor_copy(om[m][:, o0:o0 + HD], bank[b][:, 0:HD]))
                else:
                    o0 = out_col[kind] + 2 * pr * HD
                    rr = small[:, 8 + i2, 0:2]
                    k = did(dve, dve.tensor_tensor(om[m][:, o0:o0 + P].rearrange("p (a b) -> p a b", a=2),
                                                   bank[b][:, 0:P].rearrange("p (a b) -> p a b", a=2), bc(rr, 2, HD), ALU.mult))
                bank_o[b] = (k,)
                return k

            need(dve, lam_ok, sink_ok)
            need(act, sink_ok)
            transposes("win")
            for u in range(len(units) + 1):
                if 1 <= u:
                    stage1(u - 1)
                if u < len(units):
                    if u + 1 < len(units) and units[u + 1][0] not in ready_t:
                        transposes(units[u + 1][0])
                    stage0(u)
                if 1 <= u:
                    o_ok = stage2(u - 1)
            need(dve, o_ok)
            for m in range(M):
                d3 = om[m][:, 768:1024]
                need(dve, (c_dve, c_dve.n))
                k = did(dve, dve.tensor_tensor(sq2[:, 0:256], d3, d3, ALU.mult))
                need(dve, k)
                k = did(dve, dve.tensor_reduce(hq[:, m, 0:4], sq2[:, 0:256].rearrange("p (h d) -> p h d", d=HD), X, ALU.add))
            need(dve, k)
            k = did(dve, dve.tensor_scalar(hq[:, :, 0:4], hq[:, :, 0:4], 1.0 / HD, EPS2, ALU.mult, ALU.add))
            need(act, k)
            k = did(act, act.activation(hq[:, :, 0:4], hq[:, :, 0:4], ACT.Sqrt))
            need(dve, k)
            k = did(dve, dve.reciprocal(hq[:, :, 0:4], hq[:, :, 0:4]))
            need(dve, k)
            k = did(dve, dve.tensor_scalar(hq[:, :, 0:4], hq[:, :, 0:4], gv["init"][:, 1:2], None, ALU.mult))
            need(dve, k)
            for m in range(M):
                d3 = om[m][:, 768:1024].rearrange("p (h d) -> p h d", d=HD)
                k = did(dve, dve.tensor_tensor(d3, d3, bc(hq[:, m, 0:4], 2, HD), ALU.mult))
                need(dve, k)
                k = did(dve, dve.tensor_tensor(d3, d3, bc(gv["diff_subln_2"], 1, 4), ALU.mult))
            ct = transpose_tiles(gbo, catT, None, None, [k], extra=(*tr_state["free"][6], *tr_state["free"][7]))
            summed = out_product(A["w_out_2"][l], [*ct, *[z for d_ in (bank_s, bank_t) for v in d_.values() for z in v]])
            done = norm(summed, ALPHA, EPS2, True, lambda k: lnT[:, 1, k:k + 1], lambda k: lnT[:, 4, k:k + 1], token_gain=gb_in)
            summed = swiglu(1, done)
            gb_in = ln_rows(2, done[-1:])
            norm(summed, ALPHA, EPS2, True, lambda k: lnT[:, 2, k:k + 1], lambda k: lnT[:, 5, k:k + 1], token_gain=gb_in)


        def scatter_rows(dst_rows, at, dram1d, count):
            c_row.tick(pool.dma_start(dst_rows[at:at + count, :], dram1d.rearrange("(a n) -> a n", n=P)), 16)

        ident_in = c_ident.tick(sp.dma_start(ident[:, :], C["ident"]), 16)
        k0 = did(pool, pool.memset(zeros[:, :], 0.0))
        c = Carve()
        o_tok = n
        ig = proj[:, :, 0:D]
        gq, gk, lf = c(3, S), c(3, S), c(3, S)
        cum = c(2, 3, S)
        dd, ee = c(3 * S), c(3 * S)
        qs = c(2, 3, S)
        ks = c(2, 3, S)
        zf = ks[:, 0, 0:2, :]
        keep_at = c.at
        scoreT = [c(8, P) for _ in range(3)]
        keep = big[:, keep_at:keep_at + 2 * 3 * S].rearrange("p (a b c) -> p a b c", a=2, b=3)
        masks = c(7, P)
        c_g_end = c.at
        gain_bc = c(2, 256)
        hsum, hrs = c(M, 8), c(M, 8)

        PARS = [("norm_mix", 8), ("norm_ffn", 8), ("norm_final", 8), ("rg_b_a", 4), ("rg_b_x", 4), ("rg_lambda", 4),
                ("rg_conv_w", 16), ("rg_conv_b", 4), ("gla_b_gate", 1), ("hgrn_lower_bounds", 2)]
        off, at = {}, 0
        for name, count in PARS:
            v = A[name]
            v = v if len(v.shape) == 1 else (v.rearrange("a n -> (a n)") if len(v.shape) == 2 else v.rearrange("a b n -> (a b n)"))
            scatter_rows(rows, at, v, count)
            off[name] = at
            at += count
        n_par = at
        scatter_rows(rows2, 0, A["ffn_conv_w"].rearrange("a b n -> (a b n)"), 3 * FT1)
        scatter_rows(rows2, 3 * FT1, A["ffn_conv_b"].rearrange("a n -> (a n)"), FT1)
        rows_in = (c_row, c_row.n)

        def load_x(m):
            return c_out.tick(sp.dma_start(x[:, m, :], A["x"][0, m * P:(m + 1) * P, :]), 16)

        x_in = [load_x(m) for m in range(M)]
        x_in = [x_in[-1]]
        par_in = []
        par_in.append(c_par.tick(sp.dma_start(masks, C["masks"].bitcast(F32)), 16))
        par_in.append(c_par.tick(sp.dma_start(keep, C["keep"]), 16))
        par_in.append(c_gain.tick(pool.dma_start(gain_bc[:, 0, :], all_partitions(A["hgrn_norm"][0], 256)), 16))
        par_in.append(c_gain.tick(pool.dma_start(gain_bc[:, 1, :], all_partitions(A["gla_norm"][0], 256)), 16))

        need(pe, ident_in, rows_in)
        pe.transpose(bank[0][:, 0:n_par], rows[0:n_par, :], ident[0:n_par, 0:n_par])
        t = did(pe, pe.transpose(bank[0][:, P:P + 4 * FT1], rows2[0:4 * FT1, :], ident[0:4 * FT1, 0:4 * FT1]))
        need(dve, t)
        did(dve, dve.tensor_copy(par1[:, 0:n_par], bank[0][:, 0:n_par]))
        par_ok = did(dve, dve.tensor_copy(parc[:, :, :].rearrange("p a b -> p (a b)"), bank[0][:, P:P + 4 * FT1]))

        def col(name, i=0, count=1):
            return par1[:, off[name] + i:off[name] + i + count]

        need(act, par_ok)
        need(pe, par_ok)
        need(dve, *x_in, k0, par_ok)
        need(act, *x_in)
        need(pe, k0)
        hT_ok = norm([], 1.0, EPS1, False, lambda k: col("norm_mix", k), None)

        spl = c(4)
        e1 = did(act, act.activation(spl, col("rg_lambda", 0, 4), ACT.Exp, scale=-1.0))
        need(act, e1)
        e1 = did(act, act.activation(spl, spl, ACT.Ln, bias=1.0))
        need(act, e1)
        spl_ok = did(act, act.activation(spl, spl, ACT.Copy, scale=-8.0))
        lb, oml = c(2), c(2)
        lbt = c(2)
        e2 = did(dve, dve.tensor_tensor(lbt, col("hgrn_lower_bounds", 0, 2), col("hgrn_lower_bounds", 0, 2), ALU.subtract))
        need(act, e2)
        e2 = did(act, act.activation(lb, lbt, ACT.Exp))
        need(dve, e2)
        e2 = did(dve, dve.reciprocal(lbt, lb))
        need(dve, e2)
        e2 = did(dve, dve.tensor_tensor(lbt, lb, lbt, ALU.mult))
        need(dve, e2)
        e2 = did(dve, dve.tensor_tensor(lb, lbt, lbt, ALU.subtract))
        need(dve, e2)
        e2 = did(dve, dve.tensor_scalar(oml, lb, -1.0, 1.0, ALU.mult, ALU.add))
        lb_ok = e2

        xp = c(4, S + 4)
        g4 = gbo[:, :, :].rearrange("p a (b c) -> p (a b) c", c=S)
        b4 = gb[:, :, :].rearrange("p a (b c) -> p (a b) c", c=S)
        gbt, ra, xc, gi = g4[:, 0:4, :], g4[:, 4:8, :], b4[:, 0:4, :], b4[:, 4:8, :]
        wab = catT
        wab = catT[:, :, 0:P]
        lr = c(S)
        wup = c(P)
        zw = did(pool, pool.memset(catT[:, :, :], 0.0))
        zx = did(pool, pool.memset(xp, 0.0))
        need(pool, zw)
        for g, name in enumerate(("rg_w_a", "rg_w_x")):
            for two in range(2):
                w_in_m = c_lng.tick(pool.dma_start(wab[two * 64:two * 64 + 64, 4 * g:4 * g + 4, two * 64:two * 64 + 64],
                                                   A[name][0].rearrange("(b t) i j -> t i b j", t=2)[two]), 16)
        wup_in = c_lng.tick(pool.dma_start(wup[0:LR_RANK, :], A["gla_w_gate_up"][0]), 16)
        w_in_m = wup_in

        W = A["w_in"][0]
        t_freed = {}
        ev = {"n": 0}

        def t_block(slot, c0, width, b, evacuate):
            need(pe, *t_freed.get(b, ()))
            for k in range(KD):
                i = pe.matmul(bank[b][0:width, 0:S], wide[slot][:, k, c0:c0 + width], xT[:, k, :],
                              start=(k == 0), stop=(k == KD - 1))
            t = did(pe, i)
            e = evacuate(bank[b][0:width, 0:S], t)
            t_freed[b] = (e,)
            return t, e

        def copy_by(eng, dst, scale=None):
            def go(src, t):
                need(eng, t)
                if eng is dve:
                    return did(dve, dve.tensor_copy(dst, src) if scale is None else dve.tensor_scalar(dst, src, scale, None, ALU.mult))
                return did(act, act.activation(dst, src, ACT.Copy) if scale is None else act.activation(dst, src, ACT.Copy, scale=scale))
            return go

        need(pe, *hT_ok)
        slot, ld = load_wide(W[:, 0:512], 512)
        slot2, ld2 = load_wide(W[:, C_Q:C_Q + 256], 256)
        need(pe, ld)
        _, q0 = t_block(slot, 0, P, 4, copy_by(dve, gq[:, 0, :]))
        _, q1 = t_block(slot, 128, P, 5, copy_by(act, gq[:, 1, :]))
        _, f0 = t_block(slot, 256, P, 6, copy_by(dve, zf[:, 0, :]))
        t, f1 = t_block(slot, 384, P, 7, copy_by(act, zf[:, 1, :]))
        wide_state["free"][slot] = t
        need(pe, ld2)
        _, q2 = t_block(slot2, 0, P, 4, copy_by(dve, gq[:, 2, :], 32 ** -0.5))
        t, k2 = t_block(slot2, 128, P, 5, copy_by(act, gk[:, 2, :]))
        wide_state["free"][slot2] = t
        slot, ld = load_wide(W[:, C_LR:C_LR + LR_RANK], LR_RANK)
        need(pe, ld)
        t, l0 = t_block(slot, 0, LR_RANK, 6, copy_by(dve, lr[0:LR_RANK, :]))
        wide_state["free"][slot] = t
        need(act, f0, f1)
        sg = did(act, act.activation(ee[:, 0:512], zf.rearrange("p a b -> p (a b)"), ACT.Sigmoid))
        kg = did(act, act.activation(gk[:, 0:2, :], zf, ACT.Sigmoid, scale=-1.0))
        need(dve, sg, kg, lb_ok)
        for b in range(2):
            k = did(dve, dve.tensor_scalar(gk[:, b, :], gk[:, b, :], oml[:, b:b + 1], None, ALU.mult))
            k = did(dve, dve.tensor_scalar(lf[:, b, :], ee[:, b * S:(b + 1) * S], oml[:, b:b + 1], lb[:, b:b + 1], ALU.mult, ALU.add))
        need(dve, k)
        k = did(dve, dve.tensor_scalar(lf[:, 0:2, :], lf[:, 0:2, :], F_FLOOR, None, ALU.max))
        need(pe, l0, wup_in)
        need(pe, *t_freed[7])
        t = did(pe, pe.matmul(bank[7][:, 0:S], wup[0:LR_RANK, :], lr[0:LR_RANK, :], start=True, stop=True))
        need(dve, t)
        z2 = dd[:, 0:S]
        a2 = dd[:, S:2 * S]
        kz = did(dve, dve.tensor_scalar(z2, bank[7][:, 0:S], col("gla_b_gate"), None, ALU.add))
        t_freed[7] = (kz,)
        need(act, kz, k)
        ka = did(act, act.activation(a2, z2, ACT.Abs))
        kf = did(act, act.activation(lf[:, 0:2, :], lf[:, 0:2, :], ACT.Ln))
        need(act, ka)
        ka = did(act, act.activation(a2, a2, ACT.Exp, scale=-1.0))
        need(act, ka)
        ka = did(act, act.activation(a2, a2, ACT.Ln, bias=1.0))
        need(dve, kz)
        z3 = dd[:, 2 * S:3 * S]
        kz = did(dve, dve.tensor_scalar(z3, z2, 0.0, 1.0 / 16, ALU.min, ALU.mult))
        need(dve, ka, kz)
        k = did(dve, dve.scalar_tensor_tensor(out=lf[:, 2, :], in0=a2, scalar=-1.0 / 16, in1=z3, op0=ALU.mult, op1=ALU.add))
        need(dve, k, kf, *par_in)
        for w in range(2):
            k = did(dve, dve.tensor_tensor_scan(cum[:, w].rearrange("p a b -> p (a b)"), keep[:, w].rearrange("p a b -> p (a b)"),
                                                lf.rearrange("p a b -> p (a b)"), 0.0, ALU.mult, ALU.add))
        cum_ok = k

        for half, c0 in ((0, A_I), (1, C_V)):
            slot, ld = load_wide(W[:, c0:c0 + 512], 512)
            t = token_chunk(xT, slot, ld, 512, [], [0 + 2 * half, 1 + 2 * half])
            need(act, t)
            for m in range(M):
                ig_ok = did(act, act.activation(ig[:, m, half * 512:half * 512 + 512], bank[2 * half + m][:, :], ACT.Copy))
        slot, ld = load_wide(W[:, B_X:B_X + 512], 512)
        need(pe, ld)
        need(act, zx)
        for b in range(4):
            t, bx = t_block(slot, b * P, P, 4 + b, copy_by(act, xp[:, b, 3:3 + S]))
        wide_state["free"][slot] = t
        slot, ld = load_wide(W[:, B_G:B_G + 512], 512)
        need(pe, ld)
        for b in range(4):
            t, bg = t_block(slot, b * P, P, 4 + b, copy_by(act, gbt[:, b, :]))
        wide_state["free"][slot] = t

        need(dve, bx)
        for b in range(4):
            k = did(dve, dve.tensor_scalar(xc[:, b, :], xp[:, b, 3:3 + S], col("rg_conv_w", 12 + b), col("rg_conv_b", b), ALU.mult, ALU.add))
            for tap in range(3):
                need(dve, k)
                k = did(dve, dve.scalar_tensor_tensor(out=xc[:, b, :], in0=xp[:, b, tap:tap + S], scalar=col("rg_conv_w", 4 * tap + b),
                                                      in1=xc[:, b, :], op0=ALU.mult, op1=ALU.add))
        need(pe, k, w_in_m, bg, ig_ok)
        for b in range(4):
            pe.matmul(bank[4 + b // 2][:, (b % 2) * S:(b % 2 + 1) * S], wab[:, b, :], xc[:, b, :], start=True, stop=True)
            i = pe.matmul(bank[6 + b // 2][:, (b % 2) * S:(b % 2 + 1) * S], wab[:, 4 + b, :], xc[:, b, :], start=True, stop=True)
        t = did(pe, i)
        need(dve, t)
        for b in range(4):
            cols = slice((b % 2) * S, (b % 2 + 1) * S)
            did(dve, dve.tensor_scalar(ra[:, b, :], bank[4 + b // 2][:, cols], col("rg_b_a", b), None, ALU.add))
            k = did(dve, dve.tensor_scalar(gi[:, b, :], bank[6 + b // 2][:, cols], col("rg_b_x", b), None, ALU.add))
        rg_psum = k
        need(act, k)
        sr_ = did(act, act.activation(ra, ra, ACT.Sigmoid))
        si_ = did(act, act.activation(gi, gi, ACT.Sigmoid))
        need(dve, sr_, si_, spl_ok)
        for b in range(4):
            k = did(dve, dve.tensor_scalar(ra[:, b, :], ra[:, b, :], spl[:, b:b + 1], None, ALU.mult))
        k = did(dve, dve.tensor_tensor(gi, gi, xc, ALU.mult))
        need(act, k)
        aa, th = xc, xp[:, :, 0:S]
        tha = did(act, act.activation(th, ra, ACT.Tanh))
        exa = did(act, act.activation(aa, ra, ACT.Exp))
        need(dve, exa, tha)
        k = did(dve, dve.tensor_tensor(ra, aa, aa, ALU.mult))
        need(dve, k)
        k = did(dve, dve.scalar_tensor_tensor(out=ra, in0=ra, scalar=1.0, in1=th, op0=ALU.add, op1=ALU.mult))
        need(dve, k)
        k = did(dve, dve.tensor_scalar(ra, ra, -1.0, 2.0 ** -116, ALU.mult, ALU.max))
        need(act, k)
        k = did(act, act.activation(ra, ra, ACT.Sqrt))
        ge = did(act, act.activation(gbt, gbt, ACT.Gelu_apprx_tanh))
        need(dve, k, ge)
        k = did(dve, dve.tensor_tensor(ra, ra, gi, ALU.mult))
        need(dve, k)
        for b in range(4):
            k = did(dve, dve.tensor_tensor_scan(gi[:, b, :], aa[:, b, :], ra[:, b, :], 0.0, ALU.mult, ALU.add))
        need(dve, k)
        rg_ok = did(dve, dve.tensor_tensor(catT[:, 2:6, :], gi, gbt, ALU.mult))

        mk = masks.bitcast(I32)
        bank_free = [(rg_psum,)] * 8
        sc_mark = None
        q_reads = [(), ()]
        for lev in range(len(LEVELS) + 1):
            if lev == 0:
                qq, kk, ready = gq, gk, [q0, q1, q2, k2, cum_ok]
            else:
                s = LEVELS[lev - 1]
                cw = cum[:, 0 if s <= CHUNK // 2 else 1].rearrange("p a (n w) -> p (a n) w", w=2 * s)
                mid = bc(cw[:, :, s - 1], 2, 2 * s)
                need(dve, cum_ok, *([sc_mark] if sc_mark else []))
                k = did(dve, dve.tensor_tensor(dd.rearrange("p (n w) -> p n w", w=2 * s), cw, mid, ALU.subtract))
                need(act, k)
                k = did(act, act.activation(dd, dd, ACT.Abs))
                need(act, k, *q_reads[(lev + 1) % 2])
                k = sc_mark = did(act, act.activation(ee, dd, ACT.Exp, scale=-1.0))
                need(dve, k, *q_reads[lev % 2])
                need(pool, k, *q_reads[lev % 2])
                qq, kk = qs[:, lev % 2], ks[:, lev % 2]
                e3 = ee.rearrange("p (a b) -> p a b", a=3)
                kq = did(dve, dve.tensor_tensor(qq, gq, e3, ALU.mult))
                kp = did(pool, pool.tensor_tensor(kk, gk, e3, ALU.mult))
                ready = [kq, kp]
                sc_mark = kq
                sc_pool = kp
                need(act, kq, kp)
            need(pe, *ready)
            pairs = [(0, 0, 0), (1, 1, 1)] if lev <= 7 else [(0, 1, 2)]
            for kt, qt, dst in pairs:
                bs = [4 * (dst % 2) + b for b in range(4)]
                for b in bs:
                    need(pe, *bank_free[b])
                for r in range(3):
                    for b in range(4):
                        if r < len(BANK_HEADS[b]):
                            head, base, rws, blk = BANK_HEADS[b][r]
                            i = pe.matmul(bank[bs[b]][:, r * P:(r + 1) * P], kk[base:base + rws, blk, kt * P:(kt + 1) * P],
                                          qq[base:base + rws, blk, qt * P:(qt + 1) * P], start=True, stop=True)
                t = did(pe, i)
                need(dve, t)
                for b in range(4):
                    w = len(BANK_HEADS[b])
                    o = scoreT[dst][:, BANK_SLOT[b]:BANK_SLOT[b] + w, :]
                    p3 = bank[bs[b]][:, 0:w * P].rearrange("p (a b) -> p a b", a=w)
                    if lev == 0:
                        i = dve.tensor_tensor(o, p3, bc(ident[:, :], 1, w), ALU.mult)
                    elif dst == 2:
                        i = dve.tensor_copy(o, p3)
                    else:
                        if b == 0:
                            need(dve, (c_dve, c_dve.n))
                        i = dve.copy_predicated(o, bc(mk[:, lev - 1, :], 1, w), p3)
                    k = did(dve, i)
                    bank_free[bs[b]] = (k,)
            q_reads[lev % 2] = (t,)
        need(pe, k, ig_ok)
        for m in range(M):
            for b in range(4):
                for r, (head, _, _, _) in enumerate(BANK_HEADS[b]):
                    sl = BANK_SLOT[b] + r
                    v0 = (head * HD) if head < 4 else 512 + (head - 4) * HD
                    o = bank[m][:, head * HD:(head + 1) * HD]
                    if m:
                        pe.matmul(o, scoreT[2][:, sl, :], ig[:, 0, v0:v0 + HD], start=True, stop=False)
                    i = pe.matmul(o, scoreT[m][:, sl, :], ig[:, m, v0:v0 + HD], start=(m == 0), stop=True)
        t = did(pe, i)
        sq = dd[:, 0:512]
        need(act, t, ig_ok)
        for m in range(M):
            k = did(act, act.activation(sq, bank[m][:, :], ACT.Square))
            need(dve, k)
            k = did(dve, dve.tensor_reduce(hsum[:, m, :], sq.rearrange("p (h d) -> p h d", d=HD), X, ALU.add))
            need(act, k)
        need(dve, k)
        k = did(dve, dve.tensor_scalar(hsum, hsum, 1.0 / HD, EPS1, ALU.mult, ALU.add))
        need(act, k)
        k = did(act, act.activation(hrs, hsum, ACT.Sqrt))
        for m in range(M):
            for half in range(2):
                sl_ = did(act, act.activation(xT[:, 4 * half + m, :], ig[:, m, half * 512 + 256:half * 512 + 512], ACT.Silu))
        need(dve, k)
        k = did(dve, dve.reciprocal(hrs, hrs))
        need(dve, k, sl_)
        for m in range(M):
            for half in range(2):
                o3 = o_tok[:, m, half * 256:half * 256 + 256]
                o4 = o3.rearrange("p (h d) -> p h d", d=HD)
                k = did(dve, dve.tensor_tensor(o4, bank[m][:, half * 256:half * 256 + 256].rearrange("p (h d) -> p h d", d=HD),
                                               bc(hrs[:, m, 4 * half:4 * half + 4], 2, HD), ALU.mult))
                need(dve, k)
                k = did(dve, dve.tensor_tensor(o3, o3, gain_bc[:, half, :], ALU.mult))
                need(dve, k)
                k = did(dve, dve.tensor_tensor(o3, o3, xT[:, 4 * half + m, :], ALU.mult))
        need(pe, k)
        for j, dst in enumerate((0, 1, 6, 7)):
            b = 4 + j
            for m in range(M):
                i = pe.transpose(bank[b][:, m * P:(m + 1) * P], o_tok[:, m, j * P:(j + 1) * P], ident[:, :])
            t = did(pe, i)
            need(act, t)
            k = did(act, act.activation(catT[:, dst, :], bank[b][:, 0:S], ACT.Copy))
        summed = out_product(A["w_out"][0], [k, rg_ok])

        need(pool, rg_ok)
        g_in = c_lng.tick(pool.dma_start(gb[:, 0, :], all_partitions(A["norm_final"], D)), 16)
        hT_ok = norm(summed, 1.0, EPS1, False, lambda k: col("norm_ffn", k), None)
        Wg, Wv, Wd = A["ffn_w_gate"][0], A["ffn_w_val"][0], A["ffn_w_down"][0]
        summed = ffn(lambda j: Wg[:, bass.ds(j * P, P)], lambda j: Wv[:, bass.ds(j * P, P)], lambda j: Wd[bass.ds(j * P, P), :],
                     FT1, GELU_RING, hT_ok, True)
        norm(summed, 1.0, EPS1, False, lambda k: col("norm_final", k), None, token_gain=g_in)

        c2 = Carve()
        win_bias, dif_bias = c2(M, 4, S), c2(M, 4, S)
        rope = c2(M, 6 * 16)
        qT, kT = c2(4, S), c2(4, S)
        qT2, kT2 = c2(4, S), c2(4, S)
        wuq, wukv = actT[:, :, :], nonlin
        assert 3 * S >= 2 * 384 and 2 * S >= 512
        cn = c2(M, 384)
        cT = c2(3, S)
        pb = c2(2, 512)
        ptb = c2(2, 512)
        small = c2(16, 8)
        sq2 = c2(384)
        rt = c2(M, 2, 96)
        gains = c2(256 + 128 + 64 + 64 + 64 + 4 + 128 + 2)
        hq = c2(M, 16)
        SCALE_A, SCALE_B, SCALE_C, SCALE_D = HD ** -0.5, (NOPE + ROPE) ** -0.5, HD ** -0.5, 32 ** -0.5
        fresh_counters()
        sp.dma_start(win_bias, C["win_bias"]).then_inc(c_par.sem, 16)
        sp.dma_start(dif_bias, C["dif_bias"]).then_inc(c_par.sem, 16)
        sp.dma_start(rope, C["rope"].rearrange("p m a b -> p m (a b)")).then_inc(c_par.sem, 16)
        sp.wait_ge(c_par.sem, 48)

        with nc.Fori(0, LAYERS) as l:
            fresh_counters()
            layer(l)
        c_out.n = 0
        fresh_counters()
        for m in range(M):
            t = c_out.tick(sp.dma_start(out[0, m * P:(m + 1) * P, :], x[:, m, :]), 16)
        need(sp, t)

_INS = ["x", "norm_mix", "w_in", "hgrn_lower_bounds", "hgrn_norm", "rg_conv_w", "rg_conv_b", "rg_w_a", "rg_b_a", "rg_w_x",
        "rg_b_x", "rg_lambda", "gla_w_gate_up", "gla_b_gate", "gla_norm", "w_out", "norm_ffn", "ffn_w_gate", "ffn_w_val",
        "ffn_conv_w", "ffn_conv_b", "ffn_w_down", "norm_final", "w_in_2", "win_sink_2", "mla_q_norm_2", "mla_w_uq_2",
        "mla_kv_norm_2", "mla_w_ukv_2", "ax_q_norm_2", "ax_k_norm_2", "diff_lambda_2", "diff_subln_2", "w_out_2",
        "ffn_w_gu_2", "ffn_w_down_2", "ln_g_2", "ln_b_2"]


def kernel(**inputs):
    import numpy as _np
    import concourse.bacc as _bacc
    from concourse.bass_utils import run_bass_kernel_spmd as _run

    nc = _bacc.Bacc("TRN2", target_bir_lowering=False, num_devices=1)
    arrays, aps, consts = {}, {}, {}
    for name in _INS:
        a = _np.ascontiguousarray(inputs[name])
        arrays[f"in_{name}"] = a
        aps[name] = nc.dram_tensor(f"in_{name}", a.shape, mybir.dt.from_np(a.dtype), kind="ExternalInput").ap()
    for name, a in constants().items():
        arrays[f"const_{name}"] = a
        consts[name] = nc.dram_tensor(f"const_{name}", a.shape, mybir.dt.from_np(a.dtype), kind="ExternalInput").ap()
    out = nc.dram_tensor("out", (1, S, D), F32, kind="ExternalOutput").ap()
    program(nc, aps, consts, out)
    r = _run(nc, [arrays], core_ids=[0])
    return r.results[0]["out"]
```

```python
from contextlib import ExitStack

import numpy as np
import concourse.bass as bass
from concourse import mybir
from concourse.alu_op_type import AluOpType as ALU

F32 = mybir.dt.float32
BF16 = mybir.dt.bfloat16
I32 = mybir.dt.int32
F32R = mybir.dt.float32r
ACT = mybir.ActivationFunctionType
X = mybir.AxisListType.X

P = 128
S = 256
M = S // P
D = 1024
KD = D // P
HALF = 512
HD = 64

A_Q, A_F, A_I, A_G, B_X, B_G, C_Q, C_K, C_V, C_G, C_LR = 0, 256, 512, 768, 1024, 1536, 2048, 2176, 2304, 2560, 2816
IN1 = 2832
LR_RANK = 16
DFF1 = 2688
FT1 = DFF1 // P
EPS1 = 1e-6
F_FLOOR = 1e-20
LEVELS = [1, 2, 4, 8, 16, 32, 64, 128]
CHUNK = 64
BANK_HEADS = [[(0, 0, 64, 0), (2, 0, 64, 1), (4, 0, 32, 2)],
              [(1, 64, 64, 0), (3, 64, 64, 1), (6, 64, 32, 2)],
              [(5, 32, 32, 2)],
              [(7, 96, 32, 2)]]
BANK_SLOT = [0, 3, 6, 7]

LAYERS = 2
IN2 = 2208
WIN_Q, WIN_K, WIN_V = 0, 256, 384
MLA_Q, MLA_KV, MLA_KR = 512, 768, 896
AX_Q, AX_V = 928, 1312
DF_Q, DF_K, DF_V = 1440, 1696, 1952
NOPE, ROPE = 64, 32
DFF2 = 2816
FT2 = DFF2 // P
EPS2 = 1e-5
ALPHA = float((2 * LAYERS) ** 0.25)
WCOLS = 256


def constants():
    t = {}
    t["ident"] = np.eye(P, dtype=np.float32)
    slopes = (2.0 ** (-8.0 * (np.arange(8, dtype=np.float32) + 1.0) / 8)).astype(np.float32)
    q = np.arange(S)[:, None]
    k = np.arange(S)[None, :]
    dist = np.abs(q - k).astype(np.float32)
    win = np.where(dist <= 128, -slopes[:4, None, None] * dist, np.float32(-1e30)).astype(np.float32)
    dif = (-slopes[4:, None, None] * dist).astype(np.float32)
    t["win_bias"] = np.ascontiguousarray(win.reshape(4, M, P, S).transpose(2, 1, 0, 3))
    t["dif_bias"] = np.ascontiguousarray(dif.reshape(4, M, P, S).transpose(2, 1, 0, 3))

    def angles(pos, dim):
        inv = (np.float32(10000.0) ** (-np.arange(0, dim, 2, dtype=np.float32) / np.float32(dim))).astype(np.float32)
        a = pos.astype(np.float32)[:, None] * inv[None, :]
        return np.cos(a).astype(np.float32), np.sin(a).astype(np.float32)

    pos = np.arange(S)
    cm, sm = angles(pos, ROPE)
    cr, sr = angles(pos // 64, 32)
    cc, sc = angles(pos % 64, 32)
    rope = np.stack([cm, sm, cr, cc, sr, sc], 1)
    t["rope"] = np.ascontiguousarray(rope.reshape(M, P, 6, 16).transpose(1, 0, 2, 3))
    j = np.arange(P)[:, None]
    i = np.arange(P)[None, :]
    masks = [((j // (2 * s) == i // (2 * s)) & (j % (2 * s) < s) & (i % (2 * s) >= s)) for s in LEVELS[:-1]]
    t["masks"] = np.ascontiguousarray(np.stack(masks, 1).astype(np.int32))
    keep = np.ones((P, 2, 3, S), np.float32)
    keep[:, 0, :, ::CHUNK] = 0
    keep[:, 1, :, ::S] = 0
    t["keep"] = keep
    li = [0.8 - 0.6 * np.exp(-0.3 * l) for l in range(LAYERS)]
    t["lam_init"] = np.array([[v, 1.0 - v] for v in li], np.float32)
    return t


CONSTS = {"ident": (P, P), "win_bias": (P, M, 4, S), "dif_bias": (P, M, 4, S), "rope": (P, M, 6, 16),
          "masks": (P, 7, P), "keep": (P, 2, 3, S), "lam_init": (LAYERS, 2)}


class Counter:

    def __init__(self, nc, ctx, name):
        self.sem, self.n = ctx.enter_context(nc.semaphore(name)), 0

    def tick(self, ins, by=1):
        ins.then_inc(self.sem, by)
        self.n += by
        return (self, self.n)


def program(nc, A, C, out):
    ctx = ExitStack()
    with ctx:
        def sb(name, shape, dt=F32):
            return ctx.enter_context(nc.sbuf_tensor(name, shape, dt))

        pe, act, dve, pool, sp = nc.tensor, nc.scalar, nc.vector, nc.gpsimd, nc.sync
        bank = [ctx.enter_context(nc.psum_tensor(f"bank{i}", [P, HALF], F32)) for i in range(8)]
        counters = []

        def counter(name):
            counters.append(Counter(nc, ctx, name))
            return counters[-1]

        c_pe, c_act, c_dve, c_pool = (counter(n) for n in ("pe_steps", "act_steps", "dve_steps", "pool_steps"))
        c_gu = [counter(f"gate_up_loaded{i}") for i in range(2)]
        c_dn = [counter(f"down_loaded{i}") for i in range(2)]
        c_gu_hi = [counter(f"gate_up_hi{i}") for i in range(2)]
        c_dn_hi = [counter(f"down_hi{i}") for i in range(2)]
        c_gu_lo = [counter(f"gate_up_split{i}") for i in range(2)]
        c_dn_lo = [counter(f"down_split{i}") for i in range(2)]
        c_gate, c_up, c_down, c_conv, c_gelu, c_prod, c_ahi, c_alo = (counter(n) for n in (
            "gate_done", "up_done", "down_done", "conv_done", "nonlin_done", "product_done", "product_hi", "product_split"))
        c_par = counter("parameters_loaded")
        c_gain = counter("gains_loaded")
        c_gain2, c_row2, c_ln2 = counter("layer_gains_loaded"), counter("layer_rows_loaded"), counter("layer_ln_loaded")
        c_ident = counter("identity_loaded")
        c_uq = counter("mla_weights_loaded")
        c_row = counter("rows_loaded")
        c_lng = counter("ln_rows_loaded")
        c_out = counter("output_stored")

        def need(eng, *marks):
            best = {}
            for c, v in marks:
                best[id(c)] = (c, max(v, best.get(id(c), (c, 0))[1]))
            for c, v in best.values():
                if v > 0:
                    eng.wait_ge(c.sem, v)

        def did(eng, ins):
            return {id(pe): c_pe, id(act): c_act, id(dve): c_dve, id(pool): c_pool}[id(eng)].tick(ins)

        def fresh_counters():
            nc.all_engine_barrier()
            for c in counters:
                if c not in (c_gain, c_row, c_lng):
                    sp.sem_clear(c.sem)
                    c.n = 0
            nc.all_engine_barrier()
            ring_state.update(next=0, staged_free=[[], []], split_free=[[], []], dn_staged_free=[[], []], dn_split_free=[[], []])

        st_gu = [sb(f"st_gu{i}", [P, KD * WCOLS]) for i in range(2)]
        hi_gu = [sb(f"hi_gu{i}", [P, KD * WCOLS], F32R) for i in range(2)]
        lo_gu = [sb(f"lo_gu{i}", [P, KD * WCOLS], F32R) for i in range(2)]
        st_dn = [sb(f"st_dn{i}", [P, D]) for i in range(2)]
        hi_dn = [sb(f"hi_dn{i}", [P, D], F32R) for i in range(2)]
        lo_dn = [sb(f"lo_dn{i}", [P, D], F32R) for i in range(2)]
        x = sb("x", [P, M, D])
        n = sb("n", [P, M, D])
        xTh = sb("xTh", [P, KD, S], F32R)
        xTl = sb("xTl", [P, KD, S], F32R)
        proj = sb("proj", [P, M, IN2])
        act32 = sb("act32", [P, 2, S])
        actTh = sb("actTh", [P, 2, S], F32R)
        actTl = sb("actTl", [P, 2, S], F32R)
        nonlin = sb("nonlin", [P, 2, S])
        conv = sb("conv", [P, 2, S])
        ident = sb("ident", [P, P])
        zeros = sb("zeros", [P, HALF], BF16)
        rows = sb("rows", [P, P])
        rows2 = sb("rows2", [P, P])
        par1 = sb("par1", [P, 60])
        parc = sb("parc", [P, 4, FT1])
        lnT = sb("lnT", [P, 6, KD])
        gb = sb("gb", [P, 2, D])
        stats = sb("stats", [P, M, 2, 6])
        mv = sb("mv", [P, M, 2])
        ms = sb("ms", [P, M])
        sd = sb("sd", [P, M])
        rs = sb("rs", [P, M])
        nmr = sb("nmr", [P, M])
        gbo = sb("gbo", [P, M, D])
        big = sb("big", [P, 12900])

        class Carve:
            def __init__(self):
                self.at = 0

            def __call__(self, *shape):
                size = int(np.prod(shape))
                v = big[:, self.at:self.at + size]
                self.at += size
                assert self.at <= 12900, self.at
                if len(shape) == 2:
                    v = v.rearrange("p (a b) -> p a b", a=shape[0])
                if len(shape) == 3:
                    v = v.rearrange("p (a b c) -> p a b c", a=shape[0], b=shape[1])
                if len(shape) == 4:
                    v = v.rearrange("p (a b c d) -> p a b c d", a=shape[0], b=shape[1], c=shape[2])
                return v

        def bc(ap, axis, count):
            shape = list(ap.shape)
            shape.insert(axis, count)
            return ap.unsqueeze(axis).to_broadcast(shape)

        def all_partitions(ap1d, width):
            return ap1d.rearrange("(a n) -> a n", a=1).to_broadcast([P, width])

        ring_state = {"next": 0, "staged_free": [[], []], "split_free": [[], []], "dn_staged_free": [[], []], "dn_split_free": [[], []]}

        def mm3(o, lhs, rhs, start, stop, **kw):
            pe.matmul(o, lhs[0], rhs[0], start=start, stop=False, **kw)
            pe.matmul(o, lhs[0], rhs[1], start=False, stop=False, **kw)
            return pe.matmul(o, lhs[1], rhs[0], start=False, stop=stop, **kw)

        def prepare(dram, width=WCOLS):
            i = ring_state["next"]
            ring_state["next"] = 1 - i
            need(sp, *ring_state["staged_free"][i])
            v = st_gu[i][:, :].rearrange("p (k n) -> p k n", k=KD)
            ld = c_gu[i].tick(sp.dma_start(v[:, :, 0:width], dram.rearrange("(k p) n -> p k n", p=P)), 16)
            hv = hi_gu[i][:, :].rearrange("p (k n) -> p k n", k=KD)
            lv = lo_gu[i][:, :].rearrange("p (k n) -> p k n", k=KD)
            need(act, ld, *ring_state["split_free"][i])
            h = c_gu_hi[i].tick(act.activation(hv[:, :, 0:width], v[:, :, 0:width], ACT.Copy))
            need(dve, h)
            lo = c_gu_lo[i].tick(dve.tensor_tensor(lv[:, :, 0:width], v[:, :, 0:width], hv[:, :, 0:width].bitcast(F32), ALU.subtract))
            ring_state["staged_free"][i] = [lo]
            return i, lo, width, hv, lv

        def transpose_tiles(src, gain, bias, src_done, extra=()):
            done = []
            freed = [list(extra), list(extra)]
            tmp_free = [(), ()]
            for k in range(KD):
                b = 6 + k % 2
                need(pe, *freed[k % 2], *(src_done if len(src_done) < 4 else src_done[2 * (k // 4):2 * (k // 4) + 2]))
                for m in range(M):
                    t = pe.transpose(bank[b][:, m * P:(m + 1) * P], src[:, m, k * P:(k + 1) * P], ident[:, :])
                t = did(pe, t)
                ps, hi, lo = bank[b][:, 0:S], xTh[:, k, :], xTl[:, k, :]
                if bias:
                    full = act32[:, k % 2, :]
                    e = (dve, act)[k % 2]
                    need(e, t, *tmp_free[k % 2])
                    if e is dve:
                        f = did(dve, dve.tensor_scalar(full, ps, gain(k), bias(k), ALU.mult, ALU.add))
                    else:
                        f = did(act, act.activation(full, ps, ACT.Identity, scale=gain(k), bias=bias(k)))
                    freed[k % 2] = [f]
                    need(act, f)
                    h = did(act, act.activation(hi, full, ACT.Copy))
                    need(dve, h, f)
                    d = did(dve, dve.tensor_tensor(lo, full, hi.bitcast(F32), ALU.subtract))
                    tmp_free[k % 2] = (d,)
                else:
                    need(act, t)
                    h = did(act, act.activation(hi, ps, ACT.Copy, scale=gain(k)) if gain else act.activation(hi, ps, ACT.Copy))
                    need(dve, h)
                    if gain:
                        d = dve.scalar_tensor_tensor(out=lo, in0=ps, scalar=gain(k), in1=hi.bitcast(F32), op0=ALU.mult, op1=ALU.subtract)
                    else:
                        d = dve.tensor_tensor(lo, ps, hi.bitcast(F32), ALU.subtract)
                    d = did(dve, d)
                    freed[k % 2] = [d]
                done.append(d)
            return [done[-1], h]

        def norm(added, alpha, eps, centred, gain, bias, token_gain=None):
            act.preload_act_table(ACT.Sqrt)
            if added:
                need(dve, *added)
            yd = []
            for m in range(M):
                if added:
                    for h in range(2):
                        xs = x[:, m, h * HALF:(h + 1) * HALF]
                        yd.append(did(dve, dve.scalar_tensor_tensor(out=xs, in0=xs, scalar=alpha, in1=bank[2 * m + h][:, :],
                                                                    op0=ALU.mult, op1=ALU.add)))
                for h in range(2):
                    need(dve, *yd[2 * m + h:2 * m + h + 1])
                    k = did(dve, dve.bn_stats(stats[:, m, h, :], x[:, m, h * HALF:(h + 1) * HALF]))
            for m in range(M):
                need(dve, k)
                did(dve, dve.bn_aggr(mv[:, m, :], stats[:, m, :, :].rearrange("p a b -> p (a b)")))
            k = (c_dve, c_dve.n)
            need(dve, k)
            if centred:
                k = did(dve, dve.tensor_scalar(ms[:, :], mv[:, :, 1], eps, None, ALU.add))
            else:
                k = did(dve, dve.tensor_tensor(ms[:, :], mv[:, :, 0], mv[:, :, 0], ALU.mult))
                need(dve, k)
                k = did(dve, dve.scalar_tensor_tensor(out=ms[:, :], in0=ms[:, :], scalar=eps, in1=mv[:, :, 1], op0=ALU.add, op1=ALU.add))
            need(act, k)
            k = did(act, act.activation(sd[:, :], ms[:, :], ACT.Sqrt))
            need(dve, k)
            k = did(dve, dve.reciprocal(rs[:, :], sd[:, :]))
            if centred:
                need(dve, k)
                k = did(dve, dve.scalar_tensor_tensor(out=nmr[:, :], in0=mv[:, :, 0], scalar=-1.0, in1=rs[:, :], op0=ALU.mult, op1=ALU.mult))
            need(act, k)
            need(dve, k)
            nd = []
            for q in range(2):
                qs_ = slice(q * HALF, (q + 1) * HALF)
                for m, e in enumerate((act, dve)):
                    if e is dve:
                        if centred:
                            i = dve.tensor_scalar(n[:, m, qs_], x[:, m, qs_], rs[:, m:m + 1], nmr[:, m:m + 1], ALU.mult, ALU.add)
                        else:
                            i = dve.tensor_scalar(n[:, m, qs_], x[:, m, qs_], rs[:, m:m + 1], None, ALU.mult)
                    elif centred:
                        i = act.activation(n[:, m, qs_], x[:, m, qs_], ACT.Identity, scale=rs[:, m:m + 1], bias=nmr[:, m:m + 1])
                    else:
                        i = act.activation(n[:, m, qs_], x[:, m, qs_], ACT.Copy, scale=rs[:, m:m + 1])
                    nd.append(did(e, i))
            done = transpose_tiles(n, gain, bias, nd)
            if token_gain:
                need(pool, token_gain, *nd, *done)
                for m in range(M):
                    k = did(pool, pool.tensor_tensor(x[:, m, :], n[:, m, :], gb[:, 0, :], ALU.mult))
                    if bias:
                        need(pool, k)
                        k = did(pool, pool.tensor_tensor(x[:, m, :], x[:, m, :], gb[:, 1, :], ALU.add))
                done = [*done, k]
            return done

        def token_chunk(prepared, out_of, ready):
            slot, split, width, hv, lv = prepared
            need(pe, split, *ready)
            for m in range(M):
                ms_ = slice(m * P, (m + 1) * P)
                for k in range(KD):
                    i = mm3(out_of(m), (xTh[:, k, ms_], xTl[:, k, ms_]), (hv[:, k, 0:width], lv[:, k, 0:width]), k == 0, k == KD - 1)
            t = did(pe, i)
            ring_state["split_free"][slot] = [t]
            return t

        def out_product(w_dram, ahead, ready):
            chunks = list(ahead)
            for c in range(D // WCOLS):
                t = token_chunk(chunks[c], lambda m: bank[2 * m + c // 2][:, (c % 2) * WCOLS:(c % 2 + 1) * WCOLS], ready)
                if c + 2 < D // WCOLS:
                    chunks.append(prepare(w_dram[:, (c + 2) * WCOLS:(c + 3) * WCOLS]))
            return [t]

        def gu_view(buf, i):
            return buf[i][:, :].rearrange("p (w k n) -> p w k n", w=2, k=KD)

        def ffn_ahead(gate_w, up_w, down_w):
            ring_state["next"] = 0
            for t in range(2):
                need(sp, *ring_state["staged_free"][t])
                for w, dram in ((0, gate_w), (1, up_w)):
                    c_gu[t].tick(sp.dma_start(gu_view(st_gu, t)[:, w], dram(t).rearrange("(k p) n -> p k n", p=P)), 16)
                need(sp, *ring_state["dn_staged_free"][t])
                c_dn[t].tick(sp.dma_start(st_dn[t][:, :], down_w(t)), 16)
            for t in range(2):
                for loaded, hi_c, lo_c, staged, hi, lo, free in ((c_gu, c_gu_hi, c_gu_lo, st_gu, hi_gu, lo_gu, "split_free"),
                                                                 (c_dn, c_dn_hi, c_dn_lo, st_dn, hi_dn, lo_dn, "dn_split_free")):
                    need(act, (loaded[t], loaded[t].n), *ring_state[free][t])
                    h = hi_c[t].tick(act.activation(hi[t][:, :], staged[t][:, :], ACT.Copy))
                    need(dve, h)
                    lo_c[t].tick(dve.tensor_tensor(lo[t][:, :], staged[t][:, :], hi[t][:, :].bitcast(F32), ALU.subtract))

        def ffn(gate_w, up_w, down_w, tiles, ready, convolved):
            base = {id(c): c.n for c in counters}
            turns = -(-tiles // 2)

            def at(c, count):
                return base[id(c)] + count

            need(pe, *ready)
            for b in range(4):
                pe.matmul(bank[b][:, :], zeros[:, 0:P], zeros[:, :], start=True, stop=False, skip_group_check=True)
            need(dve, *ready)
            need(act, *ready)

            def split_next(it, t, which):
                if which == "gu":
                    act.wait_ge(c_gu[t].sem, at(c_gu[t], it * 32 + 32))
                    act.wait_ge(c_up.sem, at(c_up, it * 2 + t + 1))
                    act.activation(hi_gu[t][:, :], st_gu[t][:, :], ACT.Copy).then_inc(c_gu_hi[t].sem, 1)
                    dve.wait_ge(c_gu_hi[t].sem, at(c_gu_hi[t], it + 1))
                    dve.tensor_tensor(lo_gu[t][:, :], st_gu[t][:, :], hi_gu[t][:, :].bitcast(F32), ALU.subtract).then_inc(c_gu_lo[t].sem, 1)
                else:
                    act.wait_ge(c_dn[t].sem, at(c_dn[t], it * 16 + 16))
                    act.wait_ge(c_down.sem, at(c_down, it * 2 + t + 1))
                    act.activation(hi_dn[t][:, :], st_dn[t][:, :], ACT.Copy).then_inc(c_dn_hi[t].sem, 1)
                    dve.wait_ge(c_dn_hi[t].sem, at(c_dn_hi[t], it + 1))
                    dve.tensor_tensor(lo_dn[t][:, :], st_dn[t][:, :], hi_dn[t][:, :].bitcast(F32), ALU.subtract).then_inc(c_dn_lo[t].sem, 1)

            def turn(it, here, ahead):
                for t in range(ahead):
                    sp.wait_ge(c_gu_lo[t].sem, at(c_gu_lo[t], it))
                    for w, dram in ((0, gate_w), (1, up_w)):
                        sp.dma_start(gu_view(st_gu, t)[:, w], dram(it * 2 + (2 + t)).rearrange("(k p) n -> p k n", p=P)).then_inc(c_gu[t].sem, 16)
                for t in range(ahead):
                    sp.wait_ge(c_dn_lo[t].sem, at(c_dn_lo[t], it))
                    sp.dma_start(st_dn[t][:, :], down_w(it * 2 + (2 + t))).then_inc(c_dn[t].sem, 16)
                for t in range(here):
                    g, u = bank[4 + t], bank[6 + t]
                    hv, lv = gu_view(hi_gu, t), gu_view(lo_gu, t)
                    pe.wait_ge(c_gu_lo[t].sem, at(c_gu_lo[t], it))
                    for w, b, c in ((0, g, c_gate), (1, u, c_up)):
                        for k in range(KD):
                            i = mm3(b[:, 0:S], (hv[:, w, k, :], lv[:, w, k, :]), (xTh[:, k, :], xTl[:, k, :]), k == 0, k == KD - 1)
                        i.then_inc(c.sem, 1)
                    act.wait_ge(c_gate.sem, at(c_gate, it * 2 + t + 1))
                    if convolved:
                        tap_at = (lambda tap: parc[:, tap, bass.ds(it * 2 + t, 1)])
                        act.activation(conv[:, t, :], g[:, 0:S], ACT.Identity, scale=tap_at(2), bias=tap_at(3)).then_inc(c_conv.sem, 1)
                        for tap in (1, 0):
                            lag = 2 - tap
                            cs = conv[:, t, lag:S]
                            dve.wait_ge(c_conv.sem, at(c_conv, (it * 2 + t) * 3 + lag))
                            dve.scalar_tensor_tensor(out=cs, in0=g[:, 0:S - lag], scalar=tap_at(tap), in1=cs,
                                                     op0=ALU.mult, op1=ALU.add).then_inc(c_conv.sem, 1)
                        act.wait_ge(c_conv.sem, at(c_conv, (it * 2 + t) * 3 + 3))
                        act.activation(nonlin[:, t, :], conv[:, t, :], ACT.Gelu_apprx_tanh).then_inc(c_gelu.sem, 1)
                    else:
                        act.activation(nonlin[:, t, :], g[:, 0:S], ACT.Silu).then_inc(c_gelu.sem, 1)
                    dve.wait_ge(c_gelu.sem, at(c_gelu, it * 2 + t + 1))
                    dve.wait_ge(c_up.sem, at(c_up, it * 2 + t + 1))
                    dve.scalar_tensor_tensor(out=act32[:, t, :], in0=nonlin[:, t, :], scalar=1.0 if convolved else 0.5,
                                             in1=u[:, 0:S], op0=ALU.mult, op1=ALU.mult).then_inc(c_prod.sem, 1)
                    act.wait_ge(c_prod.sem, at(c_prod, it * 2 + t + 1))
                    act.activation(actTh[:, t, :], act32[:, t, :], ACT.Copy).then_inc(c_ahi.sem, 1)
                    dve.wait_ge(c_ahi.sem, at(c_ahi, it * 2 + t + 1))
                    dve.tensor_tensor(actTl[:, t, :], act32[:, t, :], actTh[:, t, :].bitcast(F32), ALU.subtract).then_inc(c_alo.sem, 1)
                    if t < ahead:
                        split_next(it, t, "gu")
                for t in range(here):
                    pe.wait_ge(c_alo.sem, at(c_alo, it * 2 + t + 1))
                    pe.wait_ge(c_dn_lo[t].sem, at(c_dn_lo[t], it))
                    for m in range(M):
                        for h in range(2):
                            hs = slice(h * HALF, (h + 1) * HALF)
                            ts = slice(m * P, (m + 1) * P)
                            i = mm3(bank[2 * m + h][:, :], (actTh[:, t, ts], actTl[:, t, ts]), (hi_dn[t][:, hs], lo_dn[t][:, hs]),
                                    False, False, skip_group_check=True)
                    i.then_inc(c_down.sem, 1)
                for t in range(ahead):
                    split_next(it, t, "dn")

            act.preload_act_table(ACT.Gelu_apprx_tanh if convolved else ACT.Silu)
            with nc.Fori(0, tiles // 2 - 1) as it:
                turn(it, 2, 2)
            turn(tiles // 2 - 1, 2, tiles % 2)
            if tiles % 2:
                turn(tiles // 2, 1, 0)
            for t in range(2):
                uses = (tiles + 1 - t) // 2 - 1
                for cs, per in ((c_gu, 32), (c_dn, 16), (c_gu_hi, 1), (c_dn_hi, 1), (c_gu_lo, 1), (c_dn_lo, 1)):
                    cs[t].n += per * uses
            for c, per in ((c_gate, 1), (c_up, 1), (c_down, 1), (c_gelu, 1), (c_prod, 1), (c_ahi, 1), (c_alo, 1), (c_conv, 3 if convolved else 0)):
                c.n += per * tiles
            for b in range(4):
                i = pe.matmul(bank[b][:, :], zeros[:, 0:P], zeros[:, :], start=False, stop=True, skip_group_check=True)
            t = did(pe, i)
            ring_state.update(next=0, staged_free=[[(c_gu_lo[i], c_gu_lo[i].n)] for i in range(2)], split_free=[[t], [t]],
                              dn_staged_free=[[(c_dn_lo[i], c_dn_lo[i].n)] for i in range(2)], dn_split_free=[[t], [t]])
            return [t]

        def layer(l):
            at = 0
            gv = {}
            for name, width in (("mla_q_norm_2", 256), ("mla_kv_norm_2", 128), ("ax_q_norm_2", 64), ("ax_k_norm_2", 64),
                                ("diff_subln_2", 64), ("win_sink_2", 4)):
                gv[name] = gains[:, at:at + width]
                c_gain2.tick(act.dma_start(gv[name], all_partitions(A[name][l], width)), 16)
                at += width
            gv["lam"] = gains[:, at:at + 128]
            c_gain2.tick(act.dma_start(gv["lam"], all_partitions(A["diff_lambda_2"][l].rearrange("a b -> (a b)"), 128)), 16)
            at += 128
            gv["init"] = gains[:, at:at + 2]
            gains_in = c_gain2.tick(act.dma_start(gv["init"], all_partitions(C["lam_init"][l], 2)), 16)
            c_row2.tick(act.dma_start(rows[0:24, :], A["ln_g_2"][l].rearrange("a (k p) -> (a k) p", p=P)), 16)
            rows_in = c_row2.tick(act.dma_start(rows[24:48, :], A["ln_b_2"][l].rearrange("a (k p) -> (a k) p", p=P)), 16)
            need(pe, rows_in)
            t = did(pe, pe.transpose(bank[4][:, 0:48], rows[0:48, :], ident[0:48, 0:48]))
            need(dve, t)
            ln_ok = did(dve, dve.tensor_copy(lnT[:, :, :].rearrange("p a b -> p (a b)"), bank[4][:, 0:48]))
            need(act, ln_ok)

            def ln_rows(i, free):
                need(sp, *free)
                c_ln2.tick(sp.dma_start(gb[:, 0, :], all_partitions(A["ln_g_2"][l, i], D)), 16)
                return c_ln2.tick(sp.dma_start(gb[:, 1, :], all_partitions(A["ln_b_2"][l, i], D)), 16)

            def swiglu_weights(i):
                wgu, wd = A["ffn_w_gu_2"][l, i], A["ffn_w_down_2"][l, i]
                return (lambda j: wgu[:, bass.ds(j * P, P)], lambda j: wgu[:, bass.ds(j * P + DFF2, P)],
                        lambda j: wd[bass.ds(j * P, P), :])

            gb_in = ln_rows(0, ())
            ffn_ahead(*swiglu_weights(0))
            summed = ffn(*swiglu_weights(0), FT2, [ln_ok], False)
            W2 = A["w_in_2"][l]
            starts = list(range(0, IN2, WCOLS))

            def w_in_chunk(c):
                return prepare(W2[:, starts[c]:min(starts[c] + WCOLS, IN2)], min(WCOLS, IN2 - starts[c]))

            prepared = [w_in_chunk(0), w_in_chunk(1)]
            done = norm(summed, ALPHA, EPS2, True, lambda k: lnT[:, 0, k:k + 1], lambda k: lnT[:, 3, k:k + 1], token_gain=gb_in)
            pool_done = done[-1:]

            freed = [list(done), list(done)]
            chunk_ok = []
            for ci, c0 in enumerate(starts):
                width = min(WCOLS, IN2 - c0)
                b0 = 2 * (ci % 2)
                t = token_chunk(prepared[ci], lambda m: bank[b0 + m][:, 0:width], freed[ci % 2])
                need(dve, t)
                need(act, t)
                k1 = did(dve, dve.tensor_copy(proj[:, 0, c0:c0 + width], bank[b0][:, 0:width]))
                k2_ = did(act, act.activation(proj[:, 1, c0:c0 + width], bank[b0 + 1][:, 0:width], ACT.Copy))
                freed[ci % 2] = [k1, k2_]
                chunk_ok += [k1, k2_]
                if ci + 2 < len(starts):
                    prepared.append(w_in_chunk(ci + 2))
            W2o = A["w_out_2"][l]
            out_ahead = [prepare(W2o[:, c * WCOLS:(c + 1) * WCOLS]) for c in range(2)]
            wuq3 = st_dn[0][:, 0:768].rearrange("p (k n) -> p k n", k=2)
            wukv2 = st_dn[1][:, 0:HALF]
            need(sp, *ring_state["dn_staged_free"][0], *ring_state["dn_staged_free"][1])
            uq_in = c_uq.tick(sp.dma_start(wuq3, A["mla_w_uq_2"][l].rearrange("(k p) n -> p k n", p=P)), 16)
            ukv_in = c_uq.tick(sp.dma_start(wukv2, A["mla_w_ukv_2"][l]), 16)
            gb_in = ln_rows(1, pool_done)

            need(dve, gains_in)
            lp = gv["lam"].rearrange("p (a b) -> p a b", a=4)
            lsum, lexp, lam = small[:, 0, 0:2], small[:, 1, 0:2], small[:, 2, 0:1]
            k = did(dve, dve.tensor_tensor(sq2[:, 0:64].rearrange("p (a b) -> p a b", a=2), lp[:, 0:4:2, :], lp[:, 1:4:2, :], ALU.mult))
            need(dve, k)
            k = did(dve, dve.tensor_reduce(lsum, sq2[:, 0:64].rearrange("p (a b) -> p a b", a=2), X, ALU.add))
            need(act, k)
            k = did(act, act.activation(lexp, lsum, ACT.Exp))
            need(dve, k)
            k = did(dve, dve.tensor_tensor(lam, lexp[:, 0:1], lexp[:, 1:2], ALU.subtract))
            need(dve, k)
            lam_ok = did(dve, dve.tensor_tensor(lam, lam, gv["init"][:, 0:1], ALU.add))
            nsink = small[:, 3, 0:4]
            sink_ok = did(dve, dve.tensor_scalar(nsink, gv["win_sink_2"], -1.0, None, ALU.mult))

            mq = n[:, :, 0:384].rearrange("p m (h d) -> p m h d", d=96)
            mkk = n[:, :, 384:768].rearrange("p m (h d) -> p m h d", d=96)
            mv_ = n[:, :, 768:1024].rearrange("p m (h d) -> p m h d", d=HD)
            hr = hq[:, :, 8:16]
            mark = {}
            tr_free = {6: tuple(done), 7: tuple(done)}

            def sums_of_squares():
                need(act, *chunk_ok, gains_in)
                for m in range(M):
                    did(act, act.activation(cn[m][:, 0:256], proj[:, m, MLA_Q:MLA_Q + 256], ACT.Square, accum_out=hq[:, m, 0:1]))
                    k = did(act, act.activation(cn[m][:, 256:384], proj[:, m, MLA_KV:MLA_KV + 128], ACT.Square, accum_out=hq[:, m, 1:2]))
                mark["sq"] = k
                for m in range(M):
                    need(dve, (c_dve, c_dve.n))
                    k = did(dve, dve.tensor_tensor(sq2, proj[:, m, AX_Q:AX_Q + 384], proj[:, m, AX_Q:AX_Q + 384], ALU.mult))
                    need(dve, k)
                    k = did(dve, dve.tensor_reduce(hq[:, m, 2:8], sq2.rearrange("p (h d) -> p h d", d=HD), X, ALU.add))

            def rstd():
                need(dve, mark["sq"], (c_dve, c_dve.n))
                did(dve, dve.tensor_scalar(hr[:, :, 0:1], hq[:, :, 0:1], 1.0 / 256, EPS2, ALU.mult, ALU.add))
                did(dve, dve.tensor_scalar(hr[:, :, 1:2], hq[:, :, 1:2], 1.0 / 128, EPS2, ALU.mult, ALU.add))
                k = did(dve, dve.tensor_scalar(hr[:, :, 2:8], hq[:, :, 2:8], 1.0 / HD, EPS2, ALU.mult, ALU.add))
                need(act, k)
                mark["sd"] = did(act, act.activation(hr, hr, ACT.Sqrt))

            def latents():
                need(dve, mark["sd"])
                k = did(dve, dve.reciprocal(hr, hr))
                need(dve, k)
                for m in range(M):
                    did(dve, dve.scalar_tensor_tensor(out=cn[m][:, 0:256], in0=proj[:, m, MLA_Q:MLA_Q + 256], scalar=hr[:, m, 0:1],
                                                      in1=gv["mla_q_norm_2"], op0=ALU.mult, op1=ALU.mult))
                    mark["cn"] = did(dve, dve.scalar_tensor_tensor(out=cn[m][:, 256:384], in0=proj[:, m, MLA_KV:MLA_KV + 128],
                                                                   scalar=hr[:, m, 1:2], in1=gv["mla_kv_norm_2"], op0=ALU.mult, op1=ALU.mult))

            def axial_gains():
                need(pool, *chunk_ok, mark["cn"])
                for m in range(M):
                    axh = proj[:, m, AX_Q:AX_Q + 384].rearrange("p (h d) -> p h d", d=HD)
                    k = did(pool, pool.tensor_tensor(axh, axh, bc(hr[:, m, 2:8], 2, HD), ALU.mult))
                    need(pool, k)
                    did(pool, pool.tensor_tensor(axh[:, 0:4], axh[:, 0:4], bc(gv["ax_q_norm_2"], 1, 4), ALU.mult))
                    did(pool, pool.tensor_tensor(axh[:, 4:6], axh[:, 4:6], bc(gv["ax_k_norm_2"], 1, 2), ALU.mult))

            def latents_T():
                for j in range(3):
                    b = 6 + j % 2
                    need(pe, mark["cn"], *tr_free[b])
                    for m in range(M):
                        i = pe.transpose(bank[b][:, m * P:(m + 1) * P], cn[m][:, j * P:(j + 1) * P], ident[:, :])
                    t = did(pe, i)
                    need(act, t)
                    mark["cT"] = did(act, act.activation(cT[:, j, :], bank[b][:, 0:S], ACT.Copy))
                    tr_free[b] = (mark["cT"],)

            def up_projections(m):
                need(pe, mark["cT"], uq_in, ukv_in, *tr_free[6], *tr_free[7])
                for k_ in range(2):
                    pe.matmul(bank[6][:, 0:384], cT[:, k_, m * P:(m + 1) * P], wuq3[:, k_, :], start=(k_ == 0), stop=(k_ == 1))
                t = did(pe, pe.matmul(bank[7][:, :], cT[:, 2, m * P:(m + 1) * P], wukv2, start=True, stop=True))
                ring_state["dn_staged_free"] = [[t], [t]]
                need(act, t, *done)
                k = did(act, act.activation(n[:, m, 0:384], bank[6][:, 0:384], ACT.Copy))
                tr_free[6] = (k,)
                kv4 = bank[7][:, :].rearrange("p (h d) -> p h d", d=128)
                did(act, act.activation(mkk[:, m, :, 0:NOPE], kv4[:, :, 0:NOPE], ACT.Copy))
                k = did(act, act.activation(mv_[:, m, :, :], kv4[:, :, NOPE:128], ACT.Copy))
                tr_free[7] = (k,)
                mark["up"] = k

            def rotate(m, a, b_, cosv, sinv, heads):
                t1, t2 = (rt[:, m, z, 0:16 * heads].rearrange("p (h d) -> p h d", d=16) for z in range(2))
                cv, sv = bc(cosv, 1, heads), bc(sinv, 1, heads)
                need(pool, (c_pool, c_pool.n))
                did(pool, pool.tensor_tensor(t1, a, sv, ALU.mult))
                k = did(pool, pool.tensor_tensor(t2, b_, sv, ALU.mult))
                need(pool, k)
                did(pool, pool.tensor_tensor(a, a, cv, ALU.mult))
                k = did(pool, pool.tensor_tensor(b_, b_, cv, ALU.mult))
                need(pool, k)
                did(pool, pool.tensor_tensor(a, a, t2, ALU.subtract))
                return did(pool, pool.tensor_tensor(b_, b_, t1, ALU.add))

            def rotations(m):
                rp = rope[:, m, :].rearrange("p (a b) -> p a b", a=6)
                axh = proj[:, m, AX_Q:AX_Q + 384].rearrange("p (h d) -> p h d", d=HD)
                for hf in range(2):
                    mark["ax"] = rotate(m, axh[:, :, 32 * hf:32 * hf + 16], axh[:, :, 32 * hf + 16:32 * hf + 32],
                                        rp[:, 2 + hf, :], rp[:, 4 + hf, :], 6)
                kr = proj[:, m, MLA_KR:MLA_KR + 32].rearrange("p (a b) -> p a b", a=2)
                k = rotate(m, kr[:, 0:1, :], kr[:, 1:2, :], rp[:, 0, :], rp[:, 1, :], 1)
                need(pool, k, mark["up"])
                did(pool, pool.tensor_copy(mkk[:, m, :, 64:96], bc(proj[:, m, MLA_KR:MLA_KR + 32], 1, 4)))
                mark["mla"] = rotate(m, mq[:, m, :, 64:80], mq[:, m, :, 80:96], rp[:, 0, :], rp[:, 1, :], 4)

            pieces = [sums_of_squares, rstd, latents, axial_gains, latents_T, lambda: up_projections(0), lambda: up_projections(1),
                      lambda: rotations(0), lambda: rotations(1)]

            sets = [(qT, kT), (qT2, kT2)]
            proj_h = {}

            def views(kind):
                if kind == "win":
                    return ([(lambda m, h=h: proj[:, m, WIN_Q + h * HD:WIN_Q + (h + 1) * HD]) for h in range(4)],
                            [(lambda m, h=h: proj[:, m, WIN_K + h * HD:WIN_K + (h + 1) * HD]) for h in range(2)], HD)
                if kind == "mla":
                    return ([(lambda m, h=h: mq[:, m, h, :]) for h in range(4)], [(lambda m, h=h: mkk[:, m, h, :]) for h in range(4)], 96)
                if kind == "ax":
                    return ([(lambda m, h=h: proj[:, m, AX_Q + h * HD:AX_Q + (h + 1) * HD]) for h in range(4)],
                            [(lambda m, h=h: proj[:, m, AX_Q + 256 + h * HD:AX_Q + 256 + (h + 1) * HD]) for h in range(2)], HD)
                return ([(lambda m, h=h: proj[:, m, DF_Q + h * HD:DF_Q + (h + 1) * HD]) for h in range(4)],
                        [(lambda m, h=h: proj[:, m, DF_K + h * HD:DF_K + (h + 1) * HD]) for h in range(4)], HD)

            kinds = ["win", "dif", "ax", "mla"]
            tr_n = [0]
            set_reads = [(), ()]

            def transposes(kind):
                si = kinds.index(kind) % 2
                q_, k_ = sets[si]
                qv, kv, dim = views(kind)
                need(pe, *(chunk_ok if kind in ("win", "dif") else [mark["ax"]] if kind == "ax" else [mark["mla"], mark["up"]]))
                for dst, vs in ((q_, qv), (k_, kv)):
                    for p0 in range(0, len(vs), 2):
                        b = 6 + tr_n[0] % 2
                        tr_n[0] += 1
                        need(pe, *tr_free[b])
                        for z in range(2):
                            for m in range(M):
                                i = pe.transpose(bank[b][0:dim, (2 * z + m) * P:(2 * z + m + 1) * P], vs[p0 + z](m), ident[:, :])
                        t = did(pe, i)
                        need(act, t, *set_reads[si])
                        e = did(act, act.activation(dst[0:dim, p0:p0 + 2, :], bank[b][0:dim, :].rearrange("p (a b) -> p a b", a=2), ACT.Copy))
                        tr_free[b] = (e,)
                ready_t[kind] = e

            ready_t = {}
            units = [(kind, m, pr) for kind in kinds for pr in range(4 if kind == "dif" else 2) for m in range(M)]
            out_col = {"win": 0, "mla": 256, "ax": 512, "dif": 768}
            cat = proj
            v_of = {"win": (proj, WIN_V), "mla": (n, 768), "ax": (proj, AX_V), "dif": (proj, DF_V)}
            om = [gbo[:, m, :] for m in range(M)]
            st = {}
            bank_s, bank_t, bank_o = {0: (), 1: ()}, {2: (), 3: ()}, {4: (), 5: ()}
            for d_ in (bank_s, bank_t, bank_o):
                for b in d_:
                    d_[b] = (*freed[0], *freed[1], ln_ok)
            pb_read, ptb_read = [(), ()], [(), ()]
            rr_done = {}

            def stage0(u):
                kind, m, pr = units[u]
                si = kinds.index(kind) % 2
                q_, k_ = sets[si]
                i2 = u % 2
                need(pe, ready_t[kind], *bank_s[i2])
                for z in range(2):
                    if kind == "dif":
                        r0, qh, kh, dim = 32 * z, pr, pr, 32
                    else:
                        r0, qh, dim = 0, 2 * pr + z, (96 if kind == "mla" else HD)
                        kh = qh if kind == "mla" else pr
                    i = pe.matmul(bank[i2][:, z * S:(z + 1) * S], q_[r0:r0 + dim, qh, m * P:(m + 1) * P], k_[r0:r0 + dim, kh, :],
                                  start=True, stop=True)
                    if kind == "dif" and z == 0:
                        need(pe, did(pe, i))
                t = did(pe, i)
                if u + 1 == len(units) or units[u + 1][0] != kind:
                    set_reads[si] = (t,)
                s3 = bank[i2][:, :].rearrange("p (a b) -> p a b", a=2)
                p3 = pb[:, i2, :].rearrange("p (a b) -> p a b", a=2)
                nm, sm, rr = small[:, 4 + i2, 0:2], small[:, 6 + i2, 0:2], small[:, 8 + i2, 0:2]
                scale = {"win": 1.0, "dif": 1.0, "ax": SCALE_C, "mla": SCALE_B}[kind]
                need(dve, t, *pb_read[i2])
                if kind in ("win", "dif"):
                    bias = win_bias[:, m, 2 * pr:2 * pr + 2, :] if kind == "win" else bc(dif_bias[:, m, pr, :], 1, 2)
                    k = did(dve, dve.scalar_tensor_tensor(out=p3, in0=s3, scalar=SCALE_A if kind == "win" else SCALE_D, in1=bias,
                                                          op0=ALU.mult, op1=ALU.add))
                    bank_s[i2] = (k,)
                    src = p3
                    need(dve, k)
                else:
                    src = s3
                k = did(dve, dve.tensor_reduce(nm, src, X, ALU.max, negate=True))
                need(dve, k)
                if kind == "win":
                    k = did(dve, dve.tensor_tensor(nm, nm, nsink[:, 2 * pr:2 * pr + 2], ALU.min))
                elif scale != 1.0:
                    k = did(dve, dve.tensor_scalar(nm, nm, scale, None, ALU.mult))
                need(act, k, *pb_read[i2])
                if kind == "win":
                    ex = small[:, 10 + i2, 0:2]
                    for z in range(2):
                        did(act, act.activation(ex[:, z:z + 1], nm[:, z:z + 1], ACT.Exp, bias=gv["win_sink_2"][:, 2 * pr + z:2 * pr + z + 1]))
                for z in range(2):
                    k = did(act, act.activation(p3[:, z, :], src[:, z, :], ACT.Exp, scale=scale, bias=nm[:, z:z + 1], accum_out=sm[:, z:z + 1]))
                if kind in ("ax", "mla"):
                    bank_s[i2] = (k,)
                st[u] = k

            def stage1(u):
                kind, m, pr = units[u]
                i2 = u % 2
                maps = 1 if kind == "dif" else 2
                b = 2 + i2
                p3 = pb[:, i2, :].rearrange("p (a b) -> p a b", a=2)
                sm, rr = small[:, 6 + i2, 0:2], small[:, 8 + i2, 0:2]
                k = st[u]
                need(dve, k, *bank_o[4 + i2])
                if kind == "win":
                    k2_ = did(dve, dve.tensor_tensor(sm, sm, small[:, 10 + i2, 0:2], ALU.add))
                    need(dve, k2_)
                k2_ = rr_done[i2] = did(dve, dve.reciprocal(rr, sm))
                if kind == "dif":
                    need(dve, k2_)
                    k = did(dve, dve.tensor_scalar(rr[:, 1:2], rr[:, 1:2], lam, None, ALU.mult))
                    need(dve, k)
                    k = did(dve, dve.tensor_scalar(p3[:, 1, :], p3[:, 1, :], rr[:, 1:2], None, ALU.mult))
                    need(dve, k)
                    k = did(dve, dve.scalar_tensor_tensor(out=p3[:, 0, :], in0=p3[:, 0, :], scalar=rr[:, 0:1], in1=p3[:, 1, :],
                                                          op0=ALU.mult, op1=ALU.subtract))
                need(pe, k, *bank_t[b])
                for z in range(maps):
                    for kt in range(M):
                        i = pe.transpose(bank[b][:, (2 * z + kt) * P:(2 * z + kt + 1) * P], pb[:, i2, z * S + kt * P:z * S + (kt + 1) * P], ident[:, :])
                t = did(pe, i)
                pb_read[i2] = (t,)
                need(act, t, *ptb_read[i2])
                w = 2 * maps * P
                k = did(act, act.activation(ptb[:, i2, 0:w], bank[b][:, 0:w], ACT.Copy))
                bank_t[b] = (k,)
                st[u] = k

            def stage2(u):
                kind, m, pr = units[u]
                i2 = u % 2
                maps = 1 if kind == "dif" else 2
                b = 4 + i2
                need(pe, st[u], *bank_o[b])
                vb, v0 = v_of[kind]
                for z in range(maps):
                    vh = {"win": pr, "ax": pr, "mla": 2 * pr + z, "dif": pr}[kind]
                    for kt in range(M):
                        i = pe.matmul(bank[b][:, z * HD:(z + 1) * HD], ptb[:, i2, (2 * z + kt) * P:(2 * z + kt + 1) * P],
                                      vb[:, kt, v0 + vh * HD:v0 + (vh + 1) * HD], start=(kt == 0), stop=(kt == 1))
                t = did(pe, i)
                ptb_read[i2] = (t,)
                need(dve, t)
                if kind == "dif":
                    o0 = out_col[kind] + pr * HD
                    k = did(dve, dve.tensor_copy(om[m][:, o0:o0 + HD], bank[b][:, 0:HD]))
                else:
                    o0 = out_col[kind] + 2 * pr * HD
                    rr = small[:, 8 + i2, 0:2]
                    need(dve, rr_done[i2])
                    k = did(dve, dve.tensor_tensor(om[m][:, o0:o0 + P].rearrange("p (a b) -> p a b", a=2),
                                                   bank[b][:, 0:P].rearrange("p (a b) -> p a b", a=2), bc(rr, 2, HD), ALU.mult))
                bank_o[b] = (k,)
                return k

            need(dve, lam_ok, sink_ok)
            need(act, sink_ok)
            transposes("win")
            for u in range(len(units) + 2):
                if u < len(units):
                    stage0(u)
                    if u + 3 < len(units) and units[u + 3][0] not in ready_t:
                        while pieces and units[u + 3][0] in ("ax", "mla"):
                            pieces.pop(0)()
                        transposes(units[u + 3][0])
                if 1 <= u <= len(units):
                    stage1(u - 1)
                if 2 <= u:
                    o_ok = stage2(u - 2)
                if pieces:
                    pieces.pop(0)()
            need(dve, o_ok)
            for m in range(M):
                d3 = om[m][:, 768:1024]
                need(dve, (c_dve, c_dve.n))
                k = did(dve, dve.tensor_tensor(sq2[:, 0:256], d3, d3, ALU.mult))
                need(dve, k)
                k = did(dve, dve.tensor_reduce(hq[:, m, 0:4], sq2[:, 0:256].rearrange("p (h d) -> p h d", d=HD), X, ALU.add))
            need(dve, k)
            k = did(dve, dve.tensor_scalar(hq[:, :, 0:4], hq[:, :, 0:4], 1.0 / HD, EPS2, ALU.mult, ALU.add))
            need(act, k)
            k = did(act, act.activation(hq[:, :, 0:4], hq[:, :, 0:4], ACT.Sqrt))
            need(dve, k)
            k = did(dve, dve.reciprocal(hq[:, :, 0:4], hq[:, :, 0:4]))
            need(dve, k)
            k = did(dve, dve.tensor_scalar(hq[:, :, 0:4], hq[:, :, 0:4], gv["init"][:, 1:2], None, ALU.mult))
            need(dve, k)
            for m in range(M):
                d3 = om[m][:, 768:1024].rearrange("p (h d) -> p h d", d=HD)
                k = did(dve, dve.tensor_tensor(d3, d3, bc(hq[:, m, 0:4], 2, HD), ALU.mult))
                need(dve, k)
                k = did(dve, dve.tensor_tensor(d3, d3, bc(gv["diff_subln_2"], 1, 4), ALU.mult))
            ct = transpose_tiles(gbo, None, None, [k], extra=(*tr_free[6], *tr_free[7]))
            summed = out_product(W2o, out_ahead, [*ct, *[z for d_ in (bank_s, bank_t) for v in d_.values() for z in v]])
            ffn_ahead(*swiglu_weights(1))
            done = norm(summed, ALPHA, EPS2, True, lambda k: lnT[:, 1, k:k + 1], lambda k: lnT[:, 4, k:k + 1], token_gain=gb_in)
            summed = ffn(*swiglu_weights(1), FT2, done, False)
            gb_in = ln_rows(2, done[-1:])
            norm(summed, ALPHA, EPS2, True, lambda k: lnT[:, 2, k:k + 1], lambda k: lnT[:, 5, k:k + 1], token_gain=gb_in)


        def scatter_rows(dst_rows, at, dram1d, count):
            c_row.tick(pool.dma_start(dst_rows[at:at + count, :], dram1d.rearrange("(a n) -> a n", n=P)), 16)

        ident_in = c_ident.tick(sp.dma_start(ident[:, :], C["ident"]), 16)
        k0 = did(pool, pool.memset(zeros[:, :], 0.0))
        c = Carve()
        o_tok = n
        ig = proj[:, :, 0:D]
        gq, gk, lf = c(3, S), c(3, S), c(3, S)
        cum = c(2, 3, S)
        dd, ee = c(3 * S), c(3 * S)
        sil = big[:, c.at:c.at + 4 * S].rearrange("p (a b) -> p a b", a=4)
        qs = c(2, 3, S)
        ks = c(2, 3, S)
        zf = ks[:, 0, 0:2, :]
        keep_at = c.at
        scoreT = [c(8, P) for _ in range(3)]
        keep = big[:, keep_at:keep_at + 2 * 3 * S].rearrange("p (a b c) -> p a b c", a=2, b=3)
        masks = c(7, P)
        gain_bc = proj[:, 0, 1552:2064].rearrange("p (a b) -> p a b", a=2)
        hsum, hrs = c(M, 8), c(M, 8)

        PARS = [("norm_mix", 8), ("norm_ffn", 8), ("norm_final", 8), ("rg_b_a", 4), ("rg_b_x", 4), ("rg_lambda", 4),
                ("rg_conv_w", 16), ("rg_conv_b", 4), ("gla_b_gate", 1), ("hgrn_lower_bounds", 2)]
        off, at = {}, 0
        for name, count in PARS:
            v = A[name]
            v = v if len(v.shape) == 1 else (v.rearrange("a n -> (a n)") if len(v.shape) == 2 else v.rearrange("a b n -> (a b n)"))
            scatter_rows(rows, at, v, count)
            off[name] = at
            at += count
        n_par = at
        scatter_rows(rows2, 0, A["ffn_conv_w"].rearrange("a b n -> (a b n)"), 3 * FT1)
        scatter_rows(rows2, 3 * FT1, A["ffn_conv_b"].rearrange("a n -> (a n)"), FT1)
        rows_in = (c_row, c_row.n)

        def load_x(m):
            return c_out.tick(sp.dma_start(x[:, m, :], A["x"][0, m * P:(m + 1) * P, :]), 16)

        x_in = [load_x(m) for m in range(M)]
        x_in = [x_in[-1]]
        par_in = []
        par_in.append(c_par.tick(sp.dma_start(masks, C["masks"].bitcast(F32)), 16))
        par_in.append(c_par.tick(sp.dma_start(keep, C["keep"]), 16))
        par_in.append(c_gain.tick(pool.dma_start(gain_bc[:, 0, :], all_partitions(A["hgrn_norm"][0], 256)), 16))
        par_in.append(c_gain.tick(pool.dma_start(gain_bc[:, 1, :], all_partitions(A["gla_norm"][0], 256)), 16))

        need(pe, ident_in, rows_in)
        pe.transpose(bank[0][:, 0:n_par], rows[0:n_par, :], ident[0:n_par, 0:n_par])
        t = did(pe, pe.transpose(bank[0][:, P:P + 4 * FT1], rows2[0:4 * FT1, :], ident[0:4 * FT1, 0:4 * FT1]))
        need(dve, t)
        did(dve, dve.tensor_copy(par1[:, 0:n_par], bank[0][:, 0:n_par]))
        par_ok = did(dve, dve.tensor_copy(parc[:, :, :].rearrange("p a b -> p (a b)"), bank[0][:, P:P + 4 * FT1]))

        def col(name, i=0, count=1):
            return par1[:, off[name] + i:off[name] + i + count]

        need(act, par_ok)
        need(pe, par_ok)
        need(dve, *x_in, k0, par_ok)
        need(act, *x_in)
        need(pe, k0)
        W = A["w_in"][0]
        prepared = [prepare(W[:, A_Q:A_Q + 256]), prepare(W[:, A_F:A_F + 256])]
        hT_ok = norm([], 1.0, EPS1, False, lambda k: col("norm_mix", k), None)

        spl = c(4)
        e1 = did(act, act.activation(spl, col("rg_lambda", 0, 4), ACT.Exp, scale=-1.0))
        need(act, e1)
        e1 = did(act, act.activation(spl, spl, ACT.Ln, bias=1.0))
        need(act, e1)
        spl_ok = did(act, act.activation(spl, spl, ACT.Copy, scale=-8.0))
        lb, oml = c(2), c(2)
        lbt = c(2)
        e2 = did(dve, dve.tensor_tensor(lbt, col("hgrn_lower_bounds", 0, 2), col("hgrn_lower_bounds", 0, 2), ALU.subtract))
        need(act, e2)
        e2 = did(act, act.activation(lb, lbt, ACT.Exp))
        need(dve, e2)
        e2 = did(dve, dve.reciprocal(lbt, lb))
        need(dve, e2)
        e2 = did(dve, dve.tensor_tensor(lbt, lb, lbt, ALU.mult))
        need(dve, e2)
        e2 = did(dve, dve.tensor_tensor(lb, lbt, lbt, ALU.subtract))
        need(dve, e2)
        e2 = did(dve, dve.tensor_scalar(oml, lb, -1.0, 1.0, ALU.mult, ALU.add))
        lb_ok = e2

        xpv = proj[:, :, D:D + 2 * (S + 4)].rearrange("p m (b s) -> p m b s", b=2)

        def xp(b):
            return xpv[:, b // 2, b % 2, :]

        g4 = gbo[:, :, :].rearrange("p a (b c) -> p (a b) c", c=S)
        b4 = gb[:, :, :].rearrange("p a (b c) -> p (a b) c", c=S)
        gbt, ra, xc, gi = g4[:, 0:4, :], g4[:, 4:8, :], b4[:, 0:4, :], b4[:, 4:8, :]
        wab = n[:, :, 512:1024].rearrange("p g (b j) -> p g b j", b=4)
        lr = c(S)
        wup = c(P)
        need(pool, *hT_ok)
        zw = did(pool, pool.memset(wab, 0.0))
        zx = did(pool, pool.memset(xpv, 0.0))
        need(pool, zw)
        for g, name in enumerate(("rg_w_a", "rg_w_x")):
            for two in range(2):
                w_in_m = c_lng.tick(pool.dma_start(wab[two * 64:two * 64 + 64, g, :, two * 64:two * 64 + 64],
                                                   A[name][0].rearrange("(b t) i j -> t i b j", t=2)[two]), 16)
        wup_in = c_lng.tick(pool.dma_start(wup[0:LR_RANK, :], A["gla_w_gate_up"][0]), 16)
        w_in_m = wup_in

        t_freed = {}

        def t_block(chunk, c0, width, b, evacuate):
            slot, split, _, hv, lv = chunk
            need(pe, split)
            need(pe, *t_freed.get(b, ()))
            for k in range(KD):
                i = mm3(bank[b][:, 0:S], (hv[:, k, c0:c0 + P], lv[:, k, c0:c0 + P]), (xTh[:, k, :], xTl[:, k, :]), k == 0, k == KD - 1)
            t = did(pe, i)
            ring_state["split_free"][slot] = [t]
            e = evacuate(bank[b][0:width, 0:S], t)
            t_freed[b] = (e,)
            return t, e

        def copy_by(eng, dst, scale=None):
            def go(src, t):
                need(eng, t)
                if eng is dve:
                    return did(dve, dve.tensor_copy(dst, src) if scale is None else dve.tensor_scalar(dst, src, scale, None, ALU.mult))
                return did(act, act.activation(dst, src, ACT.Copy) if scale is None else act.activation(dst, src, ACT.Copy, scale=scale))
            return go

        need(pe, *hT_ok)
        _, q0 = t_block(prepared[0], 0, P, 4, copy_by(dve, gq[:, 0, :]))
        _, q1 = t_block(prepared[0], P, P, 5, copy_by(act, gq[:, 1, :]))
        prepared.append(prepare(W[:, C_Q:C_Q + 256]))
        _, f0 = t_block(prepared[1], 0, P, 6, copy_by(dve, zf[:, 0, :]))
        _, f1 = t_block(prepared[1], P, P, 7, copy_by(act, zf[:, 1, :]))
        prepared.append(prepare(W[:, C_LR:C_LR + LR_RANK], LR_RANK))
        _, q2 = t_block(prepared[2], 0, P, 4, copy_by(dve, gq[:, 2, :], 32 ** -0.5))
        _, k2 = t_block(prepared[2], P, P, 5, copy_by(act, gk[:, 2, :]))
        _, l0 = t_block(prepared[3], 0, LR_RANK, 6, copy_by(dve, lr[0:LR_RANK, :]))
        rest = [A_I, A_G, C_V, C_G, B_X, B_X + 256, B_G, B_G + 256]
        prepared = [prepare(W[:, c0:c0 + WCOLS]) for c0 in rest[0:2]]
        need(act, f0, f1)
        sg = did(act, act.activation(ee[:, 0:512], zf.rearrange("p a b -> p (a b)"), ACT.Sigmoid))
        kg = did(act, act.activation(gk[:, 0:2, :], zf, ACT.Sigmoid, scale=-1.0))
        need(dve, sg, kg, lb_ok)
        for b in range(2):
            k = did(dve, dve.tensor_scalar(gk[:, b, :], gk[:, b, :], oml[:, b:b + 1], None, ALU.mult))
            k = did(dve, dve.tensor_scalar(lf[:, b, :], ee[:, b * S:(b + 1) * S], oml[:, b:b + 1], lb[:, b:b + 1], ALU.mult, ALU.add))
        need(dve, k)
        k = did(dve, dve.tensor_scalar(lf[:, 0:2, :], lf[:, 0:2, :], F_FLOOR, None, ALU.max))
        need(pe, l0, wup_in)
        need(pe, *t_freed[7])
        t = did(pe, pe.matmul(bank[7][:, 0:S], wup[0:LR_RANK, :], lr[0:LR_RANK, :], start=True, stop=True))
        need(dve, t)
        z2 = dd[:, 0:S]
        a2 = dd[:, S:2 * S]
        kz = did(dve, dve.tensor_scalar(z2, bank[7][:, 0:S], col("gla_b_gate"), None, ALU.add))
        t_freed[7] = (kz,)
        need(act, kz, k)
        ka = did(act, act.activation(a2, z2, ACT.Abs))
        kf = did(act, act.activation(lf[:, 0:2, :], lf[:, 0:2, :], ACT.Ln))
        need(act, ka)
        ka = did(act, act.activation(a2, a2, ACT.Exp, scale=-1.0))
        need(act, ka)
        ka = did(act, act.activation(a2, a2, ACT.Ln, bias=1.0))
        need(dve, kz)
        z3 = dd[:, 2 * S:3 * S]
        kz = did(dve, dve.tensor_scalar(z3, z2, 0.0, 1.0 / 16, ALU.min, ALU.mult))
        need(dve, ka, kz)
        k = did(dve, dve.scalar_tensor_tensor(out=lf[:, 2, :], in0=a2, scalar=-1.0 / 16, in1=z3, op0=ALU.mult, op1=ALU.add))
        need(dve, k, kf, *par_in)
        for w in range(2):
            k = did(dve, dve.tensor_tensor_scan(cum[:, w].rearrange("p a b -> p (a b)"), keep[:, w].rearrange("p a b -> p (a b)"),
                                                lf.rearrange("p a b -> p (a b)"), 0.0, ALU.mult, ALU.add))
        cum_ok = k

        for j in range(4):
            b0 = 2 * (j % 2)
            t = token_chunk(prepared[j], lambda m: bank[b0 + m][:, 0:WCOLS], [t_freed[b0]] if b0 in t_freed else [])
            need(act, t)
            for m in range(M):
                ig_ok = did(act, act.activation(ig[:, m, j * 256:j * 256 + 256], bank[b0 + m][:, 0:WCOLS], ACT.Copy))
            t_freed[b0] = ig_ok
            prepared.append(prepare(W[:, rest[j + 2]:rest[j + 2] + WCOLS]))
        need(act, zx)
        for j in range(4):
            for z in range(2):
                b = 2 * (j % 2) + z
                dst = xp(b)[:, 3:3 + S] if j < 2 else gbt[:, b, :]
                t, bg = t_block(prepared[4 + j], z * P, P, 4 + b, copy_by(act, dst))
                bx = bg if j < 2 else bx
            if j + 6 < len(rest):
                prepared.append(prepare(W[:, rest[j + 6]:rest[j + 6] + WCOLS]))
        out_ahead = [prepare(A["w_out"][0][:, c0:c0 + WCOLS]) for c0 in (0, WCOLS)]

        need(dve, bx)
        for b in range(4):
            k = did(dve, dve.tensor_scalar(xc[:, b, :], xp(b)[:, 3:3 + S], col("rg_conv_w", 12 + b), col("rg_conv_b", b), ALU.mult, ALU.add))
            for tap in range(3):
                need(dve, k)
                k = did(dve, dve.scalar_tensor_tensor(out=xc[:, b, :], in0=xp(b)[:, tap:tap + S], scalar=col("rg_conv_w", 4 * tap + b),
                                                      in1=xc[:, b, :], op0=ALU.mult, op1=ALU.add))
        need(pe, k, w_in_m, bg, ig_ok)
        for b in range(4):
            pe.matmul(bank[4 + b // 2][:, (b % 2) * S:(b % 2 + 1) * S], wab[:, 0, b, :], xc[:, b, :], start=True, stop=True)
            i = pe.matmul(bank[6 + b // 2][:, (b % 2) * S:(b % 2 + 1) * S], wab[:, 1, b, :], xc[:, b, :], start=True, stop=True)
        t = did(pe, i)
        need(dve, t)
        for b in range(4):
            cols = slice((b % 2) * S, (b % 2 + 1) * S)
            did(dve, dve.tensor_scalar(ra[:, b, :], bank[4 + b // 2][:, cols], col("rg_b_a", b), None, ALU.add))
            k = did(dve, dve.tensor_scalar(gi[:, b, :], bank[6 + b // 2][:, cols], col("rg_b_x", b), None, ALU.add))
        rg_psum = k
        need(act, k)
        sr_ = did(act, act.activation(ra, ra, ACT.Sigmoid))
        si_ = did(act, act.activation(gi, gi, ACT.Sigmoid))
        need(dve, sr_, si_, spl_ok)
        for b in range(4):
            k = did(dve, dve.tensor_scalar(ra[:, b, :], ra[:, b, :], spl[:, b:b + 1], None, ALU.mult))
        k = did(dve, dve.tensor_tensor(gi, gi, xc, ALU.mult))
        need(act, k)
        aa = xc
        for m in range(M):
            tha = did(act, act.activation(xpv[:, m, :, 0:S], ra[:, 2 * m:2 * m + 2, :], ACT.Tanh))
        exa = did(act, act.activation(aa, ra, ACT.Exp))
        need(dve, exa, tha)
        k = did(dve, dve.tensor_tensor(ra, aa, aa, ALU.mult))
        need(dve, k)
        for m in range(M):
            rm = ra[:, 2 * m:2 * m + 2, :]
            k = did(dve, dve.scalar_tensor_tensor(out=rm, in0=rm, scalar=1.0, in1=xpv[:, m, :, 0:S], op0=ALU.add, op1=ALU.mult))
        need(dve, k)
        k = did(dve, dve.tensor_scalar(ra, ra, -1.0, 2.0 ** -116, ALU.mult, ALU.max))
        need(act, k)
        k = did(act, act.activation(ra, ra, ACT.Sqrt))
        ge = did(act, act.activation(gbt, gbt, ACT.Gelu_apprx_tanh))
        need(dve, k, ge)
        k = did(dve, dve.tensor_tensor(ra, ra, gi, ALU.mult))
        need(dve, k)
        for b in range(4):
            k = did(dve, dve.tensor_tensor_scan(gi[:, b, :], aa[:, b, :], ra[:, b, :], 0.0, ALU.mult, ALU.add))
        need(dve, k)
        k = did(dve, dve.tensor_tensor(gi, gi, gbt, ALU.mult))
        need(act, k)
        k = did(act, act.activation(xTh[:, 2:6, :], gi, ACT.Copy))
        need(dve, k)
        rg_ok = did(dve, dve.tensor_tensor(xTl[:, 2:6, :], gi, xTh[:, 2:6, :].bitcast(F32), ALU.subtract))

        mk = masks.bitcast(I32)
        bank_free = [(rg_psum,)] * 8
        sc_mark = None
        q_reads = [(), ()]
        for lev in range(len(LEVELS) + 1):
            if lev == 0:
                qq, kk, ready = gq, gk, [q0, q1, q2, k2, cum_ok]
            else:
                s = LEVELS[lev - 1]
                cw = cum[:, 0 if s <= CHUNK // 2 else 1].rearrange("p a (n w) -> p (a n) w", w=2 * s)
                mid = bc(cw[:, :, s - 1], 2, 2 * s)
                need(dve, cum_ok, *([sc_mark] if sc_mark else []))
                k = did(dve, dve.tensor_tensor(dd.rearrange("p (n w) -> p n w", w=2 * s), cw, mid, ALU.subtract))
                need(act, k)
                k = did(act, act.activation(dd, dd, ACT.Abs))
                need(act, k, *q_reads[(lev + 1) % 2])
                k = sc_mark = did(act, act.activation(ee, dd, ACT.Exp, scale=-1.0))
                need(dve, k, *q_reads[lev % 2])
                need(pool, k, *q_reads[lev % 2])
                qq, kk = qs[:, lev % 2], ks[:, lev % 2]
                e3 = ee.rearrange("p (a b) -> p a b", a=3)
                kq = did(dve, dve.tensor_tensor(qq, gq, e3, ALU.mult))
                kp = did(pool, pool.tensor_tensor(kk, gk, e3, ALU.mult))
                ready = [kq, kp]
                sc_mark = kq
                sc_pool = kp
                need(act, kq, kp)
            need(pe, *ready)
            pairs = [(0, 0, 0), (1, 1, 1)] if lev <= 7 else [(0, 1, 2)]
            for kt, qt, dst in pairs:
                bs = [4 * (dst % 2) + b for b in range(4)]
                for b in bs:
                    need(pe, *bank_free[b])
                for r in range(3):
                    for b in range(4):
                        if r < len(BANK_HEADS[b]):
                            head, base, rws, blk = BANK_HEADS[b][r]
                            i = pe.matmul(bank[bs[b]][:, r * P:(r + 1) * P], kk[base:base + rws, blk, kt * P:(kt + 1) * P],
                                          qq[base:base + rws, blk, qt * P:(qt + 1) * P], start=True, stop=True)
                t = did(pe, i)
                need(dve, t)
                for b in range(4):
                    w = len(BANK_HEADS[b])
                    o = scoreT[dst][:, BANK_SLOT[b]:BANK_SLOT[b] + w, :]
                    p3 = bank[bs[b]][:, 0:w * P].rearrange("p (a b) -> p a b", a=w)
                    if lev == 0:
                        i = dve.tensor_tensor(o, p3, bc(ident[:, :], 1, w), ALU.mult)
                    elif dst == 2:
                        i = dve.tensor_copy(o, p3)
                    else:
                        if b == 0:
                            need(dve, (c_dve, c_dve.n))
                        i = dve.copy_predicated(o, bc(mk[:, lev - 1, :], 1, w), p3)
                    k = did(dve, i)
                    bank_free[bs[b]] = (k,)
            q_reads[lev % 2] = (t,)
        need(pe, k, ig_ok)
        for m in range(M):
            for b in range(4):
                for r, (head, _, _, _) in enumerate(BANK_HEADS[b]):
                    sl = BANK_SLOT[b] + r
                    v0 = (head * HD) if head < 4 else 512 + (head - 4) * HD
                    o = bank[m][:, head * HD:(head + 1) * HD]
                    if m:
                        pe.matmul(o, scoreT[2][:, sl, :], ig[:, 0, v0:v0 + HD], start=True, stop=False)
                    i = pe.matmul(o, scoreT[m][:, sl, :], ig[:, m, v0:v0 + HD], start=(m == 0), stop=True)
        t = did(pe, i)
        sq = dd[:, 0:512]
        need(act, t, ig_ok)
        for m in range(M):
            k = did(act, act.activation(sq, bank[m][:, :], ACT.Square))
            need(dve, k)
            k = did(dve, dve.tensor_reduce(hsum[:, m, :], sq.rearrange("p (h d) -> p h d", d=HD), X, ALU.add))
            need(act, k)
        need(dve, k)
        k = did(dve, dve.tensor_scalar(hsum, hsum, 1.0 / HD, EPS1, ALU.mult, ALU.add))
        need(act, k)
        k = did(act, act.activation(hrs, hsum, ACT.Sqrt))
        for m in range(M):
            for half in range(2):
                sl_ = did(act, act.activation(sil[:, 2 * half + m, :], ig[:, m, half * 512 + 256:half * 512 + 512], ACT.Silu))
        need(dve, k)
        k = did(dve, dve.reciprocal(hrs, hrs))
        need(dve, k, sl_)
        for m in range(M):
            for half in range(2):
                o3 = o_tok[:, m, half * 256:half * 256 + 256]
                o4 = o3.rearrange("p (h d) -> p h d", d=HD)
                k = did(dve, dve.tensor_tensor(o4, bank[m][:, half * 256:half * 256 + 256].rearrange("p (h d) -> p h d", d=HD),
                                               bc(hrs[:, m, 4 * half:4 * half + 4], 2, HD), ALU.mult))
                need(dve, k)
                k = did(dve, dve.tensor_tensor(o3, o3, gain_bc[:, half, :], ALU.mult))
                need(dve, k)
                k = did(dve, dve.tensor_tensor(o3, o3, sil[:, 2 * half + m, :], ALU.mult))
        need(pe, k)
        for j, dst in enumerate((0, 1, 6, 7)):
            b = 4 + j
            for m in range(M):
                i = pe.transpose(bank[b][:, m * P:(m + 1) * P], o_tok[:, m, j * P:(j + 1) * P], ident[:, :])
            t = did(pe, i)
            need(act, t)
            k = did(act, act.activation(xTh[:, dst, :], bank[b][:, 0:S], ACT.Copy))
            need(dve, k)
            k = did(dve, dve.tensor_tensor(xTl[:, dst, :], bank[b][:, 0:S], xTh[:, dst, :].bitcast(F32), ALU.subtract))
        summed = out_product(A["w_out"][0], out_ahead, [k, rg_ok])

        need(pool, rg_ok)
        g_in = c_lng.tick(pool.dma_start(gb[:, 0, :], all_partitions(A["norm_final"], D)), 16)
        Wg, Wv, Wd = A["ffn_w_gate"][0], A["ffn_w_val"][0], A["ffn_w_down"][0]
        geglu = (lambda j: Wg[:, bass.ds(j * P, P)], lambda j: Wv[:, bass.ds(j * P, P)], lambda j: Wd[bass.ds(j * P, P), :])
        ffn_ahead(*geglu)
        hT_ok = norm(summed, 1.0, EPS1, False, lambda k: col("norm_ffn", k), None)
        summed = ffn(*geglu, FT1, hT_ok, True)
        norm(summed, 1.0, EPS1, False, lambda k: col("norm_final", k), None, token_gain=g_in)

        c2 = Carve()
        win_bias, dif_bias = c2(M, 4, S), c2(M, 4, S)
        rope = c2(M, 6 * 16)
        qT, kT = c2(4, S), c2(4, S)
        qT2, kT2 = c2(4, S), c2(4, S)
        cT = c2(3, S)
        pb = c2(2, 512)
        ptb = c2(2, 512)
        small = c2(16, 8)
        sq2 = c2(384)
        cn = [t_[:, :, :].rearrange("p a b -> p (a b)")[:, 0:384] for t_ in (conv, nonlin)]
        rt = act32[:, :, :].rearrange("p a b -> p (a b)")[:, 0:384].rearrange("p (a b c) -> p a b c", a=M, b=2)
        gains = c2(256 + 128 + 64 + 64 + 64 + 4 + 128 + 2)
        hq = c2(M, 16)
        SCALE_A, SCALE_B, SCALE_C, SCALE_D = HD ** -0.5, (NOPE + ROPE) ** -0.5, HD ** -0.5, 32 ** -0.5
        fresh_counters()
        sp.dma_start(win_bias, C["win_bias"]).then_inc(c_par.sem, 16)
        sp.dma_start(dif_bias, C["dif_bias"]).then_inc(c_par.sem, 16)
        sp.dma_start(rope, C["rope"].rearrange("p m a b -> p m (a b)")).then_inc(c_par.sem, 16)
        sp.wait_ge(c_par.sem, 48)

        with nc.Fori(0, LAYERS) as l:
            fresh_counters()
            layer(l)
        c_out.n = 0
        fresh_counters()
        for m in range(M):
            t = c_out.tick(sp.dma_start(out[0, m * P:(m + 1) * P, :], x[:, m, :]), 16)
        need(sp, t)

_INS = ["x", "norm_mix", "w_in", "hgrn_lower_bounds", "hgrn_norm", "rg_conv_w", "rg_conv_b", "rg_w_a", "rg_b_a", "rg_w_x",
        "rg_b_x", "rg_lambda", "gla_w_gate_up", "gla_b_gate", "gla_norm", "w_out", "norm_ffn", "ffn_w_gate", "ffn_w_val",
        "ffn_conv_w", "ffn_conv_b", "ffn_w_down", "norm_final", "w_in_2", "win_sink_2", "mla_q_norm_2", "mla_w_uq_2",
        "mla_kv_norm_2", "mla_w_ukv_2", "ax_q_norm_2", "ax_k_norm_2", "diff_lambda_2", "diff_subln_2", "w_out_2",
        "ffn_w_gu_2", "ffn_w_down_2", "ln_g_2", "ln_b_2"]


def kernel(**inputs):
    import numpy as _np
    import concourse.bacc as _bacc
    from concourse.bass_utils import run_bass_kernel_spmd as _run

    nc = _bacc.Bacc("TRN2", target_bir_lowering=False, num_devices=1)
    arrays, aps, consts = {}, {}, {}
    for name in _INS:
        a = _np.ascontiguousarray(inputs[name])
        arrays[f"in_{name}"] = a
        aps[name] = nc.dram_tensor(f"in_{name}", a.shape, mybir.dt.from_np(a.dtype), kind="ExternalInput").ap()
    for name, a in constants().items():
        arrays[f"const_{name}"] = a
        consts[name] = nc.dram_tensor(f"const_{name}", a.shape, mybir.dt.from_np(a.dtype), kind="ExternalInput").ap()
    out = nc.dram_tensor("out", (1, S, D), F32, kind="ExternalOutput").ap()
    program(nc, aps, consts, out)
    r = _run(nc, [arrays], core_ids=[0])
    return r.results[0]["out"]
```

```python
from contextlib import ExitStack

import numpy as np
import concourse.bass as bass
from concourse import mybir
from concourse.alu_op_type import AluOpType as ALU

F32 = mybir.dt.float32
BF16 = mybir.dt.bfloat16
I32 = mybir.dt.int32
F32R = mybir.dt.float32r
ACT = mybir.ActivationFunctionType
X = mybir.AxisListType.X

P = 128
S = 256
M = S // P
D = 1024
KD = D // P
HALF = 512
HD = 64

A_Q, A_F, A_I, A_G, B_X, B_G, C_Q, C_K, C_V, C_G, C_LR = 0, 256, 512, 768, 1024, 1536, 2048, 2176, 2304, 2560, 2816
IN1 = 2832
LR_RANK = 16
DFF1 = 2688
FT1 = DFF1 // P
EPS1 = 1e-6
F_FLOOR = 1e-20
LEVELS = [1, 2, 4, 8, 16, 32, 64, 128]
CHUNK = 64
BANK_HEADS = [[(0, 0, 64, 0), (2, 0, 64, 1), (4, 0, 32, 2)],
              [(1, 64, 64, 0), (3, 64, 64, 1), (6, 64, 32, 2)],
              [(5, 32, 32, 2)],
              [(7, 96, 32, 2)]]
BANK_SLOT = [0, 3, 6, 7]

LAYERS = 2
IN2 = 2208
WIN_Q, WIN_K, WIN_V = 0, 256, 384
MLA_Q, MLA_KV, MLA_KR = 512, 768, 896
AX_Q, AX_V = 928, 1312
DF_Q, DF_K, DF_V = 1440, 1696, 1952
NOPE, ROPE = 64, 32
DFF2 = 2816
FT2 = DFF2 // P
EPS2 = 1e-5
ALPHA = float((2 * LAYERS) ** 0.25)
WCOLS = 256


def constants():
    t = {}
    t["ident"] = np.eye(P, dtype=np.float32)
    slopes = (2.0 ** (-8.0 * (np.arange(8, dtype=np.float32) + 1.0) / 8)).astype(np.float32)
    q = np.arange(S)[:, None]
    k = np.arange(S)[None, :]
    dist = np.abs(q - k).astype(np.float32)
    win = np.where(dist <= 128, -slopes[:4, None, None] * dist, np.float32(-1e30)).astype(np.float32)
    dif = (-slopes[4:, None, None] * dist).astype(np.float32)
    t["win_bias"] = np.ascontiguousarray(win.reshape(4, M, P, S).transpose(2, 1, 0, 3))
    t["dif_bias"] = np.ascontiguousarray(dif.reshape(4, M, P, S).transpose(2, 1, 0, 3))

    def angles(pos, dim):
        inv = (np.float32(10000.0) ** (-np.arange(0, dim, 2, dtype=np.float32) / np.float32(dim))).astype(np.float32)
        a = pos.astype(np.float32)[:, None] * inv[None, :]
        return np.cos(a).astype(np.float32), np.sin(a).astype(np.float32)

    pos = np.arange(S)
    cm, sm = angles(pos, ROPE)
    cr, sr = angles(pos // 64, 32)
    cc, sc = angles(pos % 64, 32)
    rope = np.stack([cm, sm, cr, cc, sr, sc], 1)
    t["rope"] = np.ascontiguousarray(rope.reshape(M, P, 6, 16).transpose(1, 0, 2, 3))
    j = np.arange(P)[:, None]
    i = np.arange(P)[None, :]
    masks = [((j // (2 * s) == i // (2 * s)) & (j % (2 * s) < s) & (i % (2 * s) >= s)) for s in LEVELS[:-1]]
    t["masks"] = np.ascontiguousarray(np.stack(masks, 1).astype(np.int32))
    keep = np.ones((P, 2, 3, S), np.float32)
    keep[:, 0, :, ::CHUNK] = 0
    keep[:, 1, :, ::S] = 0
    t["keep"] = keep
    li = [0.8 - 0.6 * np.exp(-0.3 * l) for l in range(LAYERS)]
    t["lam_init"] = np.array([[v, 1.0 - v] for v in li], np.float32)
    return t


CONSTS = {"ident": (P, P), "win_bias": (P, M, 4, S), "dif_bias": (P, M, 4, S), "rope": (P, M, 6, 16),
          "masks": (P, 7, P), "keep": (P, 2, 3, S), "lam_init": (LAYERS, 2)}


class Counter:

    def __init__(self, nc, ctx, name):
        self.sem, self.n = ctx.enter_context(nc.semaphore(name)), 0

    def tick(self, ins, by=1):
        ins.then_inc(self.sem, by)
        self.n += by
        return (self, self.n)


def program(nc, A, C, out):
    ctx = ExitStack()
    with ctx:
        def sb(name, shape, dt=F32):
            return ctx.enter_context(nc.sbuf_tensor(name, shape, dt))

        pe, act, dve, pool, sp = nc.tensor, nc.scalar, nc.vector, nc.gpsimd, nc.sync
        bank = [ctx.enter_context(nc.psum_tensor(f"bank{i}", [P, HALF], F32)) for i in range(8)]
        counters = []

        def counter(name):
            counters.append(Counter(nc, ctx, name))
            return counters[-1]

        c_pe, c_act, c_dve, c_pool = (counter(n) for n in ("pe_steps", "act_steps", "dve_steps", "pool_steps"))
        c_gu = [counter(f"gate_up_loaded{i}") for i in range(2)]
        c_dn = [counter(f"down_loaded{i}") for i in range(2)]
        c_gu_hi = [counter(f"gate_up_hi{i}") for i in range(2)]
        c_dn_hi = [counter(f"down_hi{i}") for i in range(2)]
        c_gu_lo = [counter(f"gate_up_split{i}") for i in range(2)]
        c_dn_lo = [counter(f"down_split{i}") for i in range(2)]
        c_gate, c_up, c_down, c_conv, c_gelu, c_prod, c_ahi, c_alo = (counter(n) for n in (
            "gate_done", "up_done", "down_done", "conv_done", "nonlin_done", "product_done", "product_hi", "product_split"))
        c_par = counter("parameters_loaded")
        c_gain2, c_row2, c_ln2 = counter("layer_gains_loaded"), counter("layer_rows_loaded"), counter("layer_ln_loaded")
        c_ident = counter("identity_loaded")
        c_uq = counter("mla_weights_loaded")
        c_row = counter("rows_loaded")
        c_lng = counter("ln_rows_loaded")
        c_out = counter("x_moved")

        def need(eng, *marks):
            best = {}
            for c, v in marks:
                best[id(c)] = (c, max(v, best.get(id(c), (c, 0))[1]))
            for c, v in best.values():
                if v > 0:
                    eng.wait_ge(c.sem, v)

        def did(eng, ins):
            return {id(pe): c_pe, id(act): c_act, id(dve): c_dve, id(pool): c_pool}[id(eng)].tick(ins)

        in_flight = []

        def land():
            need(sp, *in_flight, *((c, c.n) for c in (*c_gu, *c_dn)))
            in_flight.clear()

        def fresh_counters():
            nc.all_engine_barrier()
            for c in counters:
                sp.sem_clear(c.sem)
                c.n = 0
            sp.sem_inc(c_gu_lo[0].sem, 1)
            c_gu_lo[0].n = 1
            nc.all_engine_barrier()
            ring_state.update(next=0, staged_free=[[], []], split_free=[[], []], dn_staged_free=[[], []], dn_split_free=[[], []])
            x_ok.clear()

        st_gu = [sb(f"st_gu{i}", [P, KD * WCOLS]) for i in range(2)]
        hi_gu = [sb(f"hi_gu{i}", [P, KD * WCOLS], F32R) for i in range(2)]
        lo_gu = [sb(f"lo_gu{i}", [P, KD * WCOLS], F32R) for i in range(2)]
        st_dn = [sb(f"st_dn{i}", [P, D]) for i in range(2)]
        hi_dn = [sb(f"hi_dn{i}", [P, D], F32R) for i in range(2)]
        lo_dn = [sb(f"lo_dn{i}", [P, D], F32R) for i in range(2)]
        x = sb("x", [P, M, D])
        n = sb("n", [P, M, D])
        xTh = sb("xTh", [P, KD, S], F32R)
        xTl = sb("xTl", [P, KD, S], F32R)
        proj = sb("proj", [P, M, IN2])
        act32 = sb("act32", [P, 2, S])
        actTh = sb("actTh", [P, 2, S], F32R)
        actTl = sb("actTl", [P, 2, S], F32R)
        nonlin = sb("nonlin", [P, 2, S])
        conv = sb("conv", [P, 2, S])
        ident = sb("ident", [P, P])
        zeros = sb("zeros", [P, HALF], BF16)
        rows = sb("rows", [P, P])
        rows2 = sb("rows2", [P, P])
        par1 = sb("par1", [P, 60])
        parc = sb("parc", [P, 4, FT1])
        lnT = sb("lnT", [P, 6, KD])
        gb = sb("gb", [P, 2, D])
        stats = sb("stats", [P, M, 2, 6])
        mv = sb("mv", [P, M, 2])
        ms = sb("ms", [P, M])
        sd = sb("sd", [P, M])
        rs = sb("rs", [P, M])
        nmr = sb("nmr", [P, M])
        gbo = sb("gbo", [P, M, D])
        big = sb("big", [P, 12900])

        class Carve:
            def __init__(self):
                self.at = 0

            def __call__(self, *shape):
                size = int(np.prod(shape))
                v = big[:, self.at:self.at + size]
                self.at += size
                assert self.at <= 12900, self.at
                if len(shape) == 2:
                    v = v.rearrange("p (a b) -> p a b", a=shape[0])
                if len(shape) == 3:
                    v = v.rearrange("p (a b c) -> p a b c", a=shape[0], b=shape[1])
                if len(shape) == 4:
                    v = v.rearrange("p (a b c d) -> p a b c d", a=shape[0], b=shape[1], c=shape[2])
                return v

        def bc(ap, axis, count):
            shape = list(ap.shape)
            shape.insert(axis, count)
            return ap.unsqueeze(axis).to_broadcast(shape)

        def all_partitions(ap1d, width):
            return ap1d.rearrange("(a n) -> a n", a=1).to_broadcast([P, width])

        ring_state = {"next": 0, "staged_free": [[], []], "split_free": [[], []], "dn_staged_free": [[], []], "dn_split_free": [[], []]}

        def mm3(o, lhs, rhs, start, stop, **kw):
            pe.matmul(o, lhs[0], rhs[0], start=start, stop=False, **kw)
            pe.matmul(o, lhs[0], rhs[1], start=False, stop=False, **kw)
            return pe.matmul(o, lhs[1], rhs[0], start=False, stop=stop, **kw)

        def prepare(dram, width=WCOLS, low_by=dve):
            i = ring_state["next"]
            ring_state["next"] = 1 - i
            need(sp, *ring_state["staged_free"][i])
            v = st_gu[i][:, :].rearrange("p (k n) -> p k n", k=KD)
            ld = c_gu[i].tick(sp.dma_start(v[:, :, 0:width], dram.rearrange("(k p) n -> p k n", p=P)), 16)
            hv = hi_gu[i][:, :].rearrange("p (k n) -> p k n", k=KD)
            lv = lo_gu[i][:, :].rearrange("p (k n) -> p k n", k=KD)
            need(act, ld, *ring_state["split_free"][i])
            h = c_gu_hi[i].tick(act.activation(hv[:, :, 0:width], v[:, :, 0:width], ACT.Copy))
            need(low_by, h)
            lo = c_gu_lo[i].tick(low_by.tensor_tensor(lv[:, :, 0:width], v[:, :, 0:width], hv[:, :, 0:width].bitcast(F32), ALU.subtract))
            ring_state["staged_free"][i] = [lo]
            return i, lo, width, hv, lv

        x_ok = []

        def transpose_tiles(src, gain, bias, src_done, extra=()):
            temps = [t_[:, :, :].rearrange("p a b -> p (a b)") for t_ in (act32, conv, nonlin)]
            tmp_free = [()] * 3
            full_ok, hi_ok, done = {}, {}, []

            def full(j):
                b = 4 + j
                need(pe, *(extra if j == 0 else ()), *(src_done if len(src_done) < 4 else src_done[2 * (j // 2):2 * (j // 2) + 2]))
                for z in range(2):
                    for m in range(M):
                        t = pe.transpose(bank[b][:, z * S + m * P:z * S + (m + 1) * P], src[:, m, (2 * j + z) * P:(2 * j + z + 1) * P], ident[:, :])
                full_ok[j] = [did(pe, t)]
                if bias:
                    k = 2 * j
                    tmp = temps[j % 3]
                    for e in (dve, act):
                        need(e, full_ok[j][0], *tmp_free[j % 3])
                    f = did(dve, dve.tensor_scalar(tmp[:, 0:S], bank[b][:, 0:S], gain(k), bias(k), ALU.mult, ALU.add))
                    need(act, f)
                    g = did(act, act.activation(tmp[:, S:2 * S], bank[b][:, S:2 * S], ACT.Identity, scale=gain(k + 1), bias=bias(k + 1)))
                    full_ok[j] = [f, g]

            def high(j):
                ps = temps[j % 3] if bias else bank[4 + j][:, :]
                need(act, *full_ok[j])
                hi = xTh[:, 2 * j:2 * j + 2, :].rearrange("p a b -> p (a b)")
                if gain and not bias:
                    for z in range(2):
                        h = act.activation(hi[:, z * S:(z + 1) * S], ps[:, z * S:(z + 1) * S], ACT.Copy, scale=gain(2 * j + z))
                else:
                    h = act.activation(hi, ps, ACT.Copy)
                hi_ok[j] = did(act, h)

            def low(j):
                ps = temps[j % 3] if bias else bank[4 + j][:, :]
                hi, lo = (t_[:, 2 * j:2 * j + 2, :].rearrange("p a b -> p (a b)") for t_ in (xTh, xTl))
                need(dve, hi_ok[j], *full_ok[j])
                if gain and not bias:
                    for z in range(2):
                        zs = slice(z * S, (z + 1) * S)
                        d = dve.scalar_tensor_tensor(out=lo[:, zs], in0=ps[:, zs], scalar=gain(2 * j + z), in1=hi[:, zs].bitcast(F32),
                                                     op0=ALU.mult, op1=ALU.subtract)
                else:
                    d = dve.tensor_tensor(lo, ps, hi.bitcast(F32), ALU.subtract)
                d = did(dve, d)
                tmp_free[j % 3] = (d,)
                done.extend([d, d])

            pairs = KD // 2
            for j in range(pairs + 2):
                if j < pairs:
                    full(j)
                if 1 <= j <= pairs:
                    high(j - 1)
                if 2 <= j:
                    low(j - 2)
            return done

        def norm(added, alpha, eps, centred, gain, bias, token_gain=None):
            xd, bn, nd = {}, {}, {}

            def add(m, h):
                xs = x[:, m, h * HALF:(h + 1) * HALF]
                if added:
                    need(dve, added[m], *x_ok)
                    xd[m, h] = did(dve, dve.scalar_tensor_tensor(out=xs, in0=xs, scalar=alpha, in1=bank[2 * m + h][:, :],
                                                                 op0=ALU.mult, op1=ALU.add))

            def statistics(m, h):
                need(dve, *([xd[m, h]] if added else []))
                bn[m, h] = did(dve, dve.bn_stats(stats[:, m, h, :], x[:, m, h * HALF:(h + 1) * HALF]))

            def deviation(m):
                one = slice(m, m + 1)
                need(dve, bn[m, 0], bn[m, 1])
                k = did(dve, dve.bn_aggr(mv[:, m, :], stats[:, m, :, :].rearrange("p a b -> p (a b)")))
                need(dve, k)
                if centred:
                    k = did(dve, dve.tensor_scalar(ms[:, one], mv[:, m, 1:2], eps, None, ALU.add))
                else:
                    k = did(dve, dve.tensor_tensor(ms[:, one], mv[:, m, 0:1], mv[:, m, 0:1], ALU.mult))
                    need(dve, k)
                    k = did(dve, dve.scalar_tensor_tensor(out=ms[:, one], in0=ms[:, one], scalar=eps, in1=mv[:, m, 1:2], op0=ALU.add, op1=ALU.add))
                need(act, k)
                return did(act, act.activation(sd[:, one], ms[:, one], ACT.Sqrt))

            def scales(m, k):
                one = slice(m, m + 1)
                need(dve, k)
                k = did(dve, dve.reciprocal(rs[:, one], sd[:, one]))
                if centred:
                    need(dve, k)
                    k = did(dve, dve.scalar_tensor_tensor(out=nmr[:, one], in0=mv[:, m, 0:1], scalar=-1.0, in1=rs[:, one], op0=ALU.mult, op1=ALU.mult))
                return k

            def normed(m, q, e, k):
                qs_ = slice(q * HALF, (q + 1) * HALF)
                need(e, k)
                if e is dve:
                    if centred:
                        i = dve.tensor_scalar(n[:, m, qs_], x[:, m, qs_], rs[:, m:m + 1], nmr[:, m:m + 1], ALU.mult, ALU.add)
                    else:
                        i = dve.tensor_scalar(n[:, m, qs_], x[:, m, qs_], rs[:, m:m + 1], None, ALU.mult)
                elif centred:
                    i = act.activation(n[:, m, qs_], x[:, m, qs_], ACT.Identity, scale=rs[:, m:m + 1], bias=nmr[:, m:m + 1])
                else:
                    i = act.activation(n[:, m, qs_], x[:, m, qs_], ACT.Copy, scale=rs[:, m:m + 1])
                nd[q, m] = did(e, i)

            add(0, 0)
            add(0, 1)
            statistics(0, 0)
            statistics(0, 1)
            add(1, 0)
            k = deviation(0)
            add(1, 1)
            k0_ = scales(0, k)
            for q in range(2):
                normed(0, q, act, k0_)
            statistics(1, 0)
            statistics(1, 1)
            k = deviation(1)
            k = scales(1, k)
            normed(1, 0, dve, k)
            normed(1, 1, act, k)
            nd = [nd[0, 0], nd[0, 1], nd[1, 0], nd[1, 1]]
            done = transpose_tiles(n, gain, bias, nd)
            if token_gain:
                update_x(token_gain, *nd)
            return done

        def update_x(*ready):
            nonlocal x_ok
            need(pool, *ready)
            for m in range(M):
                k = did(pool, pool.tensor_tensor(x[:, m, :], n[:, m, :], gb[:, 0, :], ALU.mult))
                need(pool, k)
                k = did(pool, pool.tensor_tensor(x[:, m, :], x[:, m, :], gb[:, 1, :], ALU.add))
            x_ok = [k]

        def token_chunk(prepared, out_of, ready, by_tile=None):
            slot, split, width, hv, lv = prepared
            need(pe, split, *ready)
            ts = []
            for m in range(M):
                ms_ = slice(m * P, (m + 1) * P)
                for k in range(KD):
                    if by_tile and m == 0:
                        need(pe, by_tile[k])
                    i = mm3(out_of(m), (xTh[:, k, ms_], xTl[:, k, ms_]), (hv[:, k, 0:width], lv[:, k, 0:width]), k == 0, k == KD - 1)
                ts.append(did(pe, i))
            ring_state["split_free"][slot] = [ts[-1]]
            return ts

        def out_product(w_dram, ahead, ready, by_tile=None):
            chunks = list(ahead)
            for c in range(D // WCOLS):
                ts = token_chunk(chunks[c], lambda m: bank[2 * m + c // 2][:, (c % 2) * WCOLS:(c % 2 + 1) * WCOLS], ready,
                                 by_tile if c == 0 else None)
                if c + 2 < D // WCOLS:
                    chunks.append(prepare(w_dram[:, (c + 2) * WCOLS:(c + 3) * WCOLS]))
            return ts

        def gu_view(buf, i):
            return buf[i][:, :].rearrange("p (w k n) -> p w k n", w=2, k=KD)

        def ffn_loads(gate_w, up_w, down_w):
            ring_state["next"] = 0
            for t in range(2):
                need(sp, *ring_state["staged_free"][t])
                for w, dram in ((0, gate_w), (1, up_w)):
                    c_gu[t].tick(sp.dma_start(gu_view(st_gu, t)[:, w], dram(t).rearrange("(k p) n -> p k n", p=P)), 16)
            for t in range(2):
                need(sp, *ring_state["dn_staged_free"][t])
                c_dn[t].tick(sp.dma_start(st_dn[t][:, :], down_w(t)), 16)

        def first_high(t, gu):
            loaded, hi_c, staged, hi, free = (c_gu, c_gu_hi, st_gu, hi_gu, "split_free") if gu else (c_dn, c_dn_hi, st_dn, hi_dn, "dn_split_free")
            need(act, (loaded[t], loaded[t].n), *ring_state[free][t])
            hi_c[t].tick(act.activation(hi[t][:, :], staged[t][:, :], ACT.Copy))

        def first_low(eng, t, gu):
            hi_c, lo_c, staged, hi, lo = (c_gu_hi, c_gu_lo, st_gu, hi_gu, lo_gu) if gu else (c_dn_hi, c_dn_lo, st_dn, hi_dn, lo_dn)
            need(eng, (hi_c[t], hi_c[t].n))
            lo_c[t].tick(eng.tensor_tensor(lo[t][:, :], staged[t][:, :], hi[t][:, :].bitcast(F32), ALU.subtract))

        def ffn_ahead(*weights):
            ffn_loads(*weights)
            first_high(0, True)
            first_low(pool, 0, True)

        def ffn_ahead_rest():
            for t, gu in ((1, True), (0, False), (1, False)):
                first_high(t, gu)
                first_low(dve, t, gu)

        def ffn(gate_w, up_w, down_w, tiles, ready, convolved):
            base = {id(c): c.n for c in counters}
            turns = -(-tiles // 2)

            def at(c, count):
                return base[id(c)] + count

            need(pe, *ready[:1])
            for b in range(4):
                pe.matmul(bank[b][:, :], zeros[:, 0:P], zeros[:, :], start=True, stop=False, skip_group_check=True)
            def split_next(it, t, which):
                if which == "gu":
                    act.wait_ge(c_gu[t].sem, at(c_gu[t], it * 32 + 32))
                    act.wait_ge(c_up.sem, at(c_up, it * 2 + t + 1))
                    act.activation(hi_gu[t][:, :], st_gu[t][:, :], ACT.Copy).then_inc(c_gu_hi[t].sem, 1)
                    dve.wait_ge(c_gu_hi[t].sem, at(c_gu_hi[t], it + 1))
                    dve.tensor_tensor(lo_gu[t][:, :], st_gu[t][:, :], hi_gu[t][:, :].bitcast(F32), ALU.subtract).then_inc(c_gu_lo[t].sem, 1)
                else:
                    act.wait_ge(c_dn[t].sem, at(c_dn[t], it * 16 + 16))
                    act.wait_ge(c_down.sem, at(c_down, it * 2 + t + 1))
                    act.activation(hi_dn[t][:, :], st_dn[t][:, :], ACT.Copy).then_inc(c_dn_hi[t].sem, 1)
                    dve.wait_ge(c_dn_hi[t].sem, at(c_dn_hi[t], it + 1))
                    dve.tensor_tensor(lo_dn[t][:, :], st_dn[t][:, :], hi_dn[t][:, :].bitcast(F32), ALU.subtract).then_inc(c_dn_lo[t].sem, 1)

            summed = []

            def turn(it, here, ahead, last=False):
                for t in range(ahead):
                    sp.wait_ge(c_gu_lo[t].sem, at(c_gu_lo[t], it))
                    for w, dram in ((0, gate_w), (1, up_w)):
                        sp.dma_start(gu_view(st_gu, t)[:, w], dram(it * 2 + (2 + t)).rearrange("(k p) n -> p k n", p=P)).then_inc(c_gu[t].sem, 16)
                for t in range(ahead):
                    sp.wait_ge(c_dn_lo[t].sem, at(c_dn_lo[t], it))
                    sp.dma_start(st_dn[t][:, :], down_w(it * 2 + (2 + t))).then_inc(c_dn[t].sem, 16)
                for t in range(here):
                    g, u = bank[4 + t], bank[6 + t]
                    hv, lv = gu_view(hi_gu, t), gu_view(lo_gu, t)
                    pe.wait_ge(c_gu_lo[t].sem, at(c_gu_lo[t], it))
                    for w, b, c in ((0, g, c_gate), (1, u, c_up)):
                        for k in range(KD):
                            if t == 0 and w == 0 and len(ready) == KD:
                                need(pe, ready[max(k, 1)])
                            i = mm3(b[:, 0:S], (hv[:, w, k, :], lv[:, w, k, :]), (xTh[:, k, :], xTl[:, k, :]), k == 0, k == KD - 1)
                        i.then_inc(c.sem, 1)
                    act.wait_ge(c_gate.sem, at(c_gate, it * 2 + t + 1))
                    if convolved:
                        tap_at = (lambda tap: parc[:, tap, bass.ds(it * 2 + t, 1)])
                        act.activation(conv[:, t, :], g[:, 0:S], ACT.Identity, scale=tap_at(2), bias=tap_at(3)).then_inc(c_conv.sem, 1)
                        for tap in (1, 0):
                            lag = 2 - tap
                            cs = conv[:, t, lag:S]
                            dve.wait_ge(c_conv.sem, at(c_conv, (it * 2 + t) * 3 + lag))
                            dve.scalar_tensor_tensor(out=cs, in0=g[:, 0:S - lag], scalar=tap_at(tap), in1=cs,
                                                     op0=ALU.mult, op1=ALU.add).then_inc(c_conv.sem, 1)
                        act.wait_ge(c_conv.sem, at(c_conv, (it * 2 + t) * 3 + 3))
                        act.activation(nonlin[:, t, :], conv[:, t, :], ACT.Gelu_apprx_tanh).then_inc(c_gelu.sem, 1)
                    else:
                        act.activation(nonlin[:, t, :], g[:, 0:S], ACT.Silu).then_inc(c_gelu.sem, 1)
                    dve.wait_ge(c_gelu.sem, at(c_gelu, it * 2 + t + 1))
                    dve.wait_ge(c_up.sem, at(c_up, it * 2 + t + 1))
                    dve.scalar_tensor_tensor(out=act32[:, t, :], in0=nonlin[:, t, :], scalar=1.0 if convolved else 0.5,
                                             in1=u[:, 0:S], op0=ALU.mult, op1=ALU.mult).then_inc(c_prod.sem, 1)
                    act.wait_ge(c_prod.sem, at(c_prod, it * 2 + t + 1))
                    act.activation(actTh[:, t, :], act32[:, t, :], ACT.Copy).then_inc(c_ahi.sem, 1)
                    dve.wait_ge(c_ahi.sem, at(c_ahi, it * 2 + t + 1))
                    dve.tensor_tensor(actTl[:, t, :], act32[:, t, :], actTh[:, t, :].bitcast(F32), ALU.subtract).then_inc(c_alo.sem, 1)
                    if t < ahead:
                        split_next(it, t, "gu")
                for t in range(here):
                    pe.wait_ge(c_alo.sem, at(c_alo, it * 2 + t + 1))
                    pe.wait_ge(c_dn_lo[t].sem, at(c_dn_lo[t], it))
                    for m in range(M):
                        for h in range(2):
                            hs = slice(h * HALF, (h + 1) * HALF)
                            ts = slice(m * P, (m + 1) * P)
                            i = mm3(bank[2 * m + h][:, :], (actTh[:, t, ts], actTl[:, t, ts]), (hi_dn[t][:, hs], lo_dn[t][:, hs]),
                                    False, last and t == here - 1, skip_group_check=True)
                        if last and t == here - 1:
                            summed.append(did(pe, i))
                    if not last:
                        i.then_inc(c_down.sem, 1)
                for t in range(ahead):
                    split_next(it, t, "dn")

            act.preload_act_table(ACT.Gelu_apprx_tanh if convolved else ACT.Silu)
            with nc.Fori(0, tiles // 2 - 1) as it:
                turn(it, 2, 2)
            turn(tiles // 2 - 1, 2, tiles % 2, tiles % 2 == 0)
            if tiles % 2:
                turn(tiles // 2, 1, 0, True)
            act.preload_act_table(ACT.Sqrt)
            for t in range(2):
                uses = (tiles + 1 - t) // 2 - 1
                for cs, per in ((c_gu, 32), (c_dn, 16), (c_gu_hi, 1), (c_dn_hi, 1), (c_gu_lo, 1), (c_dn_lo, 1)):
                    cs[t].n += per * uses
            for c, per in ((c_gate, 1), (c_up, 1), (c_gelu, 1), (c_prod, 1), (c_ahi, 1), (c_alo, 1), (c_conv, 3 if convolved else 0)):
                c.n += per * tiles
            c_down.n += tiles - (tiles % 2 or 2)
            t = summed[-1]
            ring_state.update(next=0, staged_free=[[(c_gu_lo[i], c_gu_lo[i].n)] for i in range(2)], split_free=[[t], [t]],
                              dn_staged_free=[[(c_dn_lo[i], c_dn_lo[i].n)] for i in range(2)], dn_split_free=[[t], [t]])
            return summed

        def layer_vectors(l):
            for name, width in (("mla_q_norm_2", 256), ("mla_kv_norm_2", 128), ("ax_q_norm_2", 64), ("ax_k_norm_2", 64),
                                ("diff_subln_2", 64), ("win_sink_2", 4)):
                c_gain2.tick(sp.dma_start(gv[name], all_partitions(A[name][l], width)), 16)
            c_gain2.tick(sp.dma_start(gv["lam"], all_partitions(A["diff_lambda_2"][l].rearrange("a b -> (a b)"), 128)), 16)
            c_gain2.tick(sp.dma_start(gv["init"], all_partitions(C["lam_init"][l], 2)), 16)
            c_row2.tick(sp.dma_start(rows[0:24, :], A["ln_g_2"][l].rearrange("a (k p) -> (a k) p", p=P)), 16)
            c_row2.tick(sp.dma_start(rows[24:48, :], A["ln_b_2"][l].rearrange("a (k p) -> (a k) p", p=P)), 16)
            in_flight.extend([(c_gain2, c_gain2.n), (c_row2, c_row2.n)])

        def swiglu_weights(l, i):
            wgu, wd = A["ffn_w_gu_2"][l, i], A["ffn_w_down_2"][l, i]
            return (lambda j: wgu[:, bass.ds(j * P, P)], lambda j: wgu[:, bass.ds(j * P + DFF2, P)],
                    lambda j: wd[bass.ds(j * P, P), :])

        def layer(l):
            update_x()
            ffn_ahead_rest()
            t = did(pe, pe.transpose(bank[4][:, 0:48], rows[0:48, :], ident[0:48, 0:48]))
            need(dve, t)
            ln_ok = did(dve, dve.tensor_copy(lnT[:, :, :].rearrange("p a b -> p (a b)"), bank[4][:, 0:48]))
            need(act, ln_ok)

            def ln_rows(i, free):
                need(sp, *free)
                c_ln2.tick(sp.dma_start(gb[:, 0, :], all_partitions(A["ln_g_2"][l, i], D)), 16)
                return c_ln2.tick(sp.dma_start(gb[:, 1, :], all_partitions(A["ln_b_2"][l, i], D)), 16)

            gb_in = ln_rows(0, x_ok)
            summed = ffn(*swiglu_weights(l, 0), FT2, [ln_ok], False)
            W2 = A["w_in_2"][l]
            starts = list(range(0, IN2, WCOLS))

            def w_in_chunk(c, **kw):
                return prepare(W2[:, starts[c]:min(starts[c] + WCOLS, IN2)], min(WCOLS, IN2 - starts[c]), **kw)

            prepared = [w_in_chunk(0, low_by=pool)]
            done = norm(summed, ALPHA, EPS2, True, lambda k: lnT[:, 0, k:k + 1], lambda k: lnT[:, 3, k:k + 1], token_gain=gb_in)
            prepared.append(w_in_chunk(1))

            freed = [[done[0]], [done[0]]]
            chunk_ok = []
            W2o = A["w_out_2"][l]
            wuq3 = st_dn[0][:, 0:768].rearrange("p (k n) -> p k n", k=2)
            wukv2 = st_dn[1][:, 0:HALF]
            def project(ci):
                c0 = starts[ci]
                width = min(WCOLS, IN2 - c0)
                b0 = 2 * (ci % 2)
                t = token_chunk(prepared[ci], lambda m: bank[b0 + m][:, 0:width], freed[ci % 2],
                                done if ci == 0 else None)
                need(dve, t[0])
                need(act, t[1])
                k1 = did(dve, dve.tensor_copy(proj[:, 0, c0:c0 + width], bank[b0][:, 0:width]))
                k2_ = did(act, act.activation(proj[:, 1, c0:c0 + width], bank[b0 + 1][:, 0:width], ACT.Copy))
                freed[ci % 2] = [k1, k2_]
                chunk_ok.extend([k1, k2_])
                if ci + 2 < len(starts):
                    prepared.append(w_in_chunk(ci + 2))

            lp = gv["lam"].rearrange("p (a b) -> p a b", a=4)
            lsum, lexp, lam = small[:, 0, 0:2], small[:, 1, 0:2], small[:, 2, 0:1]
            k = did(dve, dve.tensor_tensor(sq2[:, 0:64].rearrange("p (a b) -> p a b", a=2), lp[:, 0:4:2, :], lp[:, 1:4:2, :], ALU.mult))
            need(dve, k)
            k = did(dve, dve.tensor_reduce(lsum, sq2[:, 0:64].rearrange("p (a b) -> p a b", a=2), X, ALU.add))
            need(act, k)
            k = did(act, act.activation(lexp, lsum, ACT.Exp))
            need(dve, k)
            k = did(dve, dve.tensor_tensor(lam, lexp[:, 0:1], lexp[:, 1:2], ALU.subtract))
            need(dve, k)
            lam_ok = did(dve, dve.tensor_tensor(lam, lam, gv["init"][:, 0:1], ALU.add))
            nsink = small[:, 3, 0:4]
            sink_ok = did(dve, dve.tensor_scalar(nsink, gv["win_sink_2"], -1.0, None, ALU.mult))

            mq = n[:, :, 0:384].rearrange("p m (h d) -> p m h d", d=96)
            mkk = n[:, :, 384:768].rearrange("p m (h d) -> p m h d", d=96)
            mv_ = n[:, :, 768:1024].rearrange("p m (h d) -> p m h d", d=HD)
            hr = hq[:, :, 8:16]
            mark = {}
            tr_free = {6: (done[-1],), 7: (done[-1],)}

            def sums_of_squares():
                need(act, *chunk_ok)
                for m in range(M):
                    did(act, act.activation(cn[m][:, 0:256], proj[:, m, MLA_Q:MLA_Q + 256], ACT.Square, accum_out=hq[:, m, 0:1]))
                    k = did(act, act.activation(cn[m][:, 256:384], proj[:, m, MLA_KV:MLA_KV + 128], ACT.Square, accum_out=hq[:, m, 1:2]))
                mark["sq"] = k
                for m in range(M):
                    need(dve, (c_dve, c_dve.n))
                    k = did(dve, dve.tensor_tensor(sq2, proj[:, m, AX_Q:AX_Q + 384], proj[:, m, AX_Q:AX_Q + 384], ALU.mult))
                    need(dve, k)
                    k = did(dve, dve.tensor_reduce(hq[:, m, 2:8], sq2.rearrange("p (h d) -> p h d", d=HD), X, ALU.add))

            def rstd():
                need(dve, mark["sq"], (c_dve, c_dve.n))
                did(dve, dve.tensor_scalar(hr[:, :, 0:1], hq[:, :, 0:1], 1.0 / 256, EPS2, ALU.mult, ALU.add))
                did(dve, dve.tensor_scalar(hr[:, :, 1:2], hq[:, :, 1:2], 1.0 / 128, EPS2, ALU.mult, ALU.add))
                k = did(dve, dve.tensor_scalar(hr[:, :, 2:8], hq[:, :, 2:8], 1.0 / HD, EPS2, ALU.mult, ALU.add))
                need(act, k)
                mark["sd"] = did(act, act.activation(hr, hr, ACT.Sqrt))

            def latents():
                need(dve, mark["sd"])
                k = did(dve, dve.reciprocal(hr, hr))
                need(dve, k)
                for m in range(M):
                    did(dve, dve.scalar_tensor_tensor(out=cn[m][:, 0:256], in0=proj[:, m, MLA_Q:MLA_Q + 256], scalar=hr[:, m, 0:1],
                                                      in1=gv["mla_q_norm_2"], op0=ALU.mult, op1=ALU.mult))
                    mark["cn"] = did(dve, dve.scalar_tensor_tensor(out=cn[m][:, 256:384], in0=proj[:, m, MLA_KV:MLA_KV + 128],
                                                                   scalar=hr[:, m, 1:2], in1=gv["mla_kv_norm_2"], op0=ALU.mult, op1=ALU.mult))

            def axial_gains():
                need(pool, *chunk_ok, mark["cn"])
                for m in range(M):
                    axh = proj[:, m, AX_Q:AX_Q + 384].rearrange("p (h d) -> p h d", d=HD)
                    k = did(pool, pool.tensor_tensor(axh, axh, bc(hr[:, m, 2:8], 2, HD), ALU.mult))
                    need(pool, k)
                    did(pool, pool.tensor_tensor(axh[:, 0:4], axh[:, 0:4], bc(gv["ax_q_norm_2"], 1, 4), ALU.mult))
                    did(pool, pool.tensor_tensor(axh[:, 4:6], axh[:, 4:6], bc(gv["ax_k_norm_2"], 1, 2), ALU.mult))

            def latents_T():
                for j in range(3):
                    b = 6 + j % 2
                    need(pe, mark["cn"], *tr_free[b])
                    for m in range(M):
                        i = pe.transpose(bank[b][:, m * P:(m + 1) * P], cn[m][:, j * P:(j + 1) * P], ident[:, :])
                    t = did(pe, i)
                    need(act, t)
                    mark["cT"] = did(act, act.activation(cT[:, j, :], bank[b][:, 0:S], ACT.Copy))
                    tr_free[b] = (mark["cT"],)

            def up_projections(m):
                need(pe, mark["cT"], uq_in, ukv_in, *tr_free[6], *tr_free[7])
                for k_ in range(2):
                    pe.matmul(bank[6][:, 0:384], cT[:, k_, m * P:(m + 1) * P], wuq3[:, k_, :], start=(k_ == 0), stop=(k_ == 1))
                t = did(pe, pe.matmul(bank[7][:, :], cT[:, 2, m * P:(m + 1) * P], wukv2, start=True, stop=True))
                ring_state["dn_staged_free"] = [[t], [t]]
                need(act, t, *x_ok)
                k = did(act, act.activation(n[:, m, 0:384], bank[6][:, 0:384], ACT.Copy))
                tr_free[6] = (k,)
                kv4 = bank[7][:, :].rearrange("p (h d) -> p h d", d=128)
                did(act, act.activation(mkk[:, m, :, 0:NOPE], kv4[:, :, 0:NOPE], ACT.Copy))
                k = did(act, act.activation(mv_[:, m, :, :], kv4[:, :, NOPE:128], ACT.Copy))
                tr_free[7] = (k,)
                mark["up"] = k

            def rotate(m, a, b_, cosv, sinv, heads):
                t1, t2 = (rt[:, m, z, 0:16 * heads].rearrange("p (h d) -> p h d", d=16) for z in range(2))
                cv, sv = bc(cosv, 1, heads), bc(sinv, 1, heads)
                need(pool, (c_pool, c_pool.n))
                did(pool, pool.tensor_tensor(t1, a, sv, ALU.mult))
                k = did(pool, pool.tensor_tensor(t2, b_, sv, ALU.mult))
                need(pool, k)
                did(pool, pool.tensor_tensor(a, a, cv, ALU.mult))
                k = did(pool, pool.tensor_tensor(b_, b_, cv, ALU.mult))
                need(pool, k)
                did(pool, pool.tensor_tensor(a, a, t2, ALU.subtract))
                return did(pool, pool.tensor_tensor(b_, b_, t1, ALU.add))

            def rotations(m):
                rp = rope[:, m, :].rearrange("p (a b) -> p a b", a=6)
                axh = proj[:, m, AX_Q:AX_Q + 384].rearrange("p (h d) -> p h d", d=HD)
                for hf in range(2):
                    mark["ax"] = rotate(m, axh[:, :, 32 * hf:32 * hf + 16], axh[:, :, 32 * hf + 16:32 * hf + 32],
                                        rp[:, 2 + hf, :], rp[:, 4 + hf, :], 6)
                kr = proj[:, m, MLA_KR:MLA_KR + 32].rearrange("p (a b) -> p a b", a=2)
                k = rotate(m, kr[:, 0:1, :], kr[:, 1:2, :], rp[:, 0, :], rp[:, 1, :], 1)
                need(pool, k, mark["up"])
                did(pool, pool.tensor_copy(mkk[:, m, :, 64:96], bc(proj[:, m, MLA_KR:MLA_KR + 32], 1, 4)))
                mark["mla"] = rotate(m, mq[:, m, :, 64:80], mq[:, m, :, 80:96], rp[:, 0, :], rp[:, 1, :], 4)

            pieces = [sums_of_squares, rstd, latents, axial_gains, latents_T, lambda: up_projections(0), lambda: up_projections(1),
                      lambda: rotations(0), lambda: rotations(1)]

            sets = [(qT, kT), (qT2, kT2)]

            def views(kind):
                if kind == "win":
                    return ([(lambda m, h=h: proj[:, m, WIN_Q + h * HD:WIN_Q + (h + 1) * HD]) for h in range(4)],
                            [(lambda m, h=h: proj[:, m, WIN_K + h * HD:WIN_K + (h + 1) * HD]) for h in range(2)], HD)
                if kind == "mla":
                    return ([(lambda m, h=h: mq[:, m, h, :]) for h in range(4)], [(lambda m, h=h: mkk[:, m, h, :]) for h in range(4)], 96)
                if kind == "ax":
                    return ([(lambda m, h=h: proj[:, m, AX_Q + h * HD:AX_Q + (h + 1) * HD]) for h in range(4)],
                            [(lambda m, h=h: proj[:, m, AX_Q + 256 + h * HD:AX_Q + 256 + (h + 1) * HD]) for h in range(2)], HD)
                return ([(lambda m, h=h: proj[:, m, DF_Q + h * HD:DF_Q + (h + 1) * HD]) for h in range(4)],
                        [(lambda m, h=h: proj[:, m, DF_K + h * HD:DF_K + (h + 1) * HD]) for h in range(4)], HD)

            kinds = ["win", "dif", "ax", "mla"]
            tr_n = [0]
            set_reads = [(), ()]

            def transposes(kind):
                si = kinds.index(kind) % 2
                q_, k_ = sets[si]
                qv, kv, dim = views(kind)
                need(pe, *(chunk_ok if kind in ("win", "dif") else [mark["ax"]] if kind == "ax" else [mark["mla"], mark["up"]]))
                for dst, vs in ((q_, qv), (k_, kv)):
                    for p0 in range(0, len(vs), 2):
                        b = 6 + tr_n[0] % 2
                        tr_n[0] += 1
                        need(pe, *tr_free[b])
                        for z in range(2):
                            for m in range(M):
                                i = pe.transpose(bank[b][0:dim, (2 * z + m) * P:(2 * z + m + 1) * P], vs[p0 + z](m), ident[:, :])
                        t = did(pe, i)
                        need(act, t, *set_reads[si])
                        e = did(act, act.activation(dst[0:dim, p0:p0 + 2, :], bank[b][0:dim, :].rearrange("p (a b) -> p a b", a=2), ACT.Copy))
                        tr_free[b] = (e,)
                ready_t[kind] = e

            ready_t = {}
            units = [(kind, m, pr) for kind in kinds for pr in range(4 if kind == "dif" else 2) for m in range(M)]
            out_col = {"win": 0, "mla": 256, "ax": 512, "dif": 768}
            v_of = {"win": (proj, WIN_V), "mla": (n, 768), "ax": (proj, AX_V), "dif": (proj, DF_V)}
            om = [gbo[:, m, :] for m in range(M)]
            st = {}
            bank_s, bank_t, bank_o = {0: (), 1: ()}, {2: (), 3: ()}, {4: (), 5: ()}
            out_ahead = []
            for ci in range(len(starts)):
                project(ci)
                if ci == 3:
                    transposes("win")
                if ci >= len(starts) - 2:
                    c = len(out_ahead) * WCOLS
                    out_ahead.append(prepare(W2o[:, c:c + WCOLS], low_by=pool))
            for d_ in (bank_s, bank_t, bank_o):
                for b in d_:
                    d_[b] = (*freed[0], *freed[1], ln_ok)
            need(sp, *ring_state["dn_staged_free"][0], *ring_state["dn_staged_free"][1])
            uq_in = c_uq.tick(sp.dma_start(wuq3, A["mla_w_uq_2"][l].rearrange("(k p) n -> p k n", p=P)), 16)
            ukv_in = c_uq.tick(sp.dma_start(wukv2, A["mla_w_ukv_2"][l]), 16)
            gb_in = ln_rows(1, x_ok)
            pb_read, ptb_read = [(), ()], [(), ()]
            rr_done, s_done = {}, {}

            def logits(u):
                kind, m, pr = units[u]
                si = kinds.index(kind) % 2
                q_, k_ = sets[si]
                i2 = u % 2
                need(pe, ready_t[kind], *bank_s[i2])
                for z in range(2):
                    if kind == "dif":
                        r0, qh, kh, dim = 32 * z, pr, pr, 32
                    else:
                        r0, qh, dim = 0, 2 * pr + z, (96 if kind == "mla" else HD)
                        kh = qh if kind == "mla" else pr
                    i = pe.matmul(bank[i2][:, z * S:(z + 1) * S], q_[r0:r0 + dim, qh, m * P:(m + 1) * P], k_[r0:r0 + dim, kh, :],
                                  start=True, stop=True)
                    if kind == "dif" and z == 0:
                        need(pe, did(pe, i))
                t = did(pe, i)
                if u + 1 == len(units) or units[u + 1][0] != kind:
                    set_reads[si] = (t,)
                s_done[u] = t

            def softmax(u):
                kind, m, pr = units[u]
                i2 = u % 2
                t = s_done[u]
                s3 = bank[i2][:, :].rearrange("p (a b) -> p a b", a=2)
                p3 = pb[:, i2, :].rearrange("p (a b) -> p a b", a=2)
                nm, sm = small[:, 4 + i2, 0:2], small[:, 6 + i2, 0:2]
                scale = {"win": 1.0, "dif": 1.0, "ax": SCALE_C, "mla": SCALE_B}[kind]
                need(dve, t, *pb_read[i2])
                if kind in ("win", "dif"):
                    bias = win_bias[:, m, 2 * pr:2 * pr + 2, :] if kind == "win" else bc(dif_bias[:, m, pr, :], 1, 2)
                    k = did(dve, dve.scalar_tensor_tensor(out=p3, in0=s3, scalar=SCALE_A if kind == "win" else SCALE_D, in1=bias,
                                                          op0=ALU.mult, op1=ALU.add))
                    bank_s[i2] = (k,)
                    src = p3
                    need(dve, k)
                else:
                    src = s3
                k = did(dve, dve.tensor_reduce(nm, src, X, ALU.max, negate=True))
                need(dve, k)
                if kind == "win":
                    k = did(dve, dve.tensor_tensor(nm, nm, nsink[:, 2 * pr:2 * pr + 2], ALU.min))
                elif scale != 1.0:
                    k = did(dve, dve.tensor_scalar(nm, nm, scale, None, ALU.mult))
                need(act, k, *pb_read[i2])
                if kind == "win":
                    ex = small[:, 10 + i2, 0:2]
                    for z in range(2):
                        did(act, act.activation(ex[:, z:z + 1], nm[:, z:z + 1], ACT.Exp, bias=gv["win_sink_2"][:, 2 * pr + z:2 * pr + z + 1]))
                for z in range(2):
                    k = did(act, act.activation(p3[:, z, :], src[:, z, :], ACT.Exp, scale=scale, bias=nm[:, z:z + 1], accum_out=sm[:, z:z + 1]))
                if kind in ("ax", "mla"):
                    bank_s[i2] = (k,)
                st[u] = k

            def reciprocals(u):
                kind, m, pr = units[u]
                i2 = u % 2
                p3 = pb[:, i2, :].rearrange("p (a b) -> p a b", a=2)
                sm, rr = small[:, 6 + i2, 0:2], small[:, 8 + i2, 0:2]
                k = st[u]
                need(dve, k, *bank_o[4 + i2])
                if kind == "win":
                    k2_ = did(dve, dve.tensor_tensor(sm, sm, small[:, 10 + i2, 0:2], ALU.add))
                    need(dve, k2_)
                k2_ = rr_done[i2] = did(dve, dve.reciprocal(rr, sm))
                if kind == "dif":
                    need(dve, k2_)
                    k = did(dve, dve.tensor_scalar(rr[:, 1:2], rr[:, 1:2], lam, None, ALU.mult))
                    need(dve, k)
                    k = did(dve, dve.tensor_scalar(p3[:, 1, :], p3[:, 1, :], rr[:, 1:2], None, ALU.mult))
                    need(dve, k)
                    k = did(dve, dve.scalar_tensor_tensor(out=p3[:, 0, :], in0=p3[:, 0, :], scalar=rr[:, 0:1], in1=p3[:, 1, :],
                                                          op0=ALU.mult, op1=ALU.subtract))
                st[u] = k

            def probabilities(u):
                kind, m, pr = units[u]
                i2 = u % 2
                maps = 1 if kind == "dif" else 2
                b = 2 + i2
                need(pe, st[u], *bank_t[b])
                for z in range(maps):
                    for kt in range(M):
                        i = pe.transpose(bank[b][:, (2 * z + kt) * P:(2 * z + kt + 1) * P], pb[:, i2, z * S + kt * P:z * S + (kt + 1) * P], ident[:, :])
                t = did(pe, i)
                pb_read[i2] = (t,)
                need(act, t, *ptb_read[i2])
                w = 2 * maps * P
                k = did(act, act.activation(ptb[:, i2, 0:w], bank[b][:, 0:w], ACT.Copy))
                bank_t[b] = (k,)
                st[u] = k

            def weighted(u):
                kind, m, pr = units[u]
                i2 = u % 2
                maps = 1 if kind == "dif" else 2
                b = 4 + i2
                need(pe, st[u], *bank_o[b])
                vb, v0 = v_of[kind]
                for z in range(maps):
                    vh = {"win": pr, "ax": pr, "mla": 2 * pr + z, "dif": pr}[kind]
                    for kt in range(M):
                        i = pe.matmul(bank[b][:, z * HD:(z + 1) * HD], ptb[:, i2, (2 * z + kt) * P:(2 * z + kt + 1) * P],
                                      vb[:, kt, v0 + vh * HD:v0 + (vh + 1) * HD], start=(kt == 0), stop=(kt == 1))
                t = did(pe, i)
                ptb_read[i2] = (t,)
                need(dve, t)
                if kind == "dif":
                    o0 = out_col[kind] + pr * HD
                    k = did(dve, dve.tensor_copy(om[m][:, o0:o0 + HD], bank[b][:, 0:HD]))
                else:
                    o0 = out_col[kind] + 2 * pr * HD
                    rr = small[:, 8 + i2, 0:2]
                    need(dve, rr_done[i2])
                    k = did(dve, dve.tensor_tensor(om[m][:, o0:o0 + P].rearrange("p (a b) -> p a b", a=2),
                                                   bank[b][:, 0:P].rearrange("p (a b) -> p a b", a=2), bc(rr, 2, HD), ALU.mult))
                bank_o[b] = (k,)
                return k

            need(dve, lam_ok, sink_ok)
            need(act, sink_ok)
            logits(0)
            for u in range(len(units) + 2):
                if u + 1 < len(units):
                    logits(u + 1)
                if u < len(units):
                    softmax(u)
                if 1 <= u <= len(units):
                    reciprocals(u - 1)
                if 2 <= u:
                    o_ok = weighted(u - 2)
                if 1 <= u <= len(units):
                    probabilities(u - 1)
                if u < len(units):
                    if u + 3 < len(units) and units[u + 3][0] not in ready_t:
                        while pieces and units[u + 3][0] in ("ax", "mla"):
                            pieces.pop(0)()
                        transposes(units[u + 3][0])
                if pieces:
                    pieces.pop(0)()
            need(dve, o_ok)
            for m in range(M):
                d3 = om[m][:, 768:1024]
                need(dve, (c_dve, c_dve.n))
                k = did(dve, dve.tensor_tensor(sq2[:, 0:256], d3, d3, ALU.mult))
                need(dve, k)
                k = did(dve, dve.tensor_reduce(hq[:, m, 0:4], sq2[:, 0:256].rearrange("p (h d) -> p h d", d=HD), X, ALU.add))
            need(dve, k)
            k = did(dve, dve.tensor_scalar(hq[:, :, 0:4], hq[:, :, 0:4], 1.0 / HD, EPS2, ALU.mult, ALU.add))
            need(act, k)
            k = did(act, act.activation(hq[:, :, 0:4], hq[:, :, 0:4], ACT.Sqrt))
            need(dve, k)
            k = did(dve, dve.reciprocal(hq[:, :, 0:4], hq[:, :, 0:4]))
            need(dve, k)
            k = did(dve, dve.tensor_scalar(hq[:, :, 0:4], hq[:, :, 0:4], gv["init"][:, 1:2], None, ALU.mult))
            need(dve, k)
            for m in range(M):
                d3 = om[m][:, 768:1024].rearrange("p (h d) -> p h d", d=HD)
                k = did(dve, dve.tensor_tensor(d3, d3, bc(hq[:, m, 0:4], 2, HD), ALU.mult))
                need(dve, k)
                k = did(dve, dve.tensor_tensor(d3, d3, bc(gv["diff_subln_2"], 1, 4), ALU.mult))
            ct = transpose_tiles(gbo, None, None, [k], extra=(*tr_free[6], *tr_free[7]))
            summed = out_product(W2o, out_ahead, [*[z for d_ in (bank_s, bank_t) for v in d_.values() for z in v]], ct)
            ffn_ahead(*swiglu_weights(l, 1))
            done = norm(summed, ALPHA, EPS2, True, lambda k: lnT[:, 1, k:k + 1], lambda k: lnT[:, 4, k:k + 1], token_gain=gb_in)
            ffn_ahead_rest()
            need(sp, *ct)
            layer_vectors((l + 1) % LAYERS)
            in_flight.append(ln_rows(2, x_ok))
            summed = ffn(*swiglu_weights(l, 1), FT2, done, False)
            ffn_ahead(*swiglu_weights((l + 1) % LAYERS, 0))
            norm(summed, ALPHA, EPS2, True, lambda k: lnT[:, 2, k:k + 1], lambda k: lnT[:, 5, k:k + 1])
            land()

        c = Carve()
        o_tok = n
        ig = proj[:, :, 0:D]
        gq, gk, lf = c(3, S), c(3, S), c(3, S)
        cum = c(2, 3, S)
        dd, ee = c(3 * S), c(3 * S)
        qs = c(2, 3, S)
        ks = c(2, 3, S)
        zf = ks[:, 0, 0:2, :]
        keep_at = c.at
        scoreT = c(3, 8, P)
        keep = big[:, keep_at:keep_at + 2 * 3 * S].rearrange("p (a b c) -> p a b c", a=2, b=3)
        masks = c(7, P)
        gain_bc = proj[:, 0, 1552:2064]
        hsum, hrs = c(M, 8), c(M, 8)
        sil = n[:, :, HALF:D]
        spl, lb, oml, lbt = c(4), c(2), c(2), c(2)
        lr, wup = c(S), c(P)
        xpv = proj[:, :, D:D + 2 * (S + 4)].rearrange("p m (b s) -> p m b s", b=2)

        def xp(b):
            return xpv[:, b // 2, b % 2, :]

        g4 = gbo[:, :, :].rearrange("p a (b c) -> p (a b) c", c=S)
        b4 = gb[:, :, :].rearrange("p a (b c) -> p (a b) c", c=S)
        gbt, ra, xc, gi = g4[:, 0:4, :], g4[:, 4:8, :], b4[:, 0:4, :], b4[:, 4:8, :]
        wab = [t_[:, :, :].rearrange("p a b -> p (a b)").rearrange("p (b j) -> p b j", b=4) for t_ in (nonlin, act32)]

        W = A["w_in"][0]
        x_in = [c_out.tick(sp.dma_start(x[:, m, :], A["x"][0, m * P:(m + 1) * P, :]), 16) for m in range(M)]
        ident_in = c_ident.tick(sp.dma_start(ident[:, :], C["ident"]), 16)

        def scatter_rows(dst_rows, at, dram1d, count, by=sp):
            (c_row if by is sp else c_row2).tick(by.dma_start(dst_rows[at:at + count, :], dram1d.rearrange("(a n) -> a n", n=P)), 16)

        PARS = [("norm_mix", 8), ("norm_ffn", 8), ("norm_final", 8), ("rg_b_a", 4), ("rg_b_x", 4), ("rg_lambda", 4),
                ("rg_conv_w", 16), ("rg_conv_b", 4), ("gla_b_gate", 1), ("hgrn_lower_bounds", 2)]
        off, at = {}, 0
        for name, count in PARS:
            v = A[name]
            v = v if len(v.shape) == 1 else (v.rearrange("a n -> (a n)") if len(v.shape) == 2 else v.rearrange("a b n -> (a b n)"))
            scatter_rows(rows, at, v, count, act if name == "norm_mix" else sp)
            if name == "norm_mix":
                prepared = [prepare(W[:, A_Q:A_Q + 256], low_by=pool)]
            off[name] = at
            at += count
        n_par = at
        scatter_rows(rows2, 0, A["ffn_conv_w"].rearrange("a b n -> (a b n)"), 3 * FT1)
        scatter_rows(rows2, 3 * FT1, A["ffn_conv_b"].rearrange("a n -> (a n)"), FT1)
        rows_in = (c_row, c_row.n)
        for w_ in wab:
            zw = did(pool, pool.memset(w_, 0.0))
        k0 = did(pool, pool.memset(zeros[:, :], 0.0))
        zx = did(pool, pool.memset(xpv, 0.0))

        need(pe, ident_in, (c_row2, c_row2.n))
        t = did(pe, pe.transpose(bank[0][:, 0:8], rows[0:8, :], ident[0:8, 0:8]))
        need(act, t)
        par_ok = did(act, act.activation(par1[:, 0:8], bank[0][:, 0:8], ACT.Copy))

        def col(name, i=0, count=1):
            return par1[:, off[name] + i:off[name] + i + count]

        act.preload_act_table(ACT.Sqrt)
        need(act, par_ok, *x_in)
        need(dve, *x_in)
        hT_ok = norm([], 1.0, EPS1, False, lambda k: col("norm_mix", k), None)
        prepared.append(prepare(W[:, A_F:A_F + 256]))
        need(pe, rows_in, par_ok)
        pe.transpose(bank[0][:, 0:n_par], rows[0:n_par, :], ident[0:n_par, 0:n_par])
        t = did(pe, pe.transpose(bank[0][:, P:P + 4 * FT1], rows2[0:4 * FT1, :], ident[0:4 * FT1, 0:4 * FT1]))
        need(dve, t)
        did(dve, dve.tensor_copy(par1[:, 8:n_par], bank[0][:, 8:n_par]))
        par_ok = did(dve, dve.tensor_copy(parc[:, :, :].rearrange("p a b -> p (a b)"), bank[0][:, P:P + 4 * FT1]))
        need(act, par_ok)

        need(sp, zw)
        for g, name in enumerate(("rg_w_a", "rg_w_x")):
            for two in range(2):
                c_lng.tick(sp.dma_start(wab[g][two * 64:two * 64 + 64, :, two * 64:two * 64 + 64],
                                        A[name][0].rearrange("(b t) i j -> t i b j", t=2)[two]), 16)
        w_in_m = c_lng.tick(sp.dma_start(wup[0:LR_RANK, :], A["gla_w_gate_up"][0]), 16)
        c_par.tick(sp.dma_start(masks, C["masks"].bitcast(F32)), 16)
        c_par.tick(sp.dma_start(keep, C["keep"]), 16)
        c_par.tick(sp.dma_start(gain_bc[:, 0:256], all_partitions(A["hgrn_norm"][0], 256)), 16)
        par_in = c_par.tick(sp.dma_start(gain_bc[:, 256:512], all_partitions(A["gla_norm"][0], 256)), 16)

        need(dve, par_ok)
        e2 = did(dve, dve.tensor_tensor(lbt, col("hgrn_lower_bounds", 0, 2), col("hgrn_lower_bounds", 0, 2), ALU.subtract))
        need(act, e2)
        e1 = did(act, act.activation(spl, col("rg_lambda", 0, 4), ACT.Exp, scale=-1.0))
        e2 = did(act, act.activation(lb, lbt, ACT.Exp))
        need(act, e1)
        e1 = did(act, act.activation(spl, spl, ACT.Ln, bias=1.0))
        need(act, e1)
        spl_ok = did(act, act.activation(spl, spl, ACT.Copy, scale=-8.0))
        need(dve, e2)
        e2 = did(dve, dve.reciprocal(lbt, lb))
        need(dve, e2)
        e2 = did(dve, dve.tensor_tensor(lbt, lb, lbt, ALU.mult))
        need(dve, e2)
        e2 = did(dve, dve.tensor_tensor(lb, lbt, lbt, ALU.subtract))
        need(dve, e2)
        lb_ok = did(dve, dve.tensor_scalar(oml, lb, -1.0, 1.0, ALU.mult, ALU.add))

        t_freed = {}

        def t_block(chunk, c0, width, b, evacuate):
            slot, split, _, hv, lv = chunk
            need(pe, split)
            need(pe, *t_freed.get(b, ()))
            for k in range(KD):
                i = mm3(bank[b][:, 0:S], (hv[:, k, c0:c0 + P], lv[:, k, c0:c0 + P]), (xTh[:, k, :], xTl[:, k, :]), k == 0, k == KD - 1)
            t = did(pe, i)
            ring_state["split_free"][slot] = [t]
            e = evacuate(bank[b][0:width, 0:S], t)
            t_freed[b] = (e,)
            return e

        def copy_by(eng, dst, scale=None):
            def go(src, t):
                need(eng, t)
                if eng is dve:
                    return did(dve, dve.tensor_copy(dst, src) if scale is None else dve.tensor_scalar(dst, src, scale, None, ALU.mult))
                return did(act, act.activation(dst, src, ACT.Copy) if scale is None else act.activation(dst, src, ACT.Copy, scale=scale))
            return go

        need(pe, *hT_ok)
        q0 = t_block(prepared[0], 0, P, 4, copy_by(dve, gq[:, 0, :]))
        q1 = t_block(prepared[0], P, P, 5, copy_by(act, gq[:, 1, :]))
        prepared.append(prepare(W[:, C_Q:C_Q + 256]))
        f0 = t_block(prepared[1], 0, P, 6, copy_by(dve, zf[:, 0, :]))
        f1 = t_block(prepared[1], P, P, 7, copy_by(act, zf[:, 1, :]))
        prepared.append(prepare(W[:, C_LR:C_LR + LR_RANK], LR_RANK))
        need(act, f0, f1)
        sg = did(act, act.activation(ee[:, 0:512], zf.rearrange("p a b -> p (a b)"), ACT.Sigmoid))
        kg = did(act, act.activation(gk[:, 0:2, :], zf, ACT.Sigmoid, scale=-1.0))
        q2 = t_block(prepared[2], 0, P, 4, copy_by(dve, gq[:, 2, :], 32 ** -0.5))
        k2 = t_block(prepared[2], P, P, 5, copy_by(act, gk[:, 2, :]))
        l0 = t_block(prepared[3], 0, LR_RANK, 6, copy_by(dve, lr[0:LR_RANK, :]))
        need(pe, l0, w_in_m)
        need(pe, *t_freed[7])
        tz = did(pe, pe.matmul(bank[7][:, 0:S], wup[0:LR_RANK, :], lr[0:LR_RANK, :], start=True, stop=True))
        rest = [B_X, B_X + 256, B_G, B_G + 256, A_I, A_G, C_V, C_G]
        prepared = [prepare(W[:, c0:c0 + WCOLS]) for c0 in rest[0:2]]
        need(dve, sg, kg, lb_ok)
        for b in range(2):
            k = did(dve, dve.tensor_scalar(gk[:, b, :], gk[:, b, :], oml[:, b:b + 1], None, ALU.mult))
            k = did(dve, dve.tensor_scalar(lf[:, b, :], ee[:, b * S:(b + 1) * S], oml[:, b:b + 1], lb[:, b:b + 1], ALU.mult, ALU.add))
        need(dve, k)
        k = did(dve, dve.tensor_scalar(lf[:, 0:2, :], lf[:, 0:2, :], F_FLOOR, None, ALU.max))
        z2, a2, z3 = dd[:, 0:S], dd[:, S:2 * S], dd[:, 2 * S:3 * S]
        need(dve, tz)
        kz = did(dve, dve.tensor_scalar(z2, bank[7][:, 0:S], col("gla_b_gate"), None, ALU.add))
        t_freed[7] = (kz,)
        need(act, kz, k)
        ka = did(act, act.activation(a2, z2, ACT.Abs))
        need(act, ka)
        ka = did(act, act.activation(a2, a2, ACT.Exp, scale=-1.0))
        need(act, ka)
        ka = did(act, act.activation(a2, a2, ACT.Ln, bias=1.0))
        kf = did(act, act.activation(lf[:, 0:2, :], lf[:, 0:2, :], ACT.Ln))
        need(dve, kz)
        kz = did(dve, dve.tensor_scalar(z3, z2, 0.0, 1.0 / 16, ALU.min, ALU.mult))
        need(dve, ka, kz)
        k = did(dve, dve.scalar_tensor_tensor(out=lf[:, 2, :], in0=a2, scalar=-1.0 / 16, in1=z3, op0=ALU.mult, op1=ALU.add))
        need(dve, k, kf, par_in)
        for w in range(2):
            k = did(dve, dve.tensor_tensor_scan(cum[:, w].rearrange("p a b -> p (a b)"), keep[:, w].rearrange("p a b -> p (a b)"),
                                                lf.rearrange("p a b -> p (a b)"), 0.0, ALU.mult, ALU.add))
        cum_ok = k
        need(act, zx)

        done_of = {}
        out_ahead = []

        def chunk(j):
            if j < 4:
                for z in range(2):
                    b = 2 * (j % 2) + z
                    done_of[j] = t_block(prepared[j], z * P, P, 6 + z, copy_by(act, xp(b)[:, 3:3 + S] if j < 2 else gbt[:, b, :]))
            else:
                t = token_chunk(prepared[j], lambda m: bank[6 + m][:, 0:WCOLS], [*t_freed[6], *t_freed[7]])
                for m in range(M):
                    need(act, t[m])
                    done_of[j] = did(act, act.activation(ig[:, m, (j - 4) * 256:(j - 3) * 256], bank[6 + m][:, 0:WCOLS], ACT.Copy))
                    t_freed[6 + m] = (done_of[j],)

        def next_chunk(j):
            if j < len(rest):
                prepared.append(prepare(W[:, rest[j]:rest[j] + WCOLS]))
            else:
                c0 = (j - len(rest)) * WCOLS
                out_ahead.append(prepare(A["w_out"][0][:, c0:c0 + WCOLS]))

        rg = {}

        def conv_block(b):
            need(dve, done_of[b // 2])
            k = did(dve, dve.tensor_scalar(xc[:, b, :], xp(b)[:, 3:3 + S], col("rg_conv_w", 12 + b), col("rg_conv_b", b), ALU.mult, ALU.add))
            for tap in range(3):
                need(dve, k)
                k = did(dve, dve.scalar_tensor_tensor(out=xc[:, b, :], in0=xp(b)[:, tap:tap + S], scalar=col("rg_conv_w", 4 * tap + b),
                                                      in1=xc[:, b, :], op0=ALU.mult, op1=ALU.add))
            rg["xc"] = k

        def gates(g, dst, bias):
            for pair in range(2):
                need(pe, rg["xc"], w_in_m, *t_freed[6 + pair])
                for b in (2 * pair, 2 * pair + 1):
                    i = pe.matmul(bank[6 + pair][:, (b % 2) * S:(b % 2 + 1) * S], wab[g][:, b, :], xc[:, b, :], start=True, stop=True)
                t = did(pe, i)
                need(act, t)
                for b in (2 * pair, 2 * pair + 1):
                    k = did(act, act.activation(dst[:, b, :], bank[6 + pair][:, (b % 2) * S:(b % 2 + 1) * S], ACT.Sigmoid, bias=col(bias, b)))
                t_freed[6 + pair] = (k,)
            rg[bias] = k

        aa = xc

        def decay():
            need(pool, rg["rg_b_x"])
            rg["gx"] = did(pool, pool.tensor_tensor(gi, gi, xc, ALU.mult))
            need(act, rg["rg_b_a"], spl_ok, rg["xc"])
            for b in range(4):
                rg["tanh"] = did(act, act.activation(xp(b)[:, 0:S], ra[:, b, :], ACT.Tanh, scale=spl[:, b:b + 1]))
            need(act, rg["gx"])
            for b in range(4):
                k = did(act, act.activation(aa[:, b, :], ra[:, b, :], ACT.Exp, scale=spl[:, b:b + 1]))
            need(act, k)
            rg["a2"] = did(act, act.activation(ra, aa, ACT.Square))

        def remainder():
            need(dve, rg["a2"], rg["tanh"])
            for m in range(M):
                rm = ra[:, 2 * m:2 * m + 2, :]
                k = did(dve, dve.scalar_tensor_tensor(out=rm, in0=rm, scalar=1.0, in1=xpv[:, m, :, 0:S], op0=ALU.add, op1=ALU.mult))
            need(dve, k)
            rg["rem"] = did(dve, dve.tensor_scalar(ra, ra, -1.0, 2.0 ** -116, ALU.mult, ALU.max))

        def roots():
            need(act, rg["rem"])
            rg["root"] = did(act, act.activation(ra, ra, ACT.Sqrt))
            rg["gelu"] = did(act, act.activation(gbt, gbt, ACT.Gelu_apprx_tanh))
            need(pool, rg["root"], rg["gx"])
            rg["u"] = did(pool, pool.tensor_tensor(ra, ra, gi, ALU.mult))

        def recurrence():
            need(dve, rg["u"], rg["a2"])
            for b in range(4):
                k = did(dve, dve.tensor_tensor_scan(gi[:, b, :], aa[:, b, :], ra[:, b, :], 0.0, ALU.mult, ALU.add))
            need(pool, k, rg["gelu"])
            rg["out"] = did(pool, pool.tensor_tensor(gi, gi, gbt, ALU.mult))

        def rg_split():
            need(act, rg["out"], t_proj)
            k = did(act, act.activation(xTh[:, 2:6, :], gi, ACT.Copy))
            need(dve, k)
            rg["ok"] = did(dve, dve.tensor_tensor(xTl[:, 2:6, :], gi, xTh[:, 2:6, :].bitcast(F32), ALU.subtract))

        rg_pieces = {1: [lambda: conv_block(0), lambda: conv_block(1)], 2: [lambda: conv_block(2), lambda: conv_block(3)],
                     3: [lambda: gates(0, ra, "rg_b_a"), lambda: gates(1, gi, "rg_b_x")], 4: [decay], 5: [remainder],
                     6: [roots], 7: [recurrence], 8: [rg_split]}

        mk = masks.bitcast(I32)
        e3 = ee.rearrange("p (a b) -> p a b", a=3)
        lev_n = len(LEVELS) + 1
        ops = {0: (gq, gk, [q0, q1, q2, k2, cum_ok])}
        q_reads = {}
        ga = {"exp": (), "used": ()}

        def decays(lev):
            s_ = LEVELS[lev - 1]
            cw = cum[:, 0 if s_ <= CHUNK // 2 else 1].rearrange("p a (n w) -> p (a n) w", w=2 * s_)
            mid = bc(cw[:, :, s_ - 1], 2, 2 * s_)
            need(dve, cum_ok, *ga["exp"])
            k = did(dve, dve.tensor_tensor(dd.rearrange("p (n w) -> p n w", w=2 * s_), cw, mid, ALU.subtract))
            need(act, k)
            k = did(act, act.activation(dd, dd, ACT.Abs))
            need(act, k, *ga["used"])
            k = did(act, act.activation(ee, dd, ACT.Exp, scale=-1.0))
            ga["exp"] = (k,)

        def factors(lev):
            z = lev % 2
            for e in (dve, pool):
                need(e, *ga["exp"], *q_reads.get(lev - 2, ()), kg)
            kq = did(dve, dve.tensor_tensor(qs[:, z], gq, e3, ALU.mult))
            kp = did(pool, pool.tensor_tensor(ks[:, z], gk, e3, ALU.mult))
            ga["used"] = (kq, kp)
            ops[lev] = (qs[:, z], ks[:, z], [kq, kp])

        def slot_of(b, r, pr):
            return (2 * pr + b, r * P) if b < 2 else (2 + b, pr * P)

        sc_free = {b: t_freed.get(b, ()) for b in range(6)}

        def scores(lev, pr, kt, qt):
            qq, kk, ready = ops[lev]
            need(pe, *ready)
            for b in range(4):
                need(pe, *sc_free[slot_of(b, 0, pr)[0]])
            for r in range(3):
                for b in range(4):
                    if r < len(BANK_HEADS[b]):
                        head, base, rws, blk = BANK_HEADS[b][r]
                        bk, c0 = slot_of(b, r, pr)
                        i = pe.matmul(bank[bk][:, c0:c0 + P], kk[base:base + rws, blk, kt * P:(kt + 1) * P],
                                      qq[base:base + rws, blk, qt * P:(qt + 1) * P], start=True, stop=True)
            t = did(pe, i)
            q_reads[lev] = (t,)
            return t

        sel_ok = {}

        def select(lev, t, b, pr, dst, both=False):
            w = len(BANK_HEADS[b])
            sl = BANK_SLOT[b]
            bk, c0 = slot_of(b, 0, 0 if both else pr)
            if both:
                o = scoreT[:, 0:2, sl, :]
                p3 = bank[bk][:, 0:2 * P].rearrange("p (a b) -> p a b", a=2)
                w = 2
            else:
                o = scoreT[:, dst, sl:sl + w, :]
                p3 = bank[bk][:, c0:c0 + w * P].rearrange("p (a b) -> p a b", a=w)
            need(dve, t, *sel_ok.get((b, pr), ()))
            if lev == 0:
                i = dve.tensor_tensor(o, p3, bc(ident[:, :], 1, w), ALU.mult)
            elif dst == 2:
                i = dve.tensor_copy(o, p3)
            else:
                i = dve.copy_predicated(o, bc(mk[:, lev - 1, :], 1, w), p3)
            k = did(dve, i)
            sel_ok[(b, pr)] = (k,)
            sc_free[bk] = (k,)
            return k

        o_done = {}

        def outputs(m, part, vt):
            if part == 1:
                pe.matmul(bank[6 + m][:, :], zeros[:, 0:P], zeros[:, :], start=True, stop=False, skip_group_check=True)
            for b in range(4):
                for r, (head, _, _, _) in enumerate(BANK_HEADS[b]):
                    v0 = (head * HD) if head < 4 else 512 + (head - 4) * HD
                    i = pe.matmul(bank[6 + m][:, head * HD:(head + 1) * HD], scoreT[:, part, BANK_SLOT[b] + r, :], ig[:, vt, v0:v0 + HD],
                                  start=(part == 0), stop=(part != 1), skip_group_check=True)
            o_done[m] = did(pe, i)

        def head_squares(m, sq):
            need(act, o_done[m], *ga["used"])
            k = did(act, act.activation(sq[:, 0:HALF], bank[6 + m][:, :], ACT.Square))
            need(dve, k)
            return did(dve, dve.tensor_reduce(hsum[:, m, :], sq[:, 0:HALF].rearrange("p (h d) -> p h d", d=HD), X, ALU.add))

        def own_tile_outputs():
            need(pe, sel_mark[0], done_of[7], k0, *t_freed[6], *t_freed[7])
            outputs(0, 0, 0)
            outputs(1, 1, 1)
            head_squares(0, ee)
            for m in range(M):
                sl_ = did(act, act.activation(sil[:, m, :].rearrange("p (a b) -> p a b", a=2),
                                              ig[:, m, :].rearrange("p (a b) -> p a b", a=4)[:, 1:4:2, :], ACT.Silu))
                need(pool, sl_, par_in)
                rg["sil"] = did(pool, pool.tensor_tensor(sil[:, m, :], sil[:, m, :], gain_bc, ALU.mult))

        sel_mark = [None]
        decays(1)
        chunk(0)
        factors(1)
        for lev in range(lev_n):
            last = lev == lev_n - 1
            pairs = [(0, 0, 0)] if last else [(0, 0, 0), (1, 1, 1)]
            if last:
                ts = [scores(lev, 0, 0, 1)]
                own_tile_outputs()
            else:
                ts = [scores(lev, 0, 0, 0), scores(lev, 1, 1, 1)]
            if lev + 2 < lev_n:
                decays(lev + 2)
            for b in range(2):
                k = select(lev, ts[0], b, 0, 2 if last else 0)
            if lev + 2 < lev_n:
                factors(lev + 2)
            for b in range(2):
                if not last:
                    k = select(lev, ts[1], b, 1, 1)
            for b in (2, 3):
                k = sel_mark[0] = select(lev, ts[-1], b, 0, 2 if last else 0, both=not last)
            if not last:
                next_chunk(lev + 2)
            if lev + 1 < len(rest):
                chunk(lev + 1)
                t_proj = (c_pe, c_pe.n)
            for piece in rg_pieces.get(lev, ()):
                piece()
        need(pe, k)
        outputs(1, 2, 0)
        k = head_squares(1, dd)
        need(dve, k)
        k = did(dve, dve.tensor_scalar(hsum, hsum, 1.0 / HD, EPS1, ALU.mult, ALU.add))
        need(act, k)
        k = did(act, act.activation(hrs, hsum, ACT.Sqrt))
        need(dve, k)
        k = did(dve, dve.reciprocal(hrs, hrs))
        need(dve, k, rg["sil"])
        ok_m = []
        for m in range(M):
            o3 = o_tok[:, m, 0:HALF]
            k = did(dve, dve.tensor_tensor(o3.rearrange("p (h d) -> p h d", d=HD), bank[6 + m][:, :].rearrange("p (h d) -> p h d", d=HD),
                                           bc(hrs[:, m, :], 2, HD), ALU.mult))
            need(dve, k)
            ok_m.append(did(dve, dve.tensor_tensor(o3, o3, sil[:, m, :], ALU.mult)))
        need(pe, *sc_free[4], *sc_free[5])
        for j, dst in enumerate((0, 1, 6, 7)):
            b = 4 + j
            need(pe, ok_m[-1])
            for m in range(M):
                i = pe.transpose(bank[b][:, m * P:(m + 1) * P], o_tok[:, m, j * P:(j + 1) * P], ident[:, :])
            t = did(pe, i)
            need(act, t, t_proj)
            k = did(act, act.activation(xTh[:, dst, :], bank[b][:, 0:S], ACT.Copy))
            need(dve, k)
            k = did(dve, dve.tensor_tensor(xTl[:, dst, :], bank[b][:, 0:S], xTh[:, dst, :].bitcast(F32), ALU.subtract))
        summed = out_product(A["w_out"][0], out_ahead, [k, rg["ok"]])
        act.preload_act_table(ACT.Sqrt)

        c2 = Carve()
        win_bias, dif_bias = c2(M, 4, S), c2(M, 4, S)
        rope = c2(M, 6 * 16)
        qT, kT = c2(4, S), c2(4, S)
        qT2, kT2 = c2(4, S), c2(4, S)
        cT = c2(3, S)
        pb = c2(2, 512)
        ptb = c2(2, 512)
        small = c2(16, 8)
        sq2 = c2(384)
        cn = [t_[:, :, :].rearrange("p a b -> p (a b)")[:, 0:384] for t_ in (conv, nonlin)]
        rt = act32[:, :, :].rearrange("p a b -> p (a b)")[:, 0:384].rearrange("p (a b c) -> p a b c", a=M, b=2)
        gains = c2(256 + 128 + 64 + 64 + 64 + 4 + 128 + 2)
        hq = c2(M, 16)
        SCALE_A, SCALE_B, SCALE_C, SCALE_D = HD ** -0.5, (NOPE + ROPE) ** -0.5, HD ** -0.5, 32 ** -0.5
        gv, at = {}, 0
        for name, width in (("mla_q_norm_2", 256), ("mla_kv_norm_2", 128), ("ax_q_norm_2", 64), ("ax_k_norm_2", 64),
                            ("diff_subln_2", 64), ("win_sink_2", 4), ("lam", 128), ("init", 2)):
            gv[name] = gains[:, at:at + width]
            at += width

        Wg, Wv, Wd = A["ffn_w_gate"][0], A["ffn_w_val"][0], A["ffn_w_down"][0]
        geglu = (lambda j: Wg[:, bass.ds(j * P, P)], lambda j: Wv[:, bass.ds(j * P, P)], lambda j: Wd[bass.ds(j * P, P), :])
        ffn_ahead(*geglu)
        hT_ok = norm(summed, 1.0, EPS1, False, lambda k: col("norm_ffn", k), None)
        ffn_ahead_rest()
        need(pool, *hT_ok)
        zb = did(pool, pool.memset(gb[:, 1, :], 0.0))
        need(sp, *hT_ok)
        c_par.tick(sp.dma_start(win_bias, C["win_bias"]), 16)
        c_par.tick(sp.dma_start(dif_bias, C["dif_bias"]), 16)
        c_par.tick(sp.dma_start(rope, C["rope"].rearrange("p m a b -> p m (a b)")), 16)
        in_flight.append(c_par.tick(sp.dma_start(gb[:, 0, :], all_partitions(A["norm_final"], D)), 16))
        layer_vectors(0)
        summed = ffn(*geglu, FT1, hT_ok, True)
        ffn_ahead(*swiglu_weights(0, 0))
        norm(summed, 1.0, EPS1, False, lambda k: col("norm_final", k), None)
        land()

        with nc.Fori(0, LAYERS) as l:
            fresh_counters()
            layer(l)
        gb_in, n_ok = (c_ln2, c_ln2.n), [(c_act, c_act.n), (c_dve, c_dve.n)]
        for m in range(M):
            for h in range(2):
                e = pool if (m, h) == (1, 1) else dve
                part = (slice(None), m, slice(h * HALF, (h + 1) * HALF))
                need(e, gb_in, *n_ok)
                k = did(e, e.tensor_tensor(x[part], n[part], gb[:, 0, h * HALF:(h + 1) * HALF], ALU.mult))
                need(e, k)
                k = did(e, e.tensor_tensor(x[part], x[part], gb[:, 1, h * HALF:(h + 1) * HALF], ALU.add))
                need(sp, k)
                t = c_out.tick(sp.dma_start(out[0, m * P:(m + 1) * P, h * HALF:(h + 1) * HALF], x[part]), 16)
        need(sp, t)

_INS = ["x", "norm_mix", "w_in", "hgrn_lower_bounds", "hgrn_norm", "rg_conv_w", "rg_conv_b", "rg_w_a", "rg_b_a", "rg_w_x",
        "rg_b_x", "rg_lambda", "gla_w_gate_up", "gla_b_gate", "gla_norm", "w_out", "norm_ffn", "ffn_w_gate", "ffn_w_val",
        "ffn_conv_w", "ffn_conv_b", "ffn_w_down", "norm_final", "w_in_2", "win_sink_2", "mla_q_norm_2", "mla_w_uq_2",
        "mla_kv_norm_2", "mla_w_ukv_2", "ax_q_norm_2", "ax_k_norm_2", "diff_lambda_2", "diff_subln_2", "w_out_2",
        "ffn_w_gu_2", "ffn_w_down_2", "ln_g_2", "ln_b_2"]


def kernel(**inputs):
    import numpy as _np
    import concourse.bacc as _bacc
    from concourse.bass_utils import run_bass_kernel_spmd as _run

    nc = _bacc.Bacc("TRN2", target_bir_lowering=False, num_devices=1)
    arrays, aps, consts = {}, {}, {}
    for name in _INS:
        a = _np.ascontiguousarray(inputs[name])
        arrays[f"in_{name}"] = a
        aps[name] = nc.dram_tensor(f"in_{name}", a.shape, mybir.dt.from_np(a.dtype), kind="ExternalInput").ap()
    for name, a in constants().items():
        arrays[f"const_{name}"] = a
        consts[name] = nc.dram_tensor(f"const_{name}", a.shape, mybir.dt.from_np(a.dtype), kind="ExternalInput").ap()
    out = nc.dram_tensor("out", (1, S, D), F32, kind="ExternalOutput").ap()
    program(nc, aps, consts, out)
    r = _run(nc, [arrays], core_ids=[0])
    return r.results[0]["out"]
```
